# Optimizing a Trainium2 kernel written in Bass

```python
import math
import jax, jax.numpy as jnp
from jax import lax
import numpy as np

D_MODEL = 1024
BATCH = 1
SEQ = 1024
DEPTH = 1
DEC_BATCH = 8
DEC_SEQ = 4
PAST_LEN = 8192
PAGE_SIZE = 128

D_MIX = D_MODEL
D_POOL = D_MIX // 4
POOL_WINDOWS = (2, 4, 8, 16)
N_POOL_GROUPS = len(POOL_WINDOWS)
POOL_GW = D_POOL // N_POOL_GROUPS
POOL_BUF = max(POOL_WINDOWS) - 1
D_SSM = D_MIX - D_POOL
SSM_HEADDIM = 64
SSM_HEADS = D_SSM // SSM_HEADDIM
SSM_GROUPS = 2
SSM_HPG = SSM_HEADS // SSM_GROUPS
SSM_STATE = 128
CONV_W = 4
CONV_DIM = D_SSM + 2 * SSM_GROUPS * SSM_STATE
CHUNK = 128
D_IN = D_POOL + D_SSM + CONV_DIM + SSM_HEADS
N_MEM = 256
MEM_HEADS = 4
MEM_HD = D_MODEL // MEM_HEADS
D_FF = 2816
EPS = 1e-6

kernel_name = 'hybrid_pool_ssd_macaron_decode_step'

def rmsnorm(x, g):
    xf = x.astype(jnp.float32)
    y = xf * lax.rsqrt(jnp.mean(xf * xf, axis=-1, keepdims=True) + EPS)
    return (y * g.astype(jnp.float32)).astype(x.dtype)

def swiglu(h, w_gate, w_up, w_down):
    return (jax.nn.silu(h @ w_gate) * (h @ w_up)) @ w_down

def pool_mix(u, buf, start_pos, w_pool, pool_scale):
    b, t, _ = u.shape
    ext = jnp.concatenate([buf, u], axis=1)
    cs = jnp.cumsum(ext.astype(jnp.float32), axis=1)
    cs = jnp.concatenate([jnp.zeros_like(cs[:, :1]), cs], axis=1)
    pos = start_pos + jnp.arange(t)
    means = []
    for g, w in enumerate(POOL_WINDOWS):
        sl = slice(g * POOL_GW, (g + 1) * POOL_GW)
        hi = cs[:, POOL_BUF + 1:POOL_BUF + 1 + t, sl]
        lo = cs[:, POOL_BUF + 1 - w:POOL_BUF + 1 - w + t, sl]
        cnt = jnp.minimum(pos + 1, w).astype(jnp.float32)
        means.append((hi - lo) / cnt[None, :, None])
    mean = jnp.concatenate(means, axis=-1).astype(u.dtype)
    p = (mean - u).reshape(b, t, N_POOL_GROUPS, POOL_GW)
    out = jnp.einsum('btgc,gcd->btgd', p, w_pool).reshape(b, t, D_POOL) * pool_scale
    return out, ext[:, -POOL_BUF:]

def causal_conv(xbc, conv_buf, conv_w, conv_b):
    t = xbc.shape[1]
    ext = jnp.concatenate([conv_buf, xbc], axis=1)
    out = sum(ext[:, k:k + t] * conv_w[k] for k in range(CONV_W)) + conv_b
    return jax.nn.silu(out), ext[:, -(CONV_W - 1):]

def ssd_chunked(x, dt, a, bm, cm, h0, chunk):
    b, t = x.shape[:2]
    nc = t // chunk
    r = lambda z: z.reshape((b, nc, chunk) + z.shape[2:])
    xc, dtc, bc, cc = r(x), r(dt), r(bm), r(cm)
    acs = jnp.cumsum(dtc * a, axis=2)
    seg = acs[:, :, :, None] - acs[:, :, None, :]
    causal = (jnp.arange(chunk)[:, None] >= jnp.arange(chunk)[None, :])[None, None, :, :, None, None]
    decay = jnp.exp(jnp.where(causal, seg, -jnp.inf))
    scores = jnp.einsum('bclgn,bcsgn->bclsg', cc, bc)
    wgt = scores[..., None] * decay * dtc[:, :, None]
    y_diag = jnp.einsum('bclsgk,bcsgkp->bclgkp', wgt, xc)
    decay_end = jnp.exp(acs[:, :, -1:] - acs) * dtc
    states = jnp.einsum('bclgn,bclgk,bclgkp->bcgkpn', bc, decay_end, xc)
    chunk_decay = jnp.exp(acs[:, :, -1])

    def step(h, inp):
        st, dec = inp
        return h * dec[..., None, None] + st, h

    h_last, h_prev = lax.scan(step, h0, (jnp.moveaxis(states, 1, 0), jnp.moveaxis(chunk_decay, 1, 0)))
    h_prev = jnp.moveaxis(h_prev, 0, 1)
    y_off = jnp.einsum('bclgn,bcgkpn,bclgk->bclgkp', cc, h_prev, jnp.exp(acs))
    y = (y_diag + y_off).reshape(b, t, SSM_GROUPS, SSM_HPG, SSM_HEADDIM)
    return y, h_last

def token_mix(h, pool_buf, conv_buf, ssm_h0, start_pos, w_in, conv_w, conv_b, dt_bias, a_log,
              d_skip, ssm_norm, w_pool, pool_scale, w_out):
    b, t, _ = h.shape
    proj = h @ w_in
    u, z, xbc, dt_raw = jnp.split(proj, [D_POOL, D_POOL + D_SSM, D_POOL + D_SSM + CONV_DIM], axis=-1)
    pool_out, new_pool = pool_mix(u, pool_buf, start_pos, w_pool, pool_scale)
    xbc, new_conv = causal_conv(xbc, conv_buf, conv_w, conv_b)
    xs, bm, cm = jnp.split(xbc, [D_SSM, D_SSM + SSM_GROUPS * SSM_STATE], axis=-1)
    xs = xs.reshape(b, t, SSM_GROUPS, SSM_HPG, SSM_HEADDIM)
    bm = bm.reshape(b, t, SSM_GROUPS, SSM_STATE)
    cm = cm.reshape(b, t, SSM_GROUPS, SSM_STATE)
    dt = jax.nn.softplus(dt_raw.astype(jnp.float32) + dt_bias.astype(jnp.float32))
    dt = dt.reshape(b, t, SSM_GROUPS, SSM_HPG)
    a = -jnp.exp(a_log.astype(jnp.float32)).reshape(SSM_GROUPS, SSM_HPG)
    h0 = ssm_h0.astype(jnp.float32).reshape(b, SSM_GROUPS, SSM_HPG, SSM_HEADDIM, SSM_STATE)
    chunk = CHUNK if t % CHUNK == 0 else t
    y, h_last = ssd_chunked(xs, dt, a, bm, cm, h0, chunk)
    y = y + xs * d_skip.reshape(SSM_GROUPS, SSM_HPG, 1)
    y = y.reshape(b, t, D_SSM).astype(h.dtype)
    y = rmsnorm(y * jax.nn.silu(z), ssm_norm)
    out = jnp.concatenate([pool_out, y], axis=-1) @ w_out
    new_ssm = h_last.reshape(b, SSM_HEADS, SSM_HEADDIM, SSM_STATE)
    return out, new_pool, new_conv, new_ssm

def mem_kv(mem, g_mem, w_mem_k, w_mem_v):
    b = mem.shape[0]
    m = rmsnorm(mem, g_mem)
    k = (m @ w_mem_k).reshape(b, N_MEM, MEM_HEADS, MEM_HD)
    v = (m @ w_mem_v).reshape(b, N_MEM, MEM_HEADS, MEM_HD)
    return k, v

def cross_attn(h, k, v, w_xq, w_xo):
    b, t, _ = h.shape
    q = (h @ w_xq).reshape(b, t, MEM_HEADS, MEM_HD)
    s = jnp.einsum('bthd,bmhd->bhtm', q, k).astype(jnp.float32) * (MEM_HD ** -0.5)
    p = jax.nn.softmax(s, axis=-1).astype(v.dtype)
    o = jnp.einsum('bhtm,bmhd->bthd', p, v).reshape(b, t, D_MODEL)
    return o @ w_xo

def layer(x, k_mem, v_mem, pool_buf, conv_buf, ssm_h0, start_pos, lw):
    (g_ffn1, w1_gate, w1_up, w1_down, g_mix, w_in, conv_w, conv_b, dt_bias, a_log, d_skip,
     ssm_norm, w_pool, pool_scale, w_out, g_xq, w_xq, w_xo, g_ffn2, w2_gate, w2_up, w2_down) = lw
    x = x + 0.5 * swiglu(rmsnorm(x, g_ffn1), w1_gate, w1_up, w1_down)
    mix, new_pool, new_conv, new_ssm = token_mix(rmsnorm(x, g_mix), pool_buf, conv_buf, ssm_h0, start_pos,
                                                 w_in, conv_w, conv_b, dt_bias, a_log, d_skip, ssm_norm,
                                                 w_pool, pool_scale, w_out)
    x = x + mix
    x = x + cross_attn(rmsnorm(x, g_xq), k_mem, v_mem, w_xq, w_xo)
    x = x + 0.5 * swiglu(rmsnorm(x, g_ffn2), w2_gate, w2_up, w2_down)
    return x, new_pool, new_conv, new_ssm

def setup_inputs(seed: int = 0) -> dict:
    key = jax.random.key(seed)
    keys = iter(jax.random.split(key, 48))
    f32 = jnp.float32
    L = DEPTH

    def nrm(shape, scale):
        return jax.random.normal(next(keys), shape, f32) * scale

    def gain(shape):
        return 1.0 + 0.05 * jax.random.normal(next(keys), shape, f32)

    d = {}
    d['x_prompt'] = nrm((BATCH, SEQ, D_MODEL), 1.0)
    d['x_sample'] = nrm((DEC_BATCH, DEC_SEQ, D_MODEL), 1.0)
    d['mem_prompt'] = nrm((BATCH, N_MEM, D_MODEL), 1.0)
    d['cache_mem_k'] = nrm((L, DEC_BATCH, N_MEM, MEM_HEADS, MEM_HD), 1.0)
    d['cache_mem_v'] = nrm((L, DEC_BATCH, N_MEM, MEM_HEADS, MEM_HD), 1.0)
    d['state_pool'] = nrm((L, DEC_BATCH, POOL_BUF, D_POOL), 1.0)
    d['state_conv'] = nrm((L, DEC_BATCH, CONV_W - 1, CONV_DIM), 1.0)
    d['state_ssm'] = nrm((L, DEC_BATCH, SSM_HEADS, SSM_HEADDIM, SSM_STATE), 0.5)
    d['g_ffn1'] = gain((L, D_MODEL))
    d['w1_gate'] = nrm((L, D_MODEL, D_FF), D_MODEL ** -0.5)
    d['w1_up'] = nrm((L, D_MODEL, D_FF), D_MODEL ** -0.5)
    d['w1_down'] = nrm((L, D_FF, D_MODEL), D_FF ** -0.5)
    d['g_mix'] = gain((L, D_MODEL))
    d['w_in'] = nrm((L, D_MODEL, D_IN), D_MODEL ** -0.5)
    d['conv_w'] = nrm((L, CONV_W, CONV_DIM), CONV_W ** -0.5)
    d['conv_b'] = nrm((L, CONV_DIM), 0.02)
    dt0 = jnp.exp(jax.random.uniform(next(keys), (L, SSM_HEADS), f32, math.log(1e-3), math.log(1e-1)))
    d['dt_bias'] = dt0 + jnp.log(-jnp.expm1(-dt0))
    d['a_log'] = jnp.log(jax.random.uniform(next(keys), (L, SSM_HEADS), f32, 1.0, 16.0))
    d['d_skip'] = gain((L, SSM_HEADS))
    d['ssm_norm'] = gain((L, D_SSM))
    d['w_pool'] = nrm((L, N_POOL_GROUPS, POOL_GW, POOL_GW), POOL_GW ** -0.5)
    d['pool_scale'] = 0.5 + 0.1 * jax.random.normal(next(keys), (L, D_POOL), f32)
    d['w_out'] = nrm((L, D_MIX, D_MODEL), D_MIX ** -0.5)
    d['g_mem'] = gain((L, D_MODEL))
    d['w_mem_k'] = nrm((L, D_MODEL, D_MODEL), D_MODEL ** -0.5)
    d['w_mem_v'] = nrm((L, D_MODEL, D_MODEL), D_MODEL ** -0.5)
    d['g_xq'] = gain((L, D_MODEL))
    d['w_xq'] = nrm((L, D_MODEL, D_MODEL), D_MODEL ** -0.5)
    d['w_xo'] = nrm((L, D_MODEL, D_MODEL), D_MODEL ** -0.5)
    d['g_ffn2'] = gain((L, D_MODEL))
    d['w2_gate'] = nrm((L, D_MODEL, D_FF), D_MODEL ** -0.5)
    d['w2_up'] = nrm((L, D_MODEL, D_FF), D_MODEL ** -0.5)
    d['w2_down'] = nrm((L, D_FF, D_MODEL), D_FF ** -0.5)
    d['g_final'] = gain((D_MODEL,))
    return d

def reference(x_prompt, x_sample, mem_prompt, cache_mem_k, cache_mem_v, state_pool, state_conv, state_ssm,
              g_ffn1, w1_gate, w1_up, w1_down, g_mix, w_in, conv_w, conv_b, dt_bias, a_log, d_skip,
              ssm_norm, w_pool, pool_scale, w_out, g_mem, w_mem_k, w_mem_v, g_xq, w_xq, w_xo,
              g_ffn2, w2_gate, w2_up, w2_down, g_final):
    bp = x_prompt.shape[0]
    hp, hs = x_prompt, x_sample
    mk_p, mv_p, pool_p, conv_p, ssm_p = [], [], [], [], []
    pool_s, conv_s, ssm_s = [], [], []
    for l in range(DEPTH):
        lw = (g_ffn1[l], w1_gate[l], w1_up[l], w1_down[l], g_mix[l], w_in[l], conv_w[l], conv_b[l],
              dt_bias[l], a_log[l], d_skip[l], ssm_norm[l], w_pool[l], pool_scale[l], w_out[l],
              g_xq[l], w_xq[l], w_xo[l], g_ffn2[l], w2_gate[l], w2_up[l], w2_down[l])
        k_p, v_p = mem_kv(mem_prompt, g_mem[l], w_mem_k[l], w_mem_v[l])
        zero_pool = jnp.zeros((bp, POOL_BUF, D_POOL), x_prompt.dtype)
        zero_conv = jnp.zeros((bp, CONV_W - 1, CONV_DIM), x_prompt.dtype)
        zero_ssm = jnp.zeros((bp, SSM_HEADS, SSM_HEADDIM, SSM_STATE), jnp.float32)
        hp, pb, cb, sb = layer(hp, k_p, v_p, zero_pool, zero_conv, zero_ssm, 0, lw)
        mk_p.append(k_p)
        mv_p.append(v_p)
        pool_p.append(pb)
        conv_p.append(cb)
        ssm_p.append(sb)
        hs, pb2, cb2, sb2 = layer(hs, cache_mem_k[l], cache_mem_v[l], state_pool[l], state_conv[l],
                                  state_ssm[l], PAST_LEN, lw)
        pool_s.append(pb2)
        conv_s.append(cb2)
        ssm_s.append(sb2)
    y_prompt = rmsnorm(hp, g_final)
    y_sample = rmsnorm(hs, g_final)
    return (y_prompt, y_sample, jnp.stack(mk_p), jnp.stack(mv_p), jnp.stack(pool_p), jnp.stack(conv_p),
            jnp.stack(ssm_p), jnp.stack(pool_s), jnp.stack(conv_s), jnp.stack(ssm_s))


_drawn_inputs = setup_inputs


def setup_inputs(seed=0):
    import zlib

    import numpy as np

    out = dict(_drawn_inputs(seed))
    spreads = {}
    factors = {'d_skip': 3.27, 'g_xq': 8.0, 'g_ffn2': 3.847}
    for name, (base, spread) in spreads.items():
        noise = np.random.default_rng([zlib.crc32(name.encode()), seed]).standard_normal(out[name].shape)
        drawn = base * np.exp(spread * noise) if base else spread * noise
        out[name] = __import__('jax').numpy.asarray(drawn.astype(out[name].dtype))
    for name, factor in factors.items():
        out[name] = (out[name] * factor).astype(out[name].dtype)
    return out
```

```python
from contextlib import ExitStack

import concourse.bass as bass
from concourse import mybir

F32 = mybir.dt.float32
F32R = mybir.dt.float32r
I32 = mybir.dt.int32
ALU = mybir.AluOpType
ACT = mybir.ActivationFunctionType
AX = mybir.AxisListType

P = 128
D = 1024
KT = D // P
SEQ = 1024
NB = 8
SL = 4
NS = NB * SL
T = SEQ + NS
TN = T // 3
NT = 3
LASTP = SEQ - 2 * TN
DFF = 2816
FT = DFF // P
CHUNKS = FT // 2
EPS = 1e-6
D_POOL, D_SSM, CONV_DIM, HEADS, HD, ST = 256, 768, 1280, 12, 64, 128
HG = HEADS // 2
YT = D_SSM // P
WINDOWS = (2, 4, 8, 16)
PBUF = 15
NMEM, MH, MHD = 256, 4, 256
ATT_SCALE = MHD ** -0.5

G1, GMIX, GMEM, GXQ, GF2, GFIN, CW, CB, GSSM, PSC = 0, 8, 16, 24, 32, 40, 48, 88, 98, 104
NPAR = 106

U_K, U_V, U_F1, U_IN, U_OUT, U_XQ, U_XO, U_F2 = 0, 8, 16, 82, 100, 108, 116, 124
U_END = U_F2 + 3 * FT
IN_BLOCKS = list(range(8, 18)) + [0, 1] + list(range(2, 8))
NORM_SUBS = ((0, 128), (128, 128), (256, 96))


def wait(eng, sem, value):
    if not (isinstance(value, int) and value <= 0):
        eng.wait_ge(sem, value)


def cols(n):
    return slice(n * TN, (n + 1) * TN)


def bc(ap, shape):
    return ap.to_broadcast(shape)


def build(nc, A, O):
    ctx = ExitStack()
    with ctx:
        base = (nc.sbuf_base + 63) // 64 * 64
        at = {}
        used = [base]

        def region(name, size):
            at[name] = used[0]
            used[0] += size
            assert used[0] <= nc.sbuf_usable_end, (name, used[0], nc.sbuf_usable_end)

        KTB = KT * T * 4
        for name, size in (("X", KTB), ("HH", KTB), ("HL", KTB), ("WH", 6 * 4096), ("WL", 6 * 4096),
                           ("WR", 3 * 4096), ("MID", 45056), ("C", 4950)):
            region(name, size)

        def sb(name, reg, off, shape, dt=F32):
            return nc.alloc_sbuf_tensor_at(name, list(shape), dt, offset=at[reg] + off)

        x = sb("x", "X", 0, [P, KT, T])
        h_hi = sb("h_hi", "HH", 0, [P, KT, T], F32R)
        h_lo = sb("h_lo", "HL", 0, [P, KT, T], F32R)
        w_hi = sb("w_hi", "WH", 0, [P, 6, 1024], F32R)
        w_lo = sb("w_lo", "WL", 0, [P, 6, 1024], F32R)
        w_raw = sb("w_raw", "WR", 0, [P, 3, 1024])
        sq = sb("sq", "MID", 0, [P, KT, TN])
        hf = sb("hf", "MID", 11264, [P, KT, TN])
        mid_hi = sb("mid_hi", "MID", 22528, [P, 2, T], F32R)
        mid_lo = sb("mid_lo", "MID", 30976, [P, 2, T], F32R)
        gate = sb("gate", "MID", 39424, [P, 2, TN])
        prod = sb("prod", "MID", 42240, [P, 2, TN])
        co = [0]

        def const(name, shape, dt=F32):
            n = 4
            for s in shape[1:]:
                n *= s
            t = sb(name, "C", co[0], shape, dt)
            co[0] += (n + 31) // 32 * 32
            assert co[0] <= 4950, name
            return t

        ident = const("ident", [P, P])
        upper = const("upper", [P, P])
        below = const("below", [P, P])
        ones = const("ones", [P, P])
        par = const("par", [P, NPAR])
        diag = const("diag", [P, 3 * P])
        nrm = const("nrm", [P, 4, 4])
        wdt_hi = const("wdt_hi", [P, KT, HEADS], F32R)
        wdt_lo = const("wdt_lo", [P, KT, HEADS], F32R)
        dskip = const("dskip", [P, YT])
        xtok = sb("xtok", "HH", 0, [P, 9, D])
        mem_hi = sb("mem_hi", "HL", 3072 + 1024, [P, KT, NMEM], F32R)
        mem_lo = sb("mem_lo", "HL", 12288, [P, KT, NMEM], F32R)
        mem = sb("mem", "HL", 20480, [P, 2, D])
        kT0 = sb("kT0", "HL", 20480, [P, KT, NMEM])
        memf = sb("memf", "MID", 11264, [P, KT, NMEM])
        ktok = sb("ktok", "MID", 22528, [P, 2, D])
        vtok = sb("vtok", "MID", 30976, [P, 2, D])
        parrow = sb("parrow", "MID", 39424, [NPAR, P])
        NPRE = 3 + SEQ + NB * 7
        pre = [sb(f"pre{i}", "X", 4352 * i, [P, NPRE]) for i in range(2)]
        convT = sb("convT", "X", 8704, [P, 10, NB, 3])
        poolT = sb("poolT", "X", 9728, [P, 2, NB, PBUF])
        wpool = sb("wpool", "X", 10752, [P, 2, P])
        ramp = sb("ramp", "X", 11776, [P, 2, PBUF])
        ramp_i = sb("ramp_i", "X", 11904, [P, PBUF], I32)
        fresh = sb("fresh", "X", 12032, [P, 2, NS])
        NUE = PBUF + SEQ + NB * (PBUF + SL)
        win_a = sb("win_a", "X", 19488, [P, NUE])
        win_b = sb("win_b", "X", 14720, [P, NUE])
        ue = [sb("ue0", "X", 29024, [P, NUE]), sb("ue1", "X", 24256, [P, NUE])]
        convrow = sb("convrow", "X", 24320, [NB * 3, CONV_DIM])
        poolrow = sb("poolrow", "X", 29440, [NB * PBUF, D_POOL])
        z = sb("z", "X", 0, [P, YT, T])
        pool_out = sb("pool_out", "X", YT * T * 4, [P, 2, T])
        bcT = sb("bcT", "MID", 0, [P, 4, T])
        xs = sb("xs", "MID", 4 * T * 4, [P, YT, T])
        tails = sb("tails", "MID", 42240, [P, 2, 256])
        wdt = sb("wdt", "MID", 42240 + 2048, [P, KT, HEADS])
        dtb = sb("dtb", "MID", 42240 + 2048 + 384, [P, 1, HEADS])
        alog = sb("alog", "MID", 42240 + 2048 + 384 + 64, [P, 1, HEADS])
        dsk_all = sb("dsk_all", "MID", 42240 + 2048 + 384 + 128, [P, HEADS])
        ho = [0]

        def hh(name, shape):
            n = 4
            for s in shape[1:]:
                n *= s
            t = sb(name, "HH", ho[0], shape)
            ho[0] += n
            assert ho[0] <= KTB
            return t

        xb = hh("xb", [P, 1024])
        xdt = hh("xdt", [P, HEADS, HD])
        xde = hh("xde", [P, HEADS, HD])
        ud = hh("ud", [P, HEADS * P])
        ew = hh("ew", [P, HEADS * P])
        sm = hh("sm", [P, 2 * P])
        ytok = hh("ytok", [P, HEADS * HD])
        ytmp = hh("ytmp", [P, HEADS * HD])
        hT = hh("hT", [P, HEADS * HD])
        h0T = sb("h0T", "HH", 10240, [P, 2, D_SSM])
        bx = sb("bx", "HH", 16384, [NS, 2, NB, P])
        hc = sb("hc", "HL", 0, [P, HEADS * HD])
        so = [3072]

        def hl(name, shape, dt=F32):
            n = 4
            for s in shape[1:]:
                n *= s
            t = sb(name, "HL", so[0], shape, dt)
            so[0] += (n + 31) // 32 * 32
            assert so[0] <= 8448, name
            return t

        NTT = SEQ // P + 1
        dt_ = hl("dt_", [P, NTT, HEADS])
        dta = hl("dta", [P, NTT, HEADS])
        ea = hl("ea", [P, NTT, HEADS])
        dedt = hl("dedt", [P, NTT, HEADS])
        cd = hl("cd", [P, NTT, HEADS])
        ea_s = hl("ea_s", [P, YT, NS + NB])
        up_s = hl("up_s", [NS, NS + NB])
        be_s = hl("be_s", [NS, NS])
        expa = hl("expa", [P, 1, HEADS])
        ser = [sb(f"ser{i}", "HH", 10240 + 448 * i, [P, NTT, HEADS]) for i in range(7)]
        dtab = sb("dtab", "HH", 10240 + 3584, [NS, HEADS, HD])
        h0 = sb("h0", "HL", 8448, [P, NB, YT, ST])
        hout = sb("hout", "HH", 25600 + 1024 + 3072 - 3072, [P, YT, ST])
        q = sb("q", "MID", 11264, [P, KT, T])
        kTs = sb("kTs", "MID", 0, [P, KT, NMEM])
        pr = [sb("pr0", "MID", 8192, [P, NMEM]), sb("pr1", "MID", 9216, [P, NMEM])]
        pT = [sb("pT0", "MID", 10240, [P, 2, P]), sb("pT1", "X", 32768, [P, 2, P])]
        kT = sb("kT", "X", 0, [P, KT, NMEM])
        v = sb("v", "X", 8192, [P, 2, D])
        kring = [sb(f"kring{i}", "X", 16384 + 8192 * i, [P, 2, D]) for i in range(2)]
        vring = [sb("vring0", "WH", 0, [P, 2, D]), sb("vring1", "WL", 0, [P, 2, D]),
                 sb("vring2", "X", 16384, [P, 2, D]), sb("vring3", "X", 24576, [P, 2, D])]
        stat = nrm
        amax = sb("amax", "C", co[0], [P, 16])
        co[0] += 64
        s_s = sb("s_s", "MID", 0, [P, 2, P])
        p_s = sb("p_s", "MID", 1024, [P, NMEM])
        pT_s = sb("pT_s", "MID", 2048, [P, 2, P])
        yrow = sb("yrow", "MID", 22528, [P, 2, D])

        bank = [ctx.enter_context(nc.psum_tensor(f"bank{i}", [P, 512], F32)) for i in range(8)]

        x_spill = nc.dram_tensor("x_spill", [P, KT, T], F32).ap()
        kT_spill = nc.dram_tensor("kT_spill", [P, KT, NMEM], F32).ap()

        def sem(name):
            return ctx.enter_context(nc.semaphore(name))

        w_dma = [sem(f"w_dma{i}") for i in range(3)]
        w_hid, w_ready, kv_used = sem("w_hid"), sem("w_ready"), sem("kv_used")
        s_const, s_par, s_part = sem("s_const"), sem("s_par"), sem("s_part")
        s_x = [sem(f"s_x{i}") for i in range(5)]
        s_mem, mem_a, mem_d = sem("s_mem"), sem("mem_a"), sem("mem_d")
        tr_ready, tr_act, tr_dve = sem("tr_ready"), sem("tr_act"), sem("tr_dve")
        kv_act, kv_dve, kt_ready, kt_copied = (sem("kv_act"), sem("kv_dve"),
                                                         sem("kt_ready"), sem("kt_copied"))
        s_kvout, s_ktout = sem("s_kvout"), sem("s_ktout")
        n_sq, n_st, n_rs, n_bc, n_hf, n_hi, n_lop, n_lod = (sem("n_sq"), sem("n_st"), sem("n_rs"), sem("n_bc"),
                                                            sem("n_hf"), sem("n_hi"), sem("n_lop"), sem("n_lod"))
        f_g, f_u, f_s, f_p, f_mh, f_ml, f_d, f_x = (sem("f_g"), sem("f_u"), sem("f_s"), sem("f_p"),
                                                    sem("f_mh"), sem("f_ml"), sem("f_d"), sem("f_x"))
        dve_c = sem("dve_c")
        act_c = sem("act_c")
        pool_c = sem("pool_c")
        p_ready, p_free = sem("p_ready"), sem("p_free")
        s_spill = sem("s_spill")
        s_back = [sem(f"s_back{n}") for n in range(NT)]
        s_strow, s_stT, s_stc, s_wdt, s_wdtr = sem("s_strow"), sem("s_stT"), sem("s_stc"), sem("s_wdt"), sem("s_wdtr")
        pre_ready, conv_done, xbc_ready = sem("pre_ready"), sem("conv_done"), sem("xbc_ready")
        tail_t, tail_c = sem("tail_t"), sem("tail_c")
        tail_d = [sem("tail_d0"), sem("tail_d1")]
        dt_ready, ue_ready, pmix, pmm = sem("dt_ready"), sem("ue_ready"), sem("pmix"), sem("pmm")
        s_wpool, s_wpz = sem("s_wpool"), sem("s_wpz")
        z_ready = sem("z_ready")
        s_mask, s_dexp, s_dec, s_dece, s_decd = (sem("s_mask"), sem("s_dexp"), sem("s_dec"), sem("s_dece"),
                                                 sem("s_decd"))
        t1, t1_ev, ud_ready, seg_ready, e_done, sc_ready, sm_done = (
            sem("t1"), sem("t1_ev"), sem("ud_ready"), sem("seg_ready"), sem("e_done"), sem("sc_ready"),
            sem("sm_done"))
        wg_ready, xd_ready, yd_ready, yo_ready, st_ready, yc_done, hc_ready, h_upd, yt_ready, y_ev, g_done = (
            sem("wg_ready"), sem("xd_ready"), sem("yd_ready"), sem("yo_ready"), sem("st_ready"), sem("yc_done"),
            sem("hc_ready"), sem("h_upd"), sem("yt_ready"), sem("y_ev"), sem("g_done"))
        s_h0, s_ho, s_hoc, s_h0t, s_h0a, s_h0d, s_h0s, s_h0st, s_h0n, s_h0o = (
            sem("s_h0"), sem("s_ho"), sem("s_hoc"), sem("s_h0t"), sem("s_h0a"), sem("s_h0d"),
            sem("s_h0s"), sem("s_h0st"), sem("s_h0n"), sem("s_h0o"))
        po_hi, po_lo = sem("po_hi"), sem("po_lo")
        s_kv2 = sem("s_kv2")
        s_kr = [sem(f"s_kr{i}") for i in range(2)]
        s_vr = [sem(f"s_vr{i}") for i in range(4)]
        q_ready = sem("q_ready")
        a_s, a_m, a_e, a_n, a_t, a_c, a_o, a_oh, a_ol = (sem("a_s"), sem("a_m"), sem("a_e"), sem("a_n"), sem("a_t"),
                                                         sem("a_c"), sem("a_o"), sem("a_oh"), sem("a_ol"))
        b_t, b_ta, b_s, b_r, b_d, b_e, b_v = (sem("b_t"), sem("b_ta"), sem("b_s"), sem("b_r"), sem("b_d"),
                                              sem("b_e"), sem("b_v"))
        y_t, y_c = sem("y_t"), sem("y_c")
        s_y = [sem("s_y0"), sem("s_y1")]
        s_dd = sem("s_dd")

        def kview(name):
            return A[name].rearrange("l (k p) m -> p (l k) m", p=P)

        wv = {n: kview(n) for n in ("w1_gate", "w1_up", "w1_down", "w2_gate", "w2_up", "w2_down", "w_in", "w_out",
                                    "w_mem_k", "w_mem_v", "w_xq", "w_xo")}
        kc = A["cache_mem_k"].rearrange("l b (t p) h d -> p (l b) t (h d)", p=P)
        vc = A["cache_mem_v"].rearrange("l b (t p) h d -> p (l b) t (h d)", p=P)
        h0_in = A["state_ssm"].rearrange("l b (j e) d n -> (e d) (l b j) n", e=2)
        h0_out = O["ssm_sample"].rearrange("l b (j e) d n -> (e d) (l b j) n", e=2)

        block = ctx.enter_context(nc.Block())

        FFN = ((U_F1, 0, "w1"), (U_F2, 1, "w2"))

        def wait_used(eng, w, i):
            if isinstance(i, int):
                w, i = w + 6 * i, 0
                if w < 0:
                    return
                if w < U_F1:
                    eng.wait_ge(kv_used, w + 1)
                    return
                if U_IN <= w < U_F2:
                    eng.wait_ge(p_ready, 6 * ((w - U_IN) // 2 + 1))
                    return
                f = 0 if w < U_IN else 1
            else:
                f = 0 if w < U_IN - 6 else 1
            u0 = (U_F1, U_F2)[f]
            stage, it = (w - u0) // 2 % 3, (w - u0) // 6
            if stage < 2:
                eng.wait_ge(f_u, 66 * f + 6 * it + 3 * (stage + 1) + 6 * i)
            else:
                eng.wait_ge(f_d, 264 * f + 24 * (it + 1) + 24 * i)

        @block.sync
        def _(eng):
            def unit(w, ring, src):
                wait(eng, w_ready, w - 2 if isinstance(w, int) else w - 2)
                dst = w_raw[:, ring, :].rearrange("p (a b) -> p a b", a=src.shape[1])
                eng.dma_start(dst, src).then_inc(w_dma[ring], 16)

            for row, name in ((G1, "g_ffn1"), (GMIX, "g_mix"), (GMEM, "g_mem"), (GXQ, "g_xq"), (GF2, "g_ffn2"),
                              (GSSM, "ssm_norm"), (PSC, "pool_scale"), (CB, "conv_b")):
                n = A[name].shape[1] // P
                eng.dma_start(parrow[row:row + n, :], A[name].rearrange("l (r c) -> (l r) c", c=P)).then_inc(s_par, 16)
            eng.dma_start(parrow[GFIN:GFIN + KT, :], A["g_final"].rearrange("(r c) -> r c", c=P)).then_inc(s_par, 16)
            eng.dma_start(parrow[CW:CW + 40, :], A["conv_w"].rearrange("l k (r c) -> (l k r) c", c=P)).then_inc(s_par, 16)
            eng.dma_start(mem[:, :, :], A["mem_prompt"].rearrange("a (t p) d -> p (a t) d", p=P)).then_inc(s_mem, 16)
            xp = A["x_prompt"].rearrange("a (t p) d -> p (a t) d", p=P)

            def xload(t):
                if t < 8:
                    eng.dma_start(xtok[:, t, :], xp[:, t, :]).then_inc(s_x[t // 2], 16)
                else:
                    eng.dma_start(xtok[0:NS, t, :], A["x_sample"].rearrange("b s d -> (b s) d")).then_inc(s_x[t // 2], 16)

            for k in range(8):
                unit(U_K + k, (U_K + k) % 3, wv["w_mem_k"][:, k:k + 1, :])
                xload(k)
            xload(8)
            for k in range(8):
                unit(U_V + k, (U_V + k) % 3, wv["w_mem_v"][:, k:k + 1, :])
                if k == 3:
                    eng.wait_ge(kv_act, 2)
                    eng.wait_ge(kv_dve, 2)
                    eng.dma_start(O["mem_k_prompt"].rearrange("l a (t p) h d -> p (l a t) (h d)", p=P), ktok[:, :, :])\
                       .then_inc(s_kvout, 16)
                if k == 7:
                    eng.wait_ge(kt_copied, 4)
                    eng.dma_start(kT_spill, kT0[:, :, :]).then_inc(s_ktout, 16)

            def ffn_units(u0, name, i):
                for j in range(6):
                    w = u0 + j + 6 * i
                    kind = ("gate", "up", "gate", "up", "down", "down")[j]
                    view = wv[f"{name}_{kind}"]
                    if j < 4:
                        first = (2 * i + j // 2) * P
                        src = view[:, :, bass.ds(first, P)]
                    else:
                        src = view[:, bass.ds(2 * i + j - 4, 1), :]
                    unit(w, (u0 + j) % 3, src)

            ffn_units(U_F1, "w1", 0)
            eng.wait_ge(kv_act, 4)
            eng.wait_ge(kv_dve, 4)
            eng.dma_start(O["mem_v_prompt"].rearrange("l a (t p) h d -> p (l a t) (h d)", p=P), vtok[:, :, :])\
               .then_inc(s_kvout, 16)
            eng.dma_start(O["pool_sample"][0, :, 0:PBUF - SL, :], A["state_pool"][0, :, SL:PBUF, :]).then_inc(s_dd, 16)
            with eng.Fori(1, CHUNKS) as i:
                ffn_units(U_F1, "w1", i)

            for k in range(4):
                unit(U_IN + k, (U_IN + k) % 3, wv["w_in"][:, :, IN_BLOCKS[k] * P:(IN_BLOCKS[k] + 1) * P])
            for n in range(NT):
                eng.wait_ge(f_x, 24 * CHUNKS - 16 + 8 * n)
                eng.dma_start(x_spill[:, :, cols(n)], x[:, :, cols(n)]).then_inc(s_spill, 16)
            eng.dma_start(wdt[:, :, :], wv["w_in"][:, :, 2304:2316]).then_inc(s_wdt, 16)
            eng.dma_start(dsk_all[:, :], A["d_skip"][0].partition_broadcast(P)).then_inc(s_wdt, 16)
            eng.dma_start(dtb[:, 0, :], A["dt_bias"][0].partition_broadcast(P)).then_inc(s_wdt, 16)
            eng.dma_start(alog[:, 0, :], A["a_log"][0].partition_broadcast(P)).then_inc(s_wdt, 16)
            eng.wait_ge(s_spill, 48)
            eng.wait_ge(n_hf, 12)
            eng.dma_start(convrow[:, :], A["state_conv"].rearrange("l b t c -> (l b t) c")).then_inc(s_strow, 16)
            eng.dma_start(poolrow[:, :], A["state_pool"].rearrange("l b t c -> (l b t) c")).then_inc(s_strow, 16)
            eng.wait_ge(s_wpz, 1)
            for g in range(4):
                a = 64 * (g % 2)
                eng.dma_start(wpool[a:a + 64, g // 2, a:a + 64], A["w_pool"][0, g]).then_inc(s_wpool, 16)

            def tail_out(m):
                eng.wait_ge(tail_c, m + 1)
                s = m % 2
                if m < 10:
                    c = slice(m * P, (m + 1) * P)
                    eng.dma_start(O["conv_prompt"][0, 0, :, c], tails[0:3, s, 0:P]).then_inc(tail_d[s], 16)
                    eng.dma_start(O["conv_sample"].rearrange("l b t c -> (l b t) c")[:, c],
                                  tails[0:NB * 3, s, P:2 * P]).then_inc(tail_d[s], 16)
                else:
                    c = slice((m - 10) * P, (m - 9) * P)
                    eng.dma_start(O["pool_prompt"][0, 0, :, c], tails[0:PBUF, s, 0:P]).then_inc(tail_d[s], 16)
                    for b in range(NB):
                        eng.dma_start(O["pool_sample"][0, b, PBUF - SL:PBUF, c],
                                      tails[SL * b:SL * b + SL, s, P:2 * P]).then_inc(tail_d[s], 16)

            for k in range(4, 18):
                unit(U_IN + k, (U_IN + k) % 3, wv["w_in"][:, :, IN_BLOCKS[k] * P:(IN_BLOCKS[k] + 1) * P])
                if k >= 7 and k % 2:
                    for m in ((k - 7), (k - 6)):
                        if m < 12:
                            tail_out(m)
            for k in range(4):
                unit(U_OUT + k, (U_OUT + k) % 3, wv["w_out"][:, :, k * P:(k + 1) * P])
            eng.wait_ge(z_ready, 6 * NT)
            eng.dma_start(h0[:, :, :, :].rearrange("p b j n -> p (b j) n"), h0_in).then_inc(s_h0, 16)
            eng.wait_ge(s_hoc, 1)
            eng.dma_start(O["ssm_prompt"].rearrange("l a (j e) d n -> (e d) (l a j) n", e=2), hout[:, :, :])\
               .then_inc(s_h0o, 16)
            for j in range(YT):
                eng.wait_ge(s_h0n, 2 * (j + 1))
                eng.dma_start(h0_out.rearrange("p (b j) n -> p b j n", j=YT)[:, :, j, :], h0[:, :, j, :])\
                   .then_inc(s_h0o, 16)
            eng.wait_ge(g_done, 9)
            eng.wait_ge(po_lo, 1)
            for n in range(NT):
                eng.dma_start(x[:, :, cols(n)], x_spill[:, :, cols(n)]).then_inc(s_back[n], 16)
            for k in range(4, 8):
                unit(U_OUT + k, (U_OUT + k) % 3, wv["w_out"][:, :, k * P:(k + 1) * P])
            for k in range(4):
                unit(U_XQ + k, (U_XQ + k) % 3, wv["w_xq"][:, :, k * P:(k + 1) * P])
            eng.wait_ge(f_x, 24 * CHUNKS + 24)
            for n in range(NT):
                eng.dma_start(x_spill[:, :, cols(n)], x[:, :, cols(n)]).then_inc(s_spill, 16)
            for k in range(4, 8):
                unit(U_XQ + k, (U_XQ + k) % 3, wv["w_xq"][:, :, k * P:(k + 1) * P])
            eng.wait_ge(s_spill, 96)
            eng.wait_ge(n_hf, 24)
            eng.wait_ge(s_ktout, 16)
            eng.wait_ge(s_kvout, 32)
            eng.dma_start(kT[:, :, :], kT_spill).then_inc(s_kv2, 16)
            eng.dma_start(v[:, :, :], O["mem_v_prompt"].rearrange("l a (t p) h d -> p (l a t) (h d)", p=P))\
               .then_inc(s_kv2, 16)
            for b in range(2):
                eng.dma_start(kring[b][:, :, :], kc[:, b]).then_inc(s_kr[b], 16)
            for k in range(4):
                unit(U_XO + k, (U_XO + k) % 3, wv["w_xo"][:, :, k * P:(k + 1) * P])
            eng.wait_ge(p_ready, 102)
            for b in range(2):
                eng.dma_start(vring[b][:, :, :], vc[:, b]).then_inc(s_vr[b], 16)
            for b in range(2, NB):
                eng.wait_ge(b_t, 4 * (b - 1))
                eng.dma_start(kring[b % 2][:, :, :], kc[:, b]).then_inc(s_kr[b % 2], 16)
            for b in range(2, NB):
                if b < 4:
                    eng.wait_ge(b_t, 4 * (NB - 2 + b - 1))
                else:
                    eng.wait_ge(b_v, b - 3)
                eng.dma_start(vring[b % 4][:, :, :], vc[:, b]).then_inc(s_vr[b % 4], 16)
            eng.wait_ge(a_o, 4 * NB)
            eng.wait_ge(b_v, NB)
            for n in range(NT):
                eng.dma_start(x[:, :, cols(n)], x_spill[:, :, cols(n)]).then_inc(s_back[n], 16)
            for k in range(4, 8):
                unit(U_XO + k, (U_XO + k) % 3, wv["w_xo"][:, :, k * P:(k + 1) * P])
            with eng.Fori(0, CHUNKS) as i:
                ffn_units(U_F2, "w2", i)
            yp = O["y_prompt"].rearrange("a (t p) d -> p (a t) d", p=P)
            for t in range(9):
                eng.wait_ge(y_c, 2 * (t + 1))
                if t < 8:
                    eng.dma_start(yp[:, t, :], yrow[:, t % 2, :]).then_inc(s_y[t % 2], 16)
                else:
                    eng.dma_start(O["y_sample"].rearrange("b s d -> (b s) d"), yrow[0:NS, t % 2, :])\
                       .then_inc(s_y[t % 2], 16)
            eng.wait_ge(s_y[0], 16 * 5)
            eng.wait_ge(s_y[1], 16 * 4)
            eng.wait_ge(s_kvout, 32)
            eng.wait_ge(s_dd, 16)
            eng.wait_ge(s_h0o, 16 * (YT + 1))
            for s in range(2):
                eng.wait_ge(tail_d[s], 16 * (2 * 5 + 9))

        @block.gpsimd
        def _(eng):
            def lo(w, slot, ring):
                eng.wait_ge(w_hid, w + 1)
                eng.tensor_tensor(w_lo[:, slot, :], w_raw[:, ring, :], w_hi[:, slot, :].bitcast(F32), ALU.subtract)\
                   .then_inc(w_ready, 1)

            def lo_pair(w):
                for d in range(2):
                    lo(w + d, (w + d) % 6, (w + d) % 3)

            def norm_lo(v, n, src=None, k0=0, half=4, off=0):
                w = 3 * v + n
                eng.wait_ge(n_hi, 2 * w + 1)
                s = hf[:, 0:half, :] if src is None else src[:, 0:half, cols(n)]
                eng.tensor_tensor(h_lo[:, off:off + half, cols(n)], s,
                                  h_hi[:, off:off + half, cols(n)].bitcast(F32), ALU.subtract).then_inc(n_lop, 1)

            eng.memset(ones[:, :], 1.0).then_inc(s_const, 1)
            eng.memset(ident[:, :], 0.0).then_inc(s_const, 1)
            eng.wait_ge(s_const, 2)
            eng.affine_select(out=ident[:, :], in_=ident[:, :], compare_op=ALU.not_equal, fill=1.0, base=0,
                              pattern=[[-1, P]], channel_multiplier=1).then_inc(s_const, 1)
            eng.affine_select(out=upper[:, :], in_=ones[:, :], compare_op=ALU.is_ge, fill=0.0, base=0,
                              pattern=[[1, P]], channel_multiplier=-1).then_inc(s_const, 1)
            eng.affine_select(out=below[:, :], in_=ones[:, :], compare_op=ALU.is_gt, fill=0.0, base=0,
                              pattern=[[-1, P]], channel_multiplier=1).then_inc(s_const, 1)
            for p in range(U_K // 2, U_F1 // 2 + 2):
                lo_pair(2 * p)
            for n in range(NT):
                norm_lo(0, n)

            def ffn_loop(u0, f):
                def body(i):
                    for stage in range(3):
                        p0 = u0 + 4 + 2 * stage
                        for d in range(2):
                            w = p0 + d + 6 * i
                            if not (isinstance(w, int) and w >= U_END):
                                lo(w, (p0 + d) % 6, (p0 + d) % 3)
                        if stage < 2:
                            for n in range(NT):
                                gi = 66 * f + 3 * stage + n + 6 * i
                                eng.wait_ge(f_mh, gi + 1)
                                eng.tensor_tensor(mid_lo[:, stage, cols(n)], prod[:, (3 * stage + n) % 2, :],
                                                  mid_hi[:, stage, cols(n)].bitcast(F32), ALU.subtract)\
                                   .then_inc(f_ml, 1)
                return body

            body = ffn_loop(U_F1, 0)
            body(0)
            with eng.Fori(1, CHUNKS) as i:
                body(i)
            for n in range(NT):
                norm_lo(1, n)
            eng.wait_ge(s_spill, 48)
            eng.wait_ge(n_hf, 12)
            eng.memset(wpool[:, :, :], 0.0).then_inc(s_wpz, 1)
            eng.iota(ramp_i[:, :], pattern=[[1, PBUF]], base=1, channel_multiplier=0).then_inc(s_wpz, 1)
            eng.wait_ge(s_wdtr, 1)
            eng.tensor_tensor(wdt_lo[:, :, :], wdt[:, :, :], wdt_hi[:, :, :].bitcast(F32), ALU.subtract)\
               .then_inc(s_wdtr, 1)
            for p in range(9):
                lo_pair(U_IN + 4 + 2 * p)
            eng.wait_ge(z_ready, 6 * NT)
            blk = up_s[:, 0:NS].rearrange("p (b t) -> p b t", t=SL)
            mem_b = up_s[:, NS:NS + NB]
            c = [0]

            def link(ins):
                c[0] += 1
                ins.then_inc(pool_c, 1)
                eng.wait_ge(pool_c, c[0])

            link(eng.memset(up_s[:, :], 1.0))
            link(eng.memset(be_s[:, :], 1.0))
            for out_, pat in ((blk, [[-SL, NB], [0, SL]]), (mem_b, [[-SL, NB]])):
                back = [[SL, NB]] + pat[1:]
                link(eng.affine_select(out=out_, in_=out_, compare_op=ALU.is_ge, fill=0.0, base=0, pattern=pat,
                                       channel_multiplier=1))
                link(eng.affine_select(out=out_, in_=out_, compare_op=ALU.is_ge, fill=0.0, base=SL - 1,
                                       pattern=back, channel_multiplier=-1))
            link(eng.affine_select(out=be_s[:, :], in_=up_s[:, 0:NS], compare_op=ALU.is_gt, fill=0.0, base=0,
                                   pattern=[[-1, NS]], channel_multiplier=1))
            link(eng.affine_select(out=up_s[:, 0:NS], in_=up_s[:, 0:NS], compare_op=ALU.is_ge, fill=0.0, base=0,
                                   pattern=[[1, NS]], channel_multiplier=-1))
            eng.memset(hc[:, :], 0.0).then_inc(s_mask, 1)
            eng.wait_ge(s_decd, 2)
            for ch in range(9):
                M = P if ch < 8 else NS
                sl = slice(ch * P, ch * P + M)
                xh = xb[0:M, 0:D_SSM].rearrange("p (h d) -> p h d", d=HD)
                eng.wait_ge(t1_ev, 2 * (ch + 1))
                wait(eng, yd_ready, ch)
                wait(eng, st_ready, ch)
                eng.tensor_tensor(xdt[0:M], xh, bc(dt_[0:M, ch, :].unsqueeze(2), [M, HEADS, HD]), ALU.mult)\
                   .then_inc(xd_ready, 1)
                eng.tensor_tensor(xde[0:M], xh, bc(dedt[0:M, ch, :].unsqueeze(2), [M, HEADS, HD]), ALU.mult)\
                   .then_inc(xd_ready, 1)
                if 0 < ch < 8:
                    eng.wait_ge(h_upd, ch)
                    eng.tensor_tensor(hc[:, :].rearrange("p (h d) -> p h d", d=HD),
                                      hT[:, :].rearrange("p (h d) -> p h d", d=HD),
                                      bc(cd[:, ch, :].unsqueeze(2), [P, HEADS, HD]), ALU.mult).then_inc(hc_ready, 1)
                eng.wait_ge(y_ev, ch + 1)
                sl = slice(ch * P, ch * P + M)
                eng.tensor_tensor(xs[:, :, sl], xs[:, :, sl], z[:, :, sl], ALU.mult).then_inc(g_done, 1)
            eng.wait_ge(s_h0t, 2 * NB)
            for j in range(YT):
                eng.tensor_tensor(h0[:, :, j, :], h0[:, :, j, :],
                                  bc(ea_s[:, j, NS:NS + NB].unsqueeze(2), [P, NB, ST]), ALU.mult).then_inc(s_h0s, 1)
            for n in range(NT):
                norm_lo(2, n, src=xs, half=3, off=2)
            for p in range(4):
                lo_pair(U_OUT + 4 + 2 * p)
            for n in range(NT):
                norm_lo(3, n)
            for p in range(4):
                lo_pair(U_XQ + 4 + 2 * p)
            for p in range(4):
                lo_pair(U_XO + 4 + 2 * p)
            for n in range(NT):
                norm_lo(4, n)
            body = ffn_loop(U_F2, 1)
            with eng.Fori(0, CHUNKS - 1) as i:
                body(i)
            body(CHUNKS - 1)

        @block.scalar
        def _(eng):
            c = [0]

            def hi_unit(u0, j, i):
                w = u0 + j
                slot, ring = w % 6, w % 3
                if isinstance(i, int) and w + 6 * i >= U_END:
                    return
                wait_used(eng, w - 6, i)
                eng.wait_ge(w_dma[ring], 32 * i + 16 * (w // 3 + 1))
                eng.activation(w_hi[:, slot, :], w_raw[:, ring, :], ACT.Copy).then_inc(w_hid, 1)

            def hi_pair(w):
                hi_unit(w, 0, 0)
                hi_unit(w, 1, 0)

            def link(ins):
                c[0] += 1
                ins.then_inc(act_c, 1)
                eng.wait_ge(act_c, c[0])

            def norm_sq(v, n, src, K=KT):
                w = 3 * v + n
                wait(eng, n_st, w)
                eng.activation(sq[:, 0:K, :], src[:, 0:K, cols(n)], ACT.Square).then_inc(n_sq, 1)

            def norm_hi(v, n, half, src=None, H=4, off=0):
                w = 3 * v + n
                eng.wait_ge(n_hf, 2 * w + half + 1)
                k = slice(H * half, H * half + H)
                s = hf[:, k, :] if src is None else src[:, k, cols(n)]
                eng.activation(h_hi[:, off + H * half:off + H * half + H, cols(n)], s, ACT.Copy).then_inc(n_hi, 1)

            eng.wait_ge(s_mem, 16)
            for t in range(2):
                eng.activation(sq[:, 0:3, 0:TN].rearrange("p a b -> p (a b)")[:, 0:D], mem[:, t, :], ACT.Square,
                               accum_out=nrm[:, 3, t:t + 1]).then_inc(mem_a, 1)
                eng.wait_ge(mem_a, t + 1)
            hi_pair(0)
            hi_pair(2)
            eng.wait_ge(mem_d, 6)
            eng.activation(mem_hi[:, :, :], memf[:, :, :], ACT.Copy).then_inc(mem_a, 1)

            def x_evac(t):
                M = P if t < 8 else NS
                eng.wait_ge(tr_ready, 4 + 2 * t + 1)
                eng.activation(x[:, 0:4, t * P:t * P + M],
                               bank[4][:, :].rearrange("p (k m) -> p k m", k=4)[:, :, 0:M], ACT.Copy).then_inc(tr_act, 1)

            def kv_evac(dst, base_):
                eng.wait_ge(kv_used, 8 * (base_ + 1))
                for h in range(2):
                    eng.activation(dst[:, 0, 512 * h:512 * h + 512], bank[h][:, :], ACT.Copy).then_inc(kv_act, 1)

            for k in range(8):
                if k % 2 == 0:
                    hi_pair(U_K + 4 + k)
                x_evac(k)
            kv_evac(ktok, 0)
            x_evac(8)
            for k in range(8):
                if k % 2 == 0:
                    hi_pair(U_V + 4 + k)
                if k == 2:
                    eng.wait_ge(tr_act, 9)
                    eng.wait_ge(tr_dve, 9)
                    norm_sq(0, 0, x)
                if k == 6:
                    norm_sq(0, 1, x)
            kv_evac(vtok, 1)
            eng.wait_ge(s_ktout, 16)
            norm_hi(0, 0, 0)
            norm_hi(0, 0, 1)
            norm_sq(0, 2, x)
            for n in (1, 2):
                norm_hi(0, n, 0)
                norm_hi(0, n, 1)
            eng.wait_ge(s_kvout, 32)

            def ffn(u0, f, i):
                for stage in range(2):
                    hi_unit(u0, 4 + 2 * stage, i)
                    hi_unit(u0, 5 + 2 * stage, i)
                    for n in range(NT):
                        gl = 3 * stage + n
                        gi = 66 * f + gl + 6 * i
                        eng.wait_ge(f_g, gi + 1)
                        wait(eng, f_p, gi - 1)
                        eng.activation(gate[:, gl % 2, :], bank[gl % 2][:, 0:TN], ACT.Silu).then_inc(f_s, 1)
                        eng.wait_ge(f_p, gi + 1)
                        wait(eng, f_d, 264 * f + 24 * i - 24 + 8 * (n + 1))
                        eng.activation(mid_hi[:, stage, cols(n)], prod[:, gl % 2, :], ACT.Copy).then_inc(f_mh, 1)
                hi_unit(u0, 8, i)
                hi_unit(u0, 9, i)

            F_X1 = 24 * CHUNKS
            F_X2 = 2 * 24 * CHUNKS + 48

            ffn(U_F1, 0, 0)
            with eng.Fori(1, CHUNKS) as i:
                ffn(U_F1, 0, i)
            for n in range(2):
                eng.wait_ge(f_x, F_X1 - 24 + 8 * (n + 1))
                norm_sq(1, n, x)
            norm_hi(1, 0, 0)
            norm_hi(1, 0, 1)
            eng.wait_ge(f_x, F_X1)
            norm_sq(1, 2, x)
            for n in (1, 2):
                norm_hi(1, n, 0)
                norm_hi(1, n, 1)
            eng.wait_ge(s_wdt, 16 * 4)
            eng.activation(wdt_hi[:, :, :], wdt[:, :, :], ACT.Copy).then_inc(s_wdtr, 1)
            eng.wait_ge(s_spill, 48)
            pj = 0
            for pair in range(9):
                hi_pair(U_IN + 4 + 2 * pair)
                if pair == 6 + 1:
                    eng.wait_ge(pmix, 2)
                    for i in range(2):
                        for n in range(NT):
                            eng.wait_ge(pmm, 3 * i + n + 1)
                            eng.activation(pool_out[:, i, cols(n)], bank[6][:, 0:TN],
                                           ACT.Copy, scale=par[:, PSC + i:PSC + i + 1]).then_inc(po_hi, 1)
                for n in range(NT):
                    for mm in range(2):
                        m = 2 * pair + mm
                        src = bank[pj % 4]
                        eng.wait_ge(p_ready, pj + 1)
                        if pair < 5:
                            dst = pre[mm]
                            if n == 0 and m >= 2:
                                eng.wait_ge(conv_done, m - 1)
                                eng.wait_ge(tail_t, m - 1)
                            a = 3 + n * TN
                            w = TN if n < 2 else LASTP
                            ins = eng.activation(dst[:, a:a + w], src[:, 0:w], ACT.Copy)
                            if n == 2:
                                eng.activation(fresh[:, mm, 0:24].rearrange("p (b t) -> p b t", t=3),
                                               src[:, LASTP:TN].rearrange("p (b t) -> p b t", t=SL)[:, :, 1:], ACT.Copy)
                                ins = eng.activation(
                                    dst[:, 3 + SEQ:].rearrange("p (b t) -> p b t", t=7)[:, :, 3:7],
                                    src[:, LASTP:TN].rearrange("p (b t) -> p b t", t=SL), ACT.Copy)
                                ins.then_inc(pre_ready, 1)
                                eng.wait_ge(pre_ready, m + 1)
                                eng.sem_inc(p_free, 1)
                            else:
                                ins.then_inc(p_free, 1)
                        elif pair == 5:
                            dst = ue[mm]
                            a = PBUF + n * TN
                            w = TN if n < 2 else LASTP
                            if n == 0:
                                eng.wait_ge(s_stc, 2)
                            ins = eng.activation(dst[:, a:a + w], src[:, 0:w], ACT.Copy)
                            if n == 2:
                                if mm == 0:
                                    eng.wait_ge(tail_t, 10)
                                eng.activation(fresh[:, mm, :], src[:, LASTP:TN], ACT.Copy)
                                ins = eng.activation(
                                    dst[:, PBUF + SEQ:].rearrange("p (b t) -> p b t", t=PBUF + SL)[:, :, PBUF:],
                                    src[:, LASTP:TN].rearrange("p (b t) -> p b t", t=SL), ACT.Copy)
                                ins.then_inc(ue_ready, 1)
                                eng.wait_ge(ue_ready, mm + 1)
                                eng.sem_inc(p_free, 1)
                            else:
                                ins.then_inc(p_free, 1)
                        else:
                            if n == 0:
                                eng.wait_ge(conv_done, 10)
                            ins = eng.activation(z[:, m - 12, cols(n)], src[:, 0:TN], ACT.Silu)
                            ins.then_inc(z_ready, 1)
                            eng.wait_ge(z_ready, pj - 36 + 1)
                            eng.sem_inc(p_free, 1)
                        pj += 1
                    if n == 1 and 1 <= pair <= 5:
                        for m in (2 * pair - 2, 2 * pair - 1):
                            eng.wait_ge(conv_done, m + 1)
                            d = xs[:, m, :] if m < 6 else bcT[:, m - 6, :]
                            eng.activation(d, d, ACT.Silu).then_inc(xbc_ready, 1)
            eng.wait_ge(s_dexp, 1)
            link(eng.activation(ser[2][:, :, :], ser[1][:, :, :], ACT.Exp, scale=-1.0))
            eng.sem_inc(s_dexp, 1)
            link(eng.activation(expa[:, :, :], alog[:, :, :], ACT.Exp))
            eng.sem_inc(s_dexp, 1)
            eng.wait_ge(s_dec, 1)
            np_ = 8 * HEADS
            B7 = bank[7]
            fl = lambda t: t[:, :, :].rearrange("p c h -> p (c h)")
            link(eng.activation(fl(ea)[:, 0:np_], B7[:, 0:np_], ACT.Exp))
            link(eng.activation(fl(dedt)[:, 0:np_], B7[:, np_:2 * np_], ACT.Exp))
            link(eng.activation(fl(cd)[:, 0:np_], B7[:, 2 * np_:3 * np_], ACT.Exp))
            link(eng.activation(fl(dedt)[0:NS, np_:np_ + HEADS], B7[0:NS, 3 * np_:3 * np_ + HEADS], ACT.Exp))
            link(eng.activation(ea_s[:, :, :].rearrange("p j t -> p (j t)"), bank[6][:, 0:YT * (NS + NB)], ACT.Exp))
            eng.sem_inc(s_dece, 1)
            for ch in range(9):
                M = P if ch < 8 else NS
                for j in range(2):
                    eng.wait_ge(t1, 2 * ch + j + 1)
                    if j == 0:
                        wait(eng, xd_ready, 2 * ch)
                        wait(eng, st_ready, ch)
                    eng.activation(xb[0:M, 512 * j:512 * j + 512], bank[j][0:M, :], ACT.Copy).then_inc(t1_ev, 1)
                wait(eng, yd_ready, ch)
                if ch < 8:
                    for j in range(3):
                        eng.wait_ge(seg_ready, 3 * ch + j + 1)
                        eng.activation(ew[:, 512 * j:512 * j + 512], bank[2 + j][:, :], ACT.Exp).then_inc(e_done, 1)
                else:
                    eng.wait_ge(seg_ready, 25)
                    eng.activation(ew[0:NS, 0:HEADS * NS], bank[2][0:NS, 0:HEADS * NS], ACT.Exp).then_inc(e_done, 1)
                if ch == 7:
                    eng.wait_ge(s_ho, 1)
                    eng.wait_ge(yc_done, 8)
                    eng.activation(hout[:, 0:4, :].rearrange("p j n -> p (j n)"), bank[7][:, :], ACT.Copy)
                    eng.activation(hout[:, 4:6, :].rearrange("p j n -> p (j n)"), bank[1][:, 0:256], ACT.Copy)\
                       .then_inc(s_hoc, 1)
            for b in range(NB):
                eng.wait_ge(s_h0t, 2 * b + 1)
                wait(eng, yo_ready, 7 + b - 1)
                eng.activation(h0T[:, b % 2, 0:512], bank[0][:, :], ACT.Copy).then_inc(s_h0a, 1)
            for n in range(NT):
                if n == 0:
                    eng.wait_ge(g_done, 9)
                norm_sq(2, n, xs, K=YT)
                if n == 0:
                    eng.wait_ge(s_h0o, 16 * (YT + 1))
                    eng.activation(h_hi[:, 0:2, :], pool_out[:, :, :], ACT.Copy).then_inc(po_hi, 1)
                for half in range(2):
                    norm_hi(2, n, half, src=xs, H=3, off=2)
            for pair in range(4):
                hi_pair(U_OUT + 4 + 2 * pair)
            for n in range(NT):
                if n == 0:
                    eng.wait_ge(f_x, F_X1 + 24)
                norm_sq(3, n, x)
                for half in range(2):
                    norm_hi(3, n, half)
            for pair in range(4):
                hi_pair(U_XQ + 4 + 2 * pair)
                for n in range(NT):
                    for mm in range(2):
                        eng.wait_ge(p_ready, pj + 24 + 1)
                        if pair == 0 and n == 0 and mm == 0:
                            eng.wait_ge(n_lop, 12)
                            eng.wait_ge(n_lod, 12)
                        eng.activation(q[:, 2 * pair + mm, cols(n)], bank[(pj + 24) % 4][:, 0:TN], ACT.Copy)\
                           .then_inc(q_ready, 1)
                        eng.wait_ge(q_ready, 6 * pair + 2 * n + mm + 1)
                        eng.sem_inc(p_free, 1)
                        pj += 1
            pj += 24
            def att_o(i):
                eng.wait_ge(a_o, i + 1)
                t, h = divmod(i, MH)
                eng.activation(h_hi[:, 2 * h:2 * h + 2, t * P:(t + 1) * P],
                               bank[(2, 5)[i % 2]][:, 0:256].rearrange("p (j t) -> p j t", j=2),
                               ACT.Copy).then_inc(a_oh, 1)

            def sample_keys(b):
                for g in range(4):
                    eng.wait_ge(b_t, 4 * b + g + 1)
                    if g == 0:
                        wait(eng, b_s, b)
                    eng.activation(kTs[:, 2 * g:2 * g + 2, :].rearrange("p a b -> p (a b)"), bank[(3, 6)[g % 2]][:, :],
                                   ACT.Copy).then_inc(b_ta, 1)

            for t in range(8):
                for h in range(MH):
                    i = MH * t + h
                    eng.wait_ge(a_m, t + 1)
                    wait(eng, a_t, i - 1)
                    wait(eng, a_n, i - 1)
                    eng.activation(pr[i % 2][:, :], bank[h // 2][:, 256 * (h % 2):256 * (h % 2) + 256],
                                   ACT.Exp, bias=amax[:, 4 * (t % 2) + h:4 * (t % 2) + h + 1], scale=ATT_SCALE,
                                   accum_out=amax[:, 8 + i % 2:9 + i % 2]).then_inc(a_e, 1)
                    if i >= 2:
                        att_o(i - 2)
                if t < 4:
                    sample_keys(2 * t)
                    sample_keys(2 * t + 1)
                if t == 4:
                    eng.wait_ge(b_d, 2)
                    eng.activation(p_s[:, :], bank[7][:, 256:512], ACT.Exp, bias=amax[:, 10:11], scale=ATT_SCALE,
                                   accum_out=amax[:, 11:12]).then_inc(b_e, 1)
            att_o(30)
            att_o(31)
            eng.wait_ge(b_v, NB)
            eng.activation(h_hi[:, :, SEQ:T], bank[7][:, 0:256].rearrange("p (j t) -> p j t", j=KT), ACT.Copy)\
               .then_inc(a_oh, 1)
            for pair in range(4):
                hi_pair(U_XO + 4 + 2 * pair)
            for n in range(NT):
                if n == 0:
                    eng.wait_ge(f_x, 2 * F_X1 + 48 - F_X1)
                norm_sq(4, n, x)
                for half in range(2):
                    norm_hi(4, n, half)
            ffn(U_F2, 1, 0)
            with eng.Fori(1, CHUNKS - 1) as i:
                ffn(U_F2, 1, i)
            ffn(U_F2, 1, CHUNKS - 1)
            for n in range(NT):
                eng.wait_ge(f_x, F_X2 - 24 + 8 * (n + 1))
                norm_sq(5, n, x)
            for t in range(9):
                M = P if t < 8 else NS
                eng.wait_ge(y_t, 2 * t + 1)
                if t >= 2:
                    eng.wait_ge(s_y[t % 2], 16 * (t // 2))
                eng.activation(yrow[0:M, t % 2, 0:512], bank[0][0:M, :], ACT.Copy).then_inc(y_c, 1)

        @block.vector
        def _(eng):
            c = [0]

            def link(ins):
                c[0] += 1
                ins.then_inc(dve_c, 1)
                eng.wait_ge(dve_c, c[0])
                return ins

            def newton(ms, y, s, last):
                link(eng.tensor_scalar(y.bitcast(I32), ms.bitcast(I32), 1, None, ALU.logical_shift_right))
                link(eng.tensor_scalar(y.bitcast(I32), y.bitcast(I32), -1.0, float(0x5F3759DF), ALU.mult, ALU.add))
                for step in range(4):
                    link(eng.tensor_tensor(s, y, y, ALU.mult))
                    link(eng.scalar_tensor_tensor(out=s, in0=s, scalar=-0.5, in1=ms, op0=ALU.mult, op1=ALU.mult))
                    link(eng.scalar_tensor_tensor(out=y, in0=s, scalar=1.5, in1=y, op0=ALU.add, op1=ALU.mult))

            def norm_rs(v, n, width):
                w = 3 * v + n
                eng.wait_ge(n_st, w + 1)
                ms, y, s = nrm[:, 0, 0:3], nrm[:, 1, 0:3], nrm[:, 2, 0:3]
                link(eng.tensor_scalar(ms, bank[6][:, 0:3], 1.0 / width, EPS, ALU.mult, ALU.add))
                newton(ms, y, s, None)
                wait(eng, n_bc, w)
                eng.tensor_tensor(diag[:, :].rearrange("p (a b) -> p a b", a=3),
                                  bc(ident[:, :].unsqueeze(1), [P, 3, P]), bc(y.unsqueeze(2), [P, 3, P]), ALU.mult)\
                   .then_inc(n_rs, 1)

            def norm_hf(v, n, k, g, src, dst=None, K=KT):
                w = 3 * v + n
                if k == 0:
                    eng.wait_ge(n_bc, w + 1)
                    if dst is None:
                        wait(eng, n_lop, w)
                        wait(eng, n_lod, w)
                out = hf[:, k, :] if dst is None else dst[:, k, cols(n)]
                ins = eng.scalar_tensor_tensor(out=out, in0=src[:, k, cols(n)], scalar=par[:, g + k:g + k + 1],
                                               in1=bank[7][:, P:P + TN], op0=ALU.mult, op1=ALU.mult)
                if k % (K // 2) == K // 2 - 1:
                    ins.then_inc(n_hf, 1)

            def norm_lo(v, n, src=None, H=4, off=0):
                w = 3 * v + n
                eng.wait_ge(n_hi, 2 * w + 2)
                s = hf[:, H:2 * H, :] if src is None else src[:, H:2 * H, cols(n)]
                o = slice(off + H, off + 2 * H)
                eng.tensor_tensor(h_lo[:, o, cols(n)], s, h_hi[:, o, cols(n)].bitcast(F32), ALU.subtract)\
                   .then_inc(n_lod, 1)

            eng.wait_ge(s_part, 1)
            link(eng.tensor_copy(par[:, :], bank[6][:, 0:NPAR]))
            eng.wait_ge(mem_a, 2)
            link(eng.tensor_scalar(nrm[:, 0, 0:2], nrm[:, 3, 0:2], 1.0 / D, EPS, ALU.mult, ALU.add))
            newton(nrm[:, 0, 0:2], nrm[:, 1, 0:2], nrm[:, 2, 0:2], None)
            for t in range(2):
                eng.tensor_scalar(mem[:, t, :], mem[:, t, :], nrm[:, 1, t:t + 1], None, ALU.mult).then_inc(mem_d, 1)
            for g in range(4):
                t, h = divmod(g, 2)
                eng.wait_ge(tr_ready, g + 1)
                eng.tensor_tensor(memf[:, 4 * h:4 * h + 4, t * P:(t + 1) * P],
                                  bank[4 + g % 2][:, :].rearrange("p (k m) -> p k m", k=4),
                                  bc(par[:, GMEM + 4 * h:GMEM + 4 * h + 4].unsqueeze(2), [P, 4, P]), ALU.mult)\
                   .then_inc(mem_d, 1)
            eng.wait_ge(mem_d, 6)
            eng.wait_ge(mem_a, 3)
            eng.tensor_tensor(mem_lo[:, :, :], memf[:, :, :], mem_hi[:, :, :].bitcast(F32), ALU.subtract)\
               .then_inc(mem_d, 1)

            def x_evac(t):
                M = P if t < 8 else NS
                eng.wait_ge(tr_ready, 4 + 2 * t + 2)
                eng.tensor_copy(x[:, 4:8, t * P:t * P + M],
                                bank[5][:, :].rearrange("p (k m) -> p k m", k=4)[:, :, 0:M]).then_inc(tr_dve, 1)

            def kv_evac(dst, base_):
                eng.wait_ge(kv_used, 8 * (base_ + 1))
                for h in range(2):
                    eng.tensor_copy(dst[:, 1, 512 * h:512 * h + 512], bank[2 + h][:, :]).then_inc(kv_dve, 1)

            for k in range(8):
                x_evac(k)
            kv_evac(ktok, 0)
            x_evac(8)
            for g in range(4):
                t, h = divmod(g, 2)
                eng.wait_ge(kt_ready, g + 1)
                eng.tensor_copy(kT0[:, 4 * h:4 * h + 4, t * P:(t + 1) * P],
                                bank[6][:, :].rearrange("p (k m) -> p k m", k=4)).then_inc(kt_copied, 1)
            norm_rs(0, 0, D)
            for k in range(KT):
                norm_hf(0, 0, k, G1, x)
            kv_evac(vtok, 1)
            norm_lo(0, 0)
            for n in (1, 2):
                norm_rs(0, n, D)
                for k in range(KT):
                    norm_hf(0, n, k, G1, x)
                norm_lo(0, n)

            def ffn_products(f, i):
                for stage in range(2):
                    for n in range(NT):
                        gl = 3 * stage + n
                        gi = 66 * f + gl + 6 * i
                        eng.wait_ge(f_s, gi + 1)
                        eng.wait_ge(f_u, gi + 1)
                        wait(eng, f_ml, gi - 1)
                        eng.tensor_tensor(prod[:, gl % 2, :], gate[:, gl % 2, :], bank[2 + gl % 2][:, 0:TN], ALU.mult)\
                           .then_inc(f_p, 1)

            def ffn_add(f, i, n, m):
                dl = 8 * n + m
                eng.wait_ge(f_d, 264 * f + dl + 24 * i + 1)
                xc = x[:, m, cols(n)]
                eng.scalar_tensor_tensor(out=xc, in0=bank[4 + dl % 2][:, 0:TN], scalar=0.5, in1=xc, op0=ALU.mult,
                                         op1=ALU.add).then_inc(f_x, 1)

            def ffn(f, i):
                ffn_products(f, i)
                for n in range(NT):
                    for m in range(KT):
                        ffn_add(f, i, n, m)

            def ffn_last(f, v, g, width, split=True):
                i = CHUNKS - 1
                ffn_products(f, i)
                for m in range(KT):
                    ffn_add(f, i, 0, m)
                for m in range(4):
                    ffn_add(f, i, 1, m)
                norm_rs(v, 0, width)
                for m in range(4, 8):
                    ffn_add(f, i, 1, m)
                eng.wait_ge(f_x, FX[f] - 16)
                for m in range(4):
                    ffn_add(f, i, 2, m)
                    norm_hf(v, 0, m, g, x)
                norm_rs(v, 1, width)
                for m in range(4, 8):
                    ffn_add(f, i, 2, m)
                    norm_hf(v, 0, m, g, x)

            FX = (24 * CHUNKS, 2 * 24 * CHUNKS + 48)
            ffn(0, 0)
            with eng.Fori(1, CHUNKS - 1) as i:
                ffn(0, i)
            ffn_last(0, 1, GMIX, D)
            norm_lo(1, 0)
            for k in range(KT):
                norm_hf(1, 1, k, GMIX, x)
            norm_lo(1, 1)
            norm_rs(1, 2, D)
            for k in range(KT):
                norm_hf(1, 2, k, GMIX, x)
            norm_lo(1, 2)
            eng.wait_ge(s_spill, 48)
            for i in range(2):
                link(eng.memset(pre[i][:, 0:3], 0.0))
            eng.wait_ge(s_stT, 1)
            link(eng.tensor_copy(convT[:, :, :, :].rearrange("p m b t -> p (m b t)"), bank[5][:, 0:240]))
            link(eng.tensor_copy(poolT[:, :, :, :].rearrange("p m b t -> p (m b t)"), bank[5][:, 240:480]))
            eng.sem_inc(s_stc, 1)
            eng.wait_ge(s_wpz, 2)
            link(eng.tensor_copy(ramp[:, 0, :], ramp_i[:, :]))
            link(eng.tensor_copy(ramp[:, 1, :], ramp[:, 0, :]))
            for g, wn in enumerate(WINDOWS):
                r = ramp[64 * (g % 2):64 * (g % 2) + 64, g // 2, :]
                link(eng.tensor_scalar(r, r, float(wn), 1.0 / wn, ALU.min, ALU.mult))
            link(eng.reciprocal(ramp[:, :, :], ramp[:, :, :]))
            eng.sem_inc(s_stc, 1)

            def conv(m):
                pc = pre[m % 2]
                ps = pc[:, 3 + SEQ:].rearrange("p (b t) -> p b t", t=7)
                if m >= 2:
                    eng.wait_ge(conv_done, m - 1)
                link(eng.tensor_copy(ps[:, :, 0:3], convT[:, m, :, :]))
                eng.wait_ge(pre_ready, m + 1)
                d = xs[:, m, :] if m < 6 else bcT[:, m - 6, :]
                ds_ = d[:, SEQ:T].rearrange("p (b t) -> p b t", t=SL)
                for k in range(4):
                    wk = par[:, CW + 10 * k + m:CW + 10 * k + m + 1]
                    if k == 0:
                        bias = par[:, CB + m:CB + m + 1]
                        eng.tensor_scalar(d[:, 0:SEQ], pc[:, 0:SEQ], wk, bias, ALU.mult, ALU.add)
                        link(eng.tensor_scalar(ds_, ps[:, :, 0:SL], wk, bias, ALU.mult, ALU.add))
                    else:
                        eng.scalar_tensor_tensor(out=d[:, 0:SEQ], in0=pc[:, k:k + SEQ], scalar=wk, in1=d[:, 0:SEQ],
                                                 op0=ALU.mult, op1=ALU.add)
                        ins = eng.scalar_tensor_tensor(out=ds_, in0=ps[:, :, k:k + SL], scalar=wk, in1=ds_,
                                                       op0=ALU.mult, op1=ALU.add)
                        if k < 3:
                            link(ins)
                        else:
                            ins.then_inc(conv_done, 1)

            def tail(m):
                eng.wait_ge(tail_t, m // 2 * 2 + 2)
                s = m % 2
                if m >= 2:
                    eng.wait_ge(tail_d[s], 32 * (m // 2))
                np_, ns_ = (3, 24) if m < 10 else (PBUF, NS)
                eng.tensor_copy(tails[0:np_, s, 0:P], bank[5][0:np_, 256 * s:256 * s + P])
                eng.tensor_copy(tails[0:ns_, s, P:2 * P], bank[5][0:ns_, 256 * s + P:256 * s + 256])\
                   .then_inc(tail_c, 1)

            for pair in range(5):
                for m in (2 * pair, 2 * pair + 1):
                    conv(m)
                for m in (2 * pair, 2 * pair + 1):
                    tail(m)
            for i in range(2):
                u_ = ue[i]
                us = u_[:, PBUF + SEQ:].rearrange("p (b t) -> p b t", t=PBUF + SL)
                eng.wait_ge(ue_ready, i + 1)
                eng.memset(u_[:, 0:PBUF], 0.0)
                link(eng.tensor_copy(us[:, :, 0:PBUF], poolT[:, i, :, :]))
                L = NUE

                def shift_add(dst, src, d, lo_):
                    link(eng.tensor_tensor(dst[:, lo_:L], src[:, lo_:L], src[:, lo_ - d:L - d], ALU.add))

                if i == 0:
                    link(eng.memset(win_a[:, 0:PBUF], 0.0))
                    link(eng.memset(win_b[:, 0:PBUF], 0.0))
                shift_add(win_a, u_, 1, 1)
                shift_add(win_b, win_a, 2, 3)
                if i == 1:
                    shift_add(win_a, win_b, 4, 7)
                    shift_add(win_b, win_a, 8, 15)
                if i == 0:
                    eng.wait_ge(tail_t, 12)
                for half, wn in ((0, WINDOWS[2 * i]), (1, WINDOWS[2 * i + 1])):
                    r = slice(64 * half, 64 * half + 64)
                    s = (win_a, win_b)[half]
                    link(eng.tensor_tensor(s[r, PBUF:2 * PBUF], s[r, PBUF:2 * PBUF], ramp[r, i, :], ALU.mult))
                    link(eng.scalar_tensor_tensor(out=(u_, win_a)[i][r, PBUF:], in0=s[r, PBUF:], scalar=1.0 / wn,
                                                  in1=u_[r, PBUF:], op0=ALU.mult, op1=ALU.subtract))
                eng.sem_inc(pmix, 1)
            for m in (10, 11):
                tail(m)
            eng.wait_ge(z_ready, 6 * NT)
            eng.wait_ge(dt_ready, 1)
            raw, ab, e_, r_, zz, qq, mx = ser
            link(eng.memset(raw[:, :, :], 0.0))
            np_ = 8 * HEADS
            link(eng.tensor_tensor(raw[:, 0:8, :], bank[4][:, 0:np_].rearrange("p (c h) -> p c h", h=HEADS),
                                   bc(dtb[:, :, :], [P, 8, HEADS]), ALU.add))
            link(eng.tensor_tensor(raw[0:NS, 8, :], bank[4][0:NS, np_:np_ + HEADS], dtb[0:NS, 0, :], ALU.add))
            link(eng.scalar_tensor_tensor(out=ab[:, :, :], in0=raw[:, :, :], scalar=-1.0, in1=raw[:, :, :],
                                          op0=ALU.mult, op1=ALU.max))
            eng.sem_inc(s_dexp, 1)
            link(eng.tensor_scalar(mx[:, :, :], raw[:, :, :], 0.0, None, ALU.max))
            eng.wait_ge(s_dexp, 2)
            link(eng.tensor_scalar(r_[:, :, :], e_[:, :, :], 2.0, None, ALU.add))
            link(eng.reciprocal(r_[:, :, :], r_[:, :, :]))
            link(eng.tensor_tensor(r_[:, :, :], e_[:, :, :], r_[:, :, :], ALU.mult))
            link(eng.tensor_tensor(zz[:, :, :], r_[:, :, :], r_[:, :, :], ALU.mult))
            link(eng.tensor_scalar(qq[:, :, :], zz[:, :, :], 1.0 / 17, None, ALU.mult))
            for k in (15, 13, 11, 9, 7, 5, 3):
                link(eng.scalar_tensor_tensor(out=qq[:, :, :], in0=qq[:, :, :], scalar=1.0 / k, in1=zz[:, :, :],
                                              op0=ALU.add, op1=ALU.mult))
            link(eng.scalar_tensor_tensor(out=qq[:, :, :], in0=qq[:, :, :], scalar=1.0, in1=r_[:, :, :],
                                          op0=ALU.add, op1=ALU.mult))
            link(eng.scalar_tensor_tensor(out=dt_[:, :, :], in0=qq[:, :, :], scalar=2.0, in1=mx[:, :, :],
                                          op0=ALU.mult, op1=ALU.add))
            eng.wait_ge(s_dexp, 3)
            link(eng.scalar_tensor_tensor(out=dta[:, :, :], in0=dt_[:, :, :], scalar=-1.0,
                                          in1=bc(expa[:, :, :], [P, NTT, HEADS]), op0=ALU.mult, op1=ALU.mult))
            link(eng.tensor_copy(dtab[:, :, :], bc(dta[0:NS, 8, :].unsqueeze(2), [NS, HEADS, HD])))
            eng.sem_inc(s_decd, 1)
            eng.wait_ge(s_dece, 1)
            link(eng.tensor_tensor(dedt[:, 0:8, :], dedt[:, 0:8, :], dt_[:, 0:8, :], ALU.mult))
            link(eng.tensor_tensor(dedt[0:NS, 8, :], dedt[0:NS, 8, :], dt_[0:NS, 8, :], ALU.mult))
            eng.sem_inc(s_decd, 1)
            eng.wait_ge(s_wdt, 16 * 4)
            for e in range(2):
                link(eng.tensor_copy(dskip[64 * e:64 * e + 64, :],
                                     dsk_all[64 * e:64 * e + 64, :].rearrange("p (j e) -> p e j", e=2)[:, e, :]))

            def make_ud(ch):
                M = P if ch < 8 else NS
                if ch:
                    eng.wait_ge(seg_ready, 3 * ch)
                tri = upper[:, :] if ch < 8 else up_s[:, 0:NS]
                if ch == 8:
                    eng.wait_ge(s_mask, 1)
                eng.tensor_tensor(ud[0:M, 0:HEADS * M].rearrange("p (h l) -> p h l", h=HEADS),
                                  bc(tri.unsqueeze(1), [M, HEADS, M]),
                                  bc(dta[0:M, ch, :].unsqueeze(2), [M, HEADS, M]), ALU.mult).then_inc(ud_ready, 1)

            make_ud(0)
            for ch in range(9):
                M = P if ch < 8 else NS
                tok = slice(ch * P, ch * P + M)
                tri = upper[:, :] if ch < 8 else up_s[:, 0:NS]
                eng.wait_ge(sc_ready, ch + 1)
                wait(eng, wg_ready, 2 * ch)
                link(eng.tensor_tensor(sm[0:M, 0:2 * M].rearrange("p (g l) -> p g l", g=2),
                                       bank[0][0:M, 0:2 * M].rearrange("p (g l) -> p g l", g=2),
                                       bc(tri.unsqueeze(1), [M, 2, M]), ALU.mult))
                eng.sem_inc(sm_done, 1)
                eng.wait_ge(e_done, 3 * (ch + 1) if ch < 8 else 25)
                for g in range(2):
                    e3 = ew[0:M, g * HG * M:(g + 1) * HG * M].rearrange("p (h l) -> p h l", h=HG)
                    eng.tensor_tensor(e3, e3, bc(sm[0:M, g * M:(g + 1) * M].unsqueeze(1), [M, HG, M]), ALU.mult)\
                       .then_inc(wg_ready, 1)
                if ch < 8:
                    make_ud(ch + 1)
                eng.wait_ge(yd_ready, ch + 1)
                wait(eng, yt_ready, ch)
                if 0 < ch < 8:
                    eng.wait_ge(yo_ready, ch)
                    for g in range(2):
                        link(eng.tensor_tensor(
                            ytmp[:, 384 * g:384 * g + 384].rearrange("p (h d) -> p h d", h=HG),
                            bank[(7, 1)[g]][:, 0:384].rearrange("p (h d) -> p h d", h=HG),
                            bc(ea[:, ch, HG * g:HG * g + HG].unsqueeze(2), [P, HG, HD]), ALU.mult))
                    for g in range(2):
                        link(eng.tensor_tensor(ytok[:, 384 * g:384 * g + 384], ytmp[:, 384 * g:384 * g + 384],
                                               bank[5 + g][:, 0:384], ALU.add))
                else:
                    for g in range(2):
                        link(eng.tensor_copy(ytok[0:M, 384 * g:384 * g + 384], bank[5 + g][0:M, 0:384]))
                eng.sem_inc(yc_done, 1)
                if ch < 8:
                    eng.wait_ge(st_ready, ch + 1)
                    if ch:
                        eng.wait_ge(hc_ready, ch)
                    for g in range(2):
                        o = hT[:, 384 * g:384 * g + 384]
                        if ch:
                            link(eng.tensor_tensor(o, hc[:, 384 * g:384 * g + 384], bank[2 + g][:, 0:384], ALU.add))
                        else:
                            link(eng.tensor_copy(o, bank[2 + g][:, 0:384]))
                    eng.sem_inc(h_upd, 1)
                eng.wait_ge(yt_ready, ch + 1)
                if ch < 8:
                    for j in range(YT):
                        ps = bank[4][:, P * j:P * j + P] if j < 4 else bank[0][:, P * (j - 4):P * (j - 4) + P]
                        ins = eng.scalar_tensor_tensor(out=xs[:, j, tok], in0=xs[:, j, tok], scalar=dskip[:, j:j + 1],
                                                       in1=ps, op0=ALU.mult, op1=ALU.add)
                    link(ins)
                    eng.sem_inc(y_ev, 1)
                else:
                    for j in range(YT):
                        link(eng.scalar_tensor_tensor(out=xs[:, j, tok], in0=xs[:, j, tok], scalar=dskip[:, j:j + 1],
                                                      in1=bank[4][:, NS * j:NS * j + NS], op0=ALU.mult, op1=ALU.add))
                    for b in range(NB):
                        eng.wait_ge(s_h0t, 2 * b + 2)
                        wait(eng, yo_ready, 7 + b - 1)
                        eng.tensor_copy(h0T[:, b % 2, 512:768], bank[1][:, 0:256]).then_inc(s_h0d, 1)
                    eng.wait_ge(yo_ready, 7 + NB)
                    eng.wait_ge(s_hoc, 1)
                    t3 = hT[:, 0:YT * NS].rearrange("p (j t) -> p j t", j=YT)
                    link(eng.tensor_tensor(t3, bank[7][:, 0:YT * NS].rearrange("p (j t) -> p j t", j=YT),
                                           ea_s[:, :, 0:NS], ALU.mult))
                    link(eng.tensor_tensor(xs[:, :, tok], xs[:, :, tok], t3, ALU.add))
                    eng.sem_inc(y_ev, 1)
            for g in range(2):
                eng.tensor_tensor(bx[:, g, :, :], bc(xb[0:NS, D_SSM + P * g:D_SSM + P * g + P].unsqueeze(1), [NS, NB, P]),
                                  bc(up_s[:, NS:NS + NB].unsqueeze(2), [NS, NB, P]), ALU.mult).then_inc(s_h0d, 1)
            for j in range(YT):
                eng.wait_ge(s_h0s, j + 1)
                for half in range(2):
                    eng.wait_ge(s_h0st, 2 * j + half + 1)
                    hb = h0[:, 4 * half:4 * half + 4, j, :]
                    eng.tensor_tensor(hb, hb, bank[(2, 3, 5, 6)[2 * (j % 2) + half]][:, :]
                                      .rearrange("p (b n) -> p b n", b=4), ALU.add).then_inc(s_h0n, 1)
            for n in range(NT):
                norm_rs(2, n, D_SSM)
                if n == 0:
                    eng.wait_ge(po_hi, 7)
                    eng.tensor_tensor(h_lo[:, 0:2, :], pool_out[:, :, :], h_hi[:, 0:2, :].bitcast(F32), ALU.subtract)\
                       .then_inc(po_lo, 1)
                for k in range(YT):
                    norm_hf(2, n, k, GSSM, xs, dst=xs, K=YT)
                norm_lo(2, n, src=xs, H=3, off=2)

            def add_out(pj, back):
                for pair in range(4):
                    for n in range(NT):
                        for mm in range(2):
                            m = 2 * pair + mm
                            if pair == 0 and mm == 0:
                                eng.wait_ge(s_back[n], 16 * (back + 1))
                            eng.wait_ge(p_ready, pj + 1)
                            xc = x[:, m, cols(n)]
                            link(eng.tensor_tensor(xc, xc, bank[pj % 4][:, 0:TN], ALU.add))
                            eng.sem_inc(p_free, 1)
                            eng.sem_inc(f_x, 1)
                            pj += 1
                return pj

            pj = add_out(54, 0)
            for n in range(NT):
                norm_rs(3, n, D)
                for k in range(KT):
                    norm_hf(3, n, k, GXQ, x)
                norm_lo(3, n)
            pj += 24

            def sample_scores_out():
                eng.wait_ge(b_s, NB)
                link(eng.tensor_copy(s_s[:, :, :].rearrange("p a b -> p (a b)"), bank[7][:, 0:256]))
                eng.sem_inc(b_d, 1)
                eng.wait_ge(b_r, 1)
                link(eng.tensor_reduce(amax[:, 10:11], bank[7][:, 256:512], AX.X, ALU.max))
                link(eng.tensor_scalar(amax[:, 10:11], amax[:, 10:11], -ATT_SCALE, None, ALU.mult))
                eng.sem_inc(b_d, 1)
                eng.wait_ge(b_e, 1)
                link(eng.reciprocal(amax[:, 11:12], amax[:, 11:12]))
                link(eng.tensor_scalar(p_s[:, :], p_s[:, :], amax[:, 11:12], None, ALU.mult))
                eng.sem_inc(b_d, 1)
                eng.wait_ge(b_r, 2)
                eng.tensor_copy(pT_s[:, :, :].rearrange("p a b -> p (a b)"), bank[7][:, 256:512]).then_inc(b_d, 1)

            def att_lo(i):
                eng.wait_ge(a_oh, i + 1)
                t, h = divmod(i, MH)
                tk = slice(t * P, (t + 1) * P)
                eng.tensor_tensor(h_lo[:, 2 * h:2 * h + 2, tk],
                                  bank[(2, 5)[i % 2]][:, 0:256].rearrange("p (j t) -> p j t", j=2),
                                  h_hi[:, 2 * h:2 * h + 2, tk].bitcast(F32), ALU.subtract).then_inc(a_ol, 1)

            for t in range(8):
                mcol = 4 * (t % 2)
                wait(eng, a_e, MH * (t - 1))
                for hb in range(2):
                    eng.wait_ge(a_s, MH * t + 2 * hb + 2)
                    link(eng.tensor_reduce(amax[:, mcol + 2 * hb:mcol + 2 * hb + 2],
                                           bank[hb][:, :].rearrange("p (h m) -> p h m", h=2),
                                           AX.X, ALU.max))
                link(eng.tensor_scalar(amax[:, mcol:mcol + 4], amax[:, mcol:mcol + 4], -ATT_SCALE, None, ALU.mult))
                eng.sem_inc(a_m, 1)
                for h in range(MH):
                    i = MH * t + h
                    eng.wait_ge(a_e, i + 1)
                    r = amax[:, 12 + i % 2:13 + i % 2]
                    link(eng.reciprocal(r, amax[:, 8 + i % 2:9 + i % 2]))
                    eng.tensor_scalar(pr[i % 2][:, :], pr[i % 2][:, :], r, None, ALU.mult).then_inc(a_n, 1)
                    eng.wait_ge(a_t, i + 1)
                    wait(eng, a_o, i - 1)
                    eng.tensor_copy(pT[i % 2][:, :, :].rearrange("p a b -> p (a b)"),
                                    bank[4][:, 0:256]).then_inc(a_c, 1)
                    if i >= 2:
                        att_lo(i - 2)
                if t == 4:
                    sample_scores_out()
            att_lo(30)
            att_lo(31)
            eng.wait_ge(a_oh, 33)
            eng.tensor_tensor(h_lo[:, :, SEQ:T], bank[7][:, 0:256].rearrange("p (j t) -> p j t", j=KT),
                              h_hi[:, :, SEQ:T].bitcast(F32), ALU.subtract).then_inc(a_ol, 1)
            pj = add_out(pj, 1)
            for n in range(NT):
                norm_rs(4, n, D)
                for k in range(KT):
                    norm_hf(4, n, k, GF2, x)
                norm_lo(4, n)
            with eng.Fori(0, CHUNKS - 1) as i:
                ffn(1, i)
            i = CHUNKS - 1
            ffn_products(1, i)
            for n in range(NT):
                for m in range(KT):
                    ffn_add(1, i, n, m)
            for n in range(NT):
                norm_rs(5, n, D)
                if n == 0:
                    eng.wait_ge(f_x, FX[1])
                for k in range(KT):
                    norm_hf(5, n, k, GFIN, x, dst=x)
            for t in range(9):
                M = P if t < 8 else NS
                eng.wait_ge(y_t, 2 * t + 2)
                if t >= 2:
                    eng.wait_ge(s_y[t % 2], 16 * (t // 2))
                eng.tensor_copy(yrow[0:M, t % 2, 512:1024], bank[1][0:M, :]).then_inc(y_c, 1)

        @block.tensor
        def _(eng):
            def three(out, a_hi, a_lo, b_hi, b_lo, first, last):
                eng.matmul(out, a_hi, b_hi, start=first, stop=False)
                eng.matmul(out, a_hi, b_lo, start=False, stop=False)
                return eng.matmul(out, a_lo, b_hi, start=False, stop=last)

            def norm_stat(v, n, K=KT):
                w = 3 * v + n
                eng.wait_ge(n_sq, w + 1)
                wait(eng, n_rs, w)
                for j, (o, m) in enumerate(NORM_SUBS):
                    for k in range(K):
                        mm = eng.matmul(bank[6][0:m, j:j + 1], sq[:, k, o:o + m], ones[:, 0:1], start=(k == 0),
                                        stop=(k == K - 1))
                mm.then_inc(n_st, 1)

            def norm_bc(v, n):
                w = 3 * v + n
                eng.wait_ge(n_rs, w + 1)
                wait(eng, n_hf, 2 * w)
                eng.matmul(bank[7][:, P:P + TN], ones[:, :], diag[:, 0:TN], start=True, stop=True).then_inc(n_bc, 1)

            def norm_ready(v, n):
                eng.wait_ge(n_lop, 3 * v + n + 1)
                eng.wait_ge(n_lod, 3 * v + n + 1)

            eng.wait_ge(s_const, 5)
            eng.wait_ge(s_par, 16 * 10)
            eng.transpose(bank[6][:, 0:NPAR], parrow[:, :], ident[0:NPAR, 0:NPAR]).then_inc(s_part, 1)
            eng.wait_ge(mem_d, 2)
            for g in range(4):
                t, h = divmod(g, 2)
                wait(eng, mem_d, g + 1 if g >= 2 else 0)
                for k in range(4):
                    mm = eng.transpose(bank[4 + g % 2][:, k * P:(k + 1) * P], mem[:, t, (4 * h + k) * P:(4 * h + k + 1) * P],
                                       ident[:, :])
                mm.then_inc(tr_ready, 1)
            eng.wait_ge(mem_d, 6)

            def x_turn(t):
                M = P if t < 8 else NS
                eng.wait_ge(s_x[t // 2], 32 if t < 8 else 16)
                for h in range(2):
                    wait(eng, (tr_act, tr_dve)[h], t)
                    for k in range(4):
                        mm = eng.transpose(bank[4 + h][:, k * P:k * P + M],
                                           xtok[0:M, t, (4 * h + k) * P:(4 * h + k + 1) * P], ident[0:M, 0:M])
                    mm.then_inc(tr_ready, 1)

            def mem_unit(w, k):
                eng.wait_ge(w_ready, w + 1)
                s = w % 6
                for t in range(2):
                    for h in range(2):
                        ms, wc = slice(t * P, (t + 1) * P), slice(512 * h, 512 * h + 512)
                        out = bank[2 * t + h][:, :]
                        eng.matmul(out, mem_hi[:, k, ms], w_hi[:, s, wc], start=(k == 0), stop=False)
                        eng.matmul(out, mem_hi[:, k, ms], w_lo[:, s, wc], start=False, stop=False)
                        mm = eng.matmul(out, mem_lo[:, k, ms], w_hi[:, s, wc], start=False, stop=(k == KT - 1))
                mm.then_inc(kv_used, 1)
                return mm

            eng.wait_ge(mem_d, 7)
            for k in range(KT):
                mem_unit(U_K + k, k)
                x_turn(k)
            x_turn(8)
            eng.wait_ge(kv_act, 2)
            eng.wait_ge(kv_dve, 2)
            for k in range(KT):
                mem_unit(U_V + k, k)
                if 1 <= k <= 4:
                    g = k - 1
                    t, h = divmod(g, 2)
                    wait(eng, kt_copied, g)
                    for kk in range(4):
                        mm = eng.transpose(bank[6][:, kk * P:(kk + 1) * P],
                                           ktok[:, t, (4 * h + kk) * P:(4 * h + kk + 1) * P], ident[:, :])
                    mm.then_inc(kt_ready, 1)
                if k == 5:
                    eng.wait_ge(kt_copied, 4)
                    norm_stat(0, 0)
                if k == 6:
                    norm_bc(0, 0)
            eng.wait_ge(kv_act, 4)
            eng.wait_ge(kv_dve, 4)

            def ffn_half(u0, f, i, stage, n, what):
                gl = 3 * stage + n
                gi = 66 * f + gl + 6 * i
                slot = (u0 + 2 * stage + what) % 6
                wait(eng, (f_s, f_p)[what], gi - 1)
                out = bank[2 * what + gl % 2][:, 0:TN]
                for k in range(KT):
                    ks = slice(k * P, (k + 1) * P)
                    mm = three(out, w_hi[:, slot, ks], w_lo[:, slot, ks], h_hi[:, k, cols(n)], h_lo[:, k, cols(n)],
                               k == 0, k == KT - 1)
                mm.then_inc((f_g, f_u)[what], 1)
                return mm

            def ffn_down(u0, f, i, n, m):
                dl = 8 * n + m
                wait(eng, f_x, FXB[f] + dl + 24 * i - 1)
                out = bank[4 + dl % 2][:, 0:TN]
                ms = slice(m * P, (m + 1) * P)
                for fi in range(2):
                    slot = (u0 + 4 + fi) % 6
                    mm = three(out, w_hi[:, slot, ms], w_lo[:, slot, ms], mid_hi[:, fi, cols(n)],
                               mid_lo[:, fi, cols(n)], fi == 0, fi == 1)
                mm.then_inc(f_d, 1)
                return mm

            FXB = (0, 24 * CHUNKS + 48)

            def ffn(u0, f, i, first=None, last=None):
                for stage in range(2):
                    eng.wait_ge(w_ready, u0 + 2 * stage + 2 + 6 * i)
                    for n in range(NT):
                        if first is not None and stage == 0:
                            norm_ready(first, n)
                            if n == 0:
                                norm_stat(first, 1) if late[0] else None
                        ffn_half(u0, f, i, stage, n, 0)
                        if first is not None and stage == 0 and n == 0:
                            if late[0]:
                                norm_bc(first, 1)
                            else:
                                norm_stat(first, 2)
                        ffn_half(u0, f, i, stage, n, 1)
                        if first is not None and stage == 0 and n == 0:
                            if late[0]:
                                norm_stat(first, 2)
                            norm_bc(first, 2)
                eng.wait_ge(w_ready, u0 + 6 + 6 * i)
                for n in range(NT):
                    eng.wait_ge(f_ml, 66 * f + 3 + n + 1 + 6 * i)
                    for m in range(KT):
                        ffn_down(u0, f, i, n, m)
                        if last is not None and m == 3:
                            if n == 1:
                                norm_stat(last, 0)
                            if n == 2:
                                norm_stat(last, 1)
                    if last is not None and n == 1:
                        norm_bc(last, 0)
                    if last is not None and n == 2:
                        norm_bc(last, 1)

            late = [True]
            ffn(U_F1, 0, 0, first=0)
            with eng.Fori(1, CHUNKS - 1) as i:
                ffn(U_F1, 0, i)
            ffn(U_F1, 0, CHUNKS - 1, last=1)

            pj = [0]

            def project(w, n, kw=False):
                wait(eng, p_free, pj[0] - 3)
                s = w % 6
                out = bank[pj[0] % 4][:, 0:TN]
                for k in range(KT):
                    ks = slice(k * P, (k + 1) * P)
                    mm = three(out, w_hi[:, s, ks], w_lo[:, s, ks], h_hi[:, k, cols(n)], h_lo[:, k, cols(n)],
                               k == 0, k == KT - 1)
                mm.then_inc(p_ready, 1)
                pj[0] += 1

            def tail_turn(m):
                s = m % 2
                wait(eng, tail_c, m // 2 * 2)
                if m < 10:
                    eng.wait_ge(pre_ready, m + 1)
                    t_ = pre[s]
                    np_, ns_ = 3, 24
                    a = t_[:, SEQ:SEQ + 3]
                    b_ = fresh[:, s, 0:24]
                else:
                    eng.wait_ge(ue_ready, m - 9)
                    t_ = ue[m - 10]
                    np_, ns_ = PBUF, NS
                    a = t_[:, SEQ:SEQ + PBUF]
                    b_ = fresh[:, s, :]
                eng.transpose(bank[5][0:np_, 256 * s:256 * s + P], a, ident[:, :])
                eng.transpose(bank[5][0:ns_, 256 * s + P:256 * s + 256], b_, ident[:, :]).then_inc(tail_t, 1)

            for pair in range(9):
                w = U_IN + 2 * pair
                eng.wait_ge(w_ready, w + 2)
                if pair == 5:
                    eng.wait_ge(s_wdtr, 2)
                    for t in range(8):
                        tk = slice(t * P, (t + 1) * P)
                        for k in range(KT):
                            three(bank[4][:, HEADS * t:HEADS * (t + 1)], h_hi[:, k, tk], h_lo[:, k, tk],
                                  wdt_hi[:, k, :], wdt_lo[:, k, :], k == 0, k == KT - 1)
                    for k in range(KT):
                        for part in range(2):
                            mm = eng.matmul(bank[4][0:NS, 8 * HEADS:9 * HEADS], (h_hi, h_lo)[part][:, k, SEQ:T].bitcast(F32),
                                            wdt[:, k, :], start=(k == 0 and part == 0), stop=(k == KT - 1 and part == 1))
                    mm.then_inc(dt_ready, 1)
                for n in range(NT):
                    if pair == 0:
                        norm_ready(1, n)
                    for mm in range(2):
                        project(w + mm, n)
                        if pair == 0 and n == 0:
                            if mm == 0:
                                norm_stat(1, 2)
                            else:
                                norm_bc(1, 2)
                    if n == 0 and 1 <= pair <= 5:
                        tail_turn(2 * pair - 2)
                        tail_turn(2 * pair - 1)
                    if n == 0 and pair == 6:
                        tail_turn(10)
                        tail_turn(11)
                if pair == 0:
                    eng.wait_ge(s_strow, 32)
                    for m in range(10):
                        eng.transpose(bank[5][:, 24 * m:24 * m + 24], convrow[:, m * P:(m + 1) * P],
                                      ident[0:24, 0:24])
                    for i in range(2):
                        t_ = eng.transpose(bank[5][:, 240 + 120 * i:360 + 120 * i],
                                           poolrow[:, i * P:(i + 1) * P], ident[0:120, 0:120])
                    t_.then_inc(s_stT, 1)
                    eng.wait_ge(s_stc, 1)
                if pair == 6:
                    eng.wait_ge(s_wpool, 64)
                    mean = (ue[0], win_a)
                    for i in range(2):
                        eng.wait_ge(pmix, i + 1)
                        for n in range(NT):
                            g = 3 * i + n
                            wait(eng, po_hi, g)
                            if n < 2:
                                a = PBUF + n * TN
                                mm = eng.matmul(bank[6][:, 0:TN], wpool[:, i, :], mean[i][:, a:a + TN], start=True, stop=True)
                            else:
                                a = PBUF + 2 * TN
                                eng.matmul(bank[6][:, 0:LASTP], wpool[:, i, :], mean[i][:, a:a + LASTP], start=True,
                                           stop=True)
                                mm = eng.matmul(bank[6][:, LASTP:TN], wpool[:, i, :],
                                                mean[i][:, PBUF + SEQ:].rearrange("p (b t) -> p b t", t=PBUF + SL)[:, :, PBUF:],
                                                start=True, stop=True)
                            mm.then_inc(pmm, 1)

            eng.wait_ge(s_decd, 1)
            eng.wait_ge(s_mask, 1)
            np_ = 8 * HEADS
            dfl = dta[:, 0:8, :].rearrange("p c h -> p (c h)")
            for j, m_ in enumerate((upper, below, ones)):
                eng.matmul(bank[7][:, j * np_:(j + 1) * np_], m_[:, :], dfl, start=True, stop=True)
            eng.matmul(bank[7][0:NS, 3 * np_:3 * np_ + HEADS], be_s[:, :], dta[0:NS, 8, :], start=True, stop=True)
            for j in range(YT):
                mm = eng.matmul(bank[6][:, j * (NS + NB):(j + 1) * (NS + NB)],
                                dtab[:, 2 * j:2 * j + 2, :].rearrange("p a b -> p (a b)"), up_s[:, :], start=True, stop=True)
            mm.then_inc(s_dec, 1)
            eng.wait_ge(xbc_ready, 10)
            eng.wait_ge(s_dece, 1)

            for ch in range(9):
                M = P if ch < 8 else NS
                tok = slice(ch * P, ch * P + M)
                wait(eng, y_ev, ch)
                wait(eng, yc_done, ch)
                if ch == 8:
                    eng.wait_ge(s_hoc, 1)
                for j in range(8):
                    src = xs[:, j, tok] if j < 6 else bcT[:, j - 6, tok]
                    mm = eng.transpose(bank[j // 4][0:M, P * (j % 4):P * (j % 4) + P], src, ident[:, :])
                    if j % 4 == 3:
                        mm.then_inc(t1, 1)
                eng.wait_ge(ud_ready, ch + 1)
                wait(eng, h_upd, min(ch, 8))
                if ch < 8:
                    for j in range(3):
                        eng.matmul(bank[2 + j][:, :], below[:, :], ud[:, 512 * j:512 * j + 512], start=True, stop=True)\
                           .then_inc(seg_ready, 1)
                else:
                    eng.matmul(bank[2][0:NS, 0:HEADS * NS], be_s[:, :], ud[0:NS, 0:HEADS * NS], start=True, stop=True)\
                       .then_inc(seg_ready, 1)
                eng.wait_ge(t1_ev, 2 * ch + 2)
                for g in range(2):
                    mm = eng.matmul(bank[0][0:M, M * g:M * g + M], bcT[:, g, tok], bcT[:, 2 + g, tok], start=True, stop=True)
                mm.then_inc(sc_ready, 1)
                if 0 < ch < 8:
                    for g in range(2):
                        mm = eng.matmul(bank[(7, 1)[g]][:, 0:384], bcT[:, 2 + g, tok], hT[:, 384 * g:384 * g + 384],
                                        start=True, stop=True)
                    mm.then_inc(yo_ready, 1)
                eng.wait_ge(xd_ready, 2 * ch + 2)
                eng.wait_ge(e_done, 3 * (ch + 1) if ch < 8 else 25)
                if ch < 8:
                    for g in range(2):
                        mm = eng.matmul(bank[2 + g][:, 0:384], xb[:, D_SSM + P * g:D_SSM + P * g + P],
                                        xde[:, HG * g:HG * g + HG, :].rearrange("p a b -> p (a b)"), start=True, stop=True)
                    mm.then_inc(st_ready, 1)
                eng.wait_ge(wg_ready, 2 * ch + 2)
                for h in range(HEADS):
                    mm = eng.matmul(bank[5 + h // HG][0:M, HD * (h % HG):HD * (h % HG) + HD], ew[0:M, M * h:M * h + M],
                                    xdt[0:M, h, :], start=True, stop=True)
                mm.then_inc(yd_ready, 1)
                if ch == 7:
                    eng.wait_ge(h_upd, 8)
                    eng.wait_ge(yc_done, 8)
                    for j in range(YT):
                        o = bank[7][:, P * j:P * j + P] if j < 4 else bank[1][:, P * (j - 4):P * (j - 4) + P]
                        mm = eng.transpose(o, hT[:, P * j:P * j + P], ident[:, :])
                    mm.then_inc(s_ho, 1)
                eng.wait_ge(yc_done, ch + 1)
                eng.wait_ge(sm_done, ch + 1)
                for j in range(YT):
                    if ch < 8:
                        o = bank[4][:, P * j:P * j + P] if j < 4 else bank[0][:, P * (j - 4):P * (j - 4) + P]
                    else:
                        o = bank[4][:, NS * j:NS * j + NS]
                    mm = eng.transpose(o, ytok[0:M, P * j:P * j + P], ident[0:M, 0:M])
                mm.then_inc(yt_ready, 1)
            eng.wait_ge(s_h0, 16)
            for b in range(NB):
                wait(eng, s_h0a, b)
                wait(eng, s_h0d, b)
                for j in range(YT):
                    o = bank[0][:, P * j:P * j + P] if j < 4 else bank[1][:, P * (j - 4):P * (j - 4) + P]
                    mm = eng.transpose(o, h0[:, b, j, :], ident[:, :])
                    if j in (3, 5):
                        mm.then_inc(s_h0t, 1)
                eng.wait_ge(s_h0a, b + 1)
                eng.wait_ge(s_h0d, b + 1)
                for j in range(YT):
                    c_ = NS * j + SL * b
                    mm = eng.matmul(bank[7][:, c_:c_ + SL], h0T[:, b % 2, P * j:P * j + P],
                                    bcT[:, 2 + j // 3, SEQ + SL * b:SEQ + SL * b + SL], start=True, stop=True)
                mm.then_inc(yo_ready, 1)
            eng.wait_ge(s_h0d, NB + 2)
            for j in range(YT):
                for half in range(2):
                    bk = bank[(2, 3, 5, 6)[2 * (j % 2) + half]]
                    wait(eng, s_h0n, 2 * j + half - 3)
                    eng.matmul(bk[:, :], xde[0:NS, 2 * j:2 * j + 2, :].rearrange("p a b -> p (a b)"),
                               bx[:, j // 3, 4 * half:4 * half + 4, :].rearrange("p a b -> p (a b)"), start=True, stop=True)\
                       .then_inc(s_h0st, 1)
            eng.wait_ge(s_h0n, 2 * YT)
            for n in range(NT):
                norm_stat(2, n, K=YT)
                norm_bc(2, n)
            eng.wait_ge(po_lo, 1)

            def project_all(u0, v=None):
                for pair in range(4):
                    w = u0 + 2 * pair
                    eng.wait_ge(w_ready, w + 2)
                    for n in range(NT):
                        if v is not None and pair == 0:
                            norm_ready(v, n)
                        for mm in range(2):
                            project(w + mm, n)

            project_all(U_OUT, 2)
            for n in range(NT):
                norm_stat(3, n)
                norm_bc(3, n)
            project_all(U_XQ, 3)

            eng.wait_ge(q_ready, 24)
            eng.wait_ge(s_kv2, 32)

            def scores(t, hb):
                wait(eng, a_e, MH * (t - 1) + 2 * hb + 2)
                for h in (2 * hb, 2 * hb + 1):
                    o = bank[h // 2][:, 256 * (h % 2):256 * (h % 2) + 256]
                    for kd in range(2):
                        mm = eng.matmul(o, q[:, 2 * h + kd, t * P:(t + 1) * P], kT[:, 2 * h + kd, :], start=(kd == 0),
                                        stop=(kd == 1))
                    mm.then_inc(a_s, 1)

            def values(i):
                t, h = divmod(i, MH)
                eng.wait_ge(a_c, i + 1)
                wait(eng, a_ol, i - 1)
                for dt2 in range(2):
                    o = bank[(2, 5)[i % 2]][:, P * dt2:P * dt2 + P]
                    for m in range(2):
                        c_ = (2 * h + dt2) * P
                        mm = eng.matmul(o, v[:, m, c_:c_ + P], pT[i % 2][:, m, :], start=(m == 0), stop=(m == 1))
                mm.then_inc(a_o, 1)

            def turn_p(i):
                eng.wait_ge(a_n, i + 1)
                wait(eng, a_c, i)
                for m in range(2):
                    mm = eng.transpose(bank[4][:, P * m:P * m + P],
                                       pr[i % 2][:, m * P:(m + 1) * P], ident[:, :])
                mm.then_inc(a_t, 1)

            def sample_keys(b):
                eng.wait_ge(s_kr[b % 2], 16 * (b // 2 + 1))
                for g in range(4):
                    wait(eng, b_ta, 4 * b + g - 1)
                    for c_ in range(4):
                        f_, m = 2 * g + c_ // 2, c_ % 2
                        mm = eng.transpose(bank[(3, 6)[g % 2]][:, P * c_:P * c_ + P],
                                           kring[b % 2][:, m, f_ * P:(f_ + 1) * P], ident[:, :])
                    mm.then_inc(b_t, 1)
                eng.wait_ge(b_ta, 4 * b + 4)
                for h in range(MH):
                    for m in range(2):
                        c_ = P * m + NS * h + SL * b
                        for kd in range(2):
                            mm = eng.matmul(bank[7][:, c_:c_ + SL], kTs[:, 2 * h + kd, m * P:(m + 1) * P],
                                            q[:, 2 * h + kd, SEQ + SL * b:SEQ + SL * b + SL], start=(kd == 0),
                                            stop=(kd == 1))
                mm.then_inc(b_s, 1)

            def sample_values(b):
                eng.wait_ge(s_vr[b % 4], 16 * (b // 4 + 1))
                for j in range(KT):
                    c_ = NS * j + SL * b
                    r = NS * (j // 2) + SL * b
                    for m in range(2):
                        mm = eng.matmul(bank[7][:, c_:c_ + SL], vring[b % 4][:, m, j * P:(j + 1) * P],
                                        pT_s[:, m, r:r + SL], start=(m == 0), stop=(m == 1))
                mm.then_inc(b_v, 1)

            scores(0, 0)
            scores(0, 1)
            for t in range(8):
                for h in range(MH):
                    turn_p(MH * t + h)
                    values(MH * t + h)
                    if h % 2 and t < 7:
                        scores(t + 1, h // 2)
                if t < 4:
                    sample_keys(2 * t)
                    sample_keys(2 * t + 1)
                if t == 4:
                    eng.wait_ge(b_d, 1)
                    for m in range(2):
                        mm = eng.transpose(bank[7][:, 256 + P * m:256 + P * m + P], s_s[:, m, :], ident[:, :])
                    mm.then_inc(b_r, 1)
                    eng.wait_ge(b_d, 3)
                    for m in range(2):
                        mm = eng.transpose(bank[7][:, 256 + P * m:256 + P * m + P], p_s[:, m * P:(m + 1) * P],
                                           ident[:, :])
                    mm.then_inc(b_r, 1)
                    eng.wait_ge(b_d, 4)
            for b in range(NB):
                sample_values(b)
            eng.wait_ge(a_ol, 33)
            project_all(U_XO)
            norm_stat(4, 0)
            norm_bc(4, 0)
            ffn(U_F2, 1, 0, first=4)
            with eng.Fori(1, CHUNKS) as i:
                ffn(U_F2, 1, i)
            for n in range(NT):
                norm_stat(5, n)
                norm_bc(5, n)
            for t in range(9):
                M = P if t < 8 else NS
                eng.wait_ge(n_hf, 2 * (15 + min(2, (t * P + M - 1) // TN) + 1))
                for h in range(2):
                    wait(eng, y_c, 2 * t)
                    for k in range(4):
                        mm = eng.transpose(bank[h][0:M, k * P:(k + 1) * P], x[:, 4 * h + k, t * P:t * P + M], ident[:, :])
                    mm.then_inc(y_t, 1)


_INS = ['x_prompt', 'x_sample', 'mem_prompt', 'cache_mem_k', 'cache_mem_v', 'state_pool', 'state_conv', 'state_ssm',
        'g_ffn1', 'w1_gate', 'w1_up', 'w1_down', 'g_mix', 'w_in', 'conv_w', 'conv_b', 'dt_bias', 'a_log', 'd_skip',
        'ssm_norm', 'w_pool', 'pool_scale', 'w_out', 'g_mem', 'w_mem_k', 'w_mem_v', 'g_xq', 'w_xq', 'w_xo',
        'g_ffn2', 'w2_gate', 'w2_up', 'w2_down', 'g_final']
_OUTS = [('y_prompt', (1, SEQ, D)), ('y_sample', (NB, SL, D)), ('mem_k_prompt', (1, 1, NMEM, MH, MHD)),
         ('mem_v_prompt', (1, 1, NMEM, MH, MHD)), ('pool_prompt', (1, 1, PBUF, D_POOL)),
         ('conv_prompt', (1, 1, 3, CONV_DIM)), ('ssm_prompt', (1, 1, HEADS, HD, ST)),
         ('pool_sample', (1, NB, PBUF, D_POOL)), ('conv_sample', (1, NB, 3, CONV_DIM)),
         ('ssm_sample', (1, NB, HEADS, HD, ST))]


def kernel(**inputs):
    import numpy as _np
    import concourse.bacc as _bacc
    from concourse import mybir as _mybir
    from concourse.bass_utils import run_bass_kernel_spmd as _run

    nc = _bacc.Bacc("TRN2", target_bir_lowering=False, num_devices=1)
    arrays, ins, outs = {}, {}, {}
    for name in _INS:
        a = _np.ascontiguousarray(inputs[name])
        arrays[f"in_{name}_dram"] = a
        ins[name] = nc.dram_tensor(f"in_{name}_dram", a.shape, _mybir.dt.from_np(a.dtype), kind="ExternalInput").ap()
    for name, shape in _OUTS:
        outs[name] = nc.dram_tensor(f"out_{name}_dram", shape, _mybir.dt.float32, kind="ExternalOutput").ap()
    build(nc, ins, outs)
    r = _run(nc, [arrays], core_ids=[0])
    return tuple(r.results[0][f"out_{name}_dram"] for name, _ in _OUTS)
```

```python
from contextlib import ExitStack

import concourse.bass as bass
from concourse import mybir

F32 = mybir.dt.float32
F32R = mybir.dt.float32r
I32 = mybir.dt.int32
ALU = mybir.AluOpType
ACT = mybir.ActivationFunctionType
AX = mybir.AxisListType

P = 128
D = 1024
KT = D // P
SEQ = 1024
NB = 8
SL = 4
NS = NB * SL
T = SEQ + NS
TN = T // 3
NT = 3
LASTP = SEQ - 2 * TN
DFF = 2816
FT = DFF // P
CHUNKS = FT // 2
EPS = 1e-6
D_POOL, D_SSM, CONV_DIM, HEADS, HD, ST = 256, 768, 1280, 12, 64, 128
HG = HEADS // 2
STEPS = 1 + SEQ // P
Y_STAT0, Y_BC0, Y_STAT1 = 5, 6, 8
YT = D_SSM // P
WINDOWS = (2, 4, 8, 16)
PBUF = 15
NMEM, MH, MHD = 256, 4, 256
ATT_SCALE = MHD ** -0.5
NHT = SEQ // P * MH
S_MAX, S_SOFT, S_SCALE, S_BACK, S_VALUES, S_OUT, S_TURN = 16, 17, 18, 20, 22, 30, 31


G1, GMIX, GMEM, GXQ, GF2, GFIN, CW, CB, GSSM, PSC = 0, 8, 16, 24, 32, 40, 48, 88, 98, 104
NPAR = 106

U_K, U_V, U_F1, U_IN, U_OUT, U_XQ, U_XO, U_F2 = 0, 8, 16, 82, 100, 108, 116, 124
U_END = U_F2 + 3 * FT
IN_BLOCKS = list(range(8, 18)) + [0, 1] + list(range(2, 8))
DT_TILES = ((0, 3 * P), (3 * P, 3 * P), (6 * P, T - 6 * P))
NORM_SUBS = ((0, 128), (128, 128), (256, 96))


def wait(eng, sem, value):
    if not (isinstance(value, int) and value <= 0):
        eng.wait_ge(sem, value)


def cols(n):
    return slice(n * TN, (n + 1) * TN)


def bc(ap, shape):
    return ap.to_broadcast(shape)


def build(nc, A, O):
    ctx = ExitStack()
    with ctx:
        base = (nc.sbuf_base + 63) // 64 * 64
        at = {}
        used = [base]

        def region(name, size):
            at[name] = used[0]
            used[0] += size
            assert used[0] <= nc.sbuf_usable_end, (name, used[0], nc.sbuf_usable_end)

        KTB = KT * T * 4
        for name, size in (("X", KTB), ("HH", KTB), ("HL", KTB), ("WH", 6 * 4096), ("WL", 6 * 4096),
                           ("WR", 3 * 4096), ("MID", 45056), ("C", 4950)):
            region(name, size)

        def sb(name, reg, off, shape, dt=F32):
            return nc.alloc_sbuf_tensor_at(name, list(shape), dt, offset=at[reg] + off)

        x = sb("x", "X", 0, [P, KT, T])
        h_hi = sb("h_hi", "HH", 0, [P, KT, T], F32R)
        h_lo = sb("h_lo", "HL", 0, [P, KT, T], F32R)
        w_hi = sb("w_hi", "WH", 0, [P, 6, 1024], F32R)
        w_lo = sb("w_lo", "WL", 0, [P, 6, 1024], F32R)
        w_raw = sb("w_raw", "WR", 0, [P, 3, 1024])
        sq = sb("sq", "MID", 0, [P, KT, TN])
        hf = sb("hf", "MID", 11264, [P, KT, TN])
        mid_hi = sb("mid_hi", "MID", 22528, [P, 2, T], F32R)
        mid_lo = sb("mid_lo", "MID", 30976, [P, 2, T], F32R)
        gate = sb("gate", "MID", 39424, [P, 2, TN])
        prod = sb("prod", "MID", 42240, [P, 2, TN])
        co = [0]

        def const(name, shape, dt=F32):
            n = 4
            for s in shape[1:]:
                n *= s
            t = sb(name, "C", co[0], shape, dt)
            co[0] += (n + 31) // 32 * 32
            assert co[0] <= 4950, name
            return t

        ident = const("ident", [P, P])
        upper_at = co[0]
        upper = const("upper", [P, P])
        below = const("below", [P, P])
        ones = const("ones", [P, P])
        par = const("par", [P, NPAR])
        diag_at = co[0]
        diag = const("diag", [P, 3 * P])
        nrm = const("nrm", [P, 4, 4])
        wdt_hi = const("wdt_hi", [P, KT, HEADS], F32R)
        wdt_lo = const("wdt_lo", [P, KT, HEADS], F32R)
        dskip = const("dskip", [P, YT])
        xtok = sb("xtok", "HH", 0, [P, 9, D])
        mem_hi = sb("mem_hi", "HL", 3072 + 1024, [P, KT, NMEM], F32R)
        mem_lo = sb("mem_lo", "HL", 12288, [P, KT, NMEM], F32R)
        mem = sb("mem", "HL", 20480, [P, 2, D])
        kT0 = sb("kT0", "HL", 20480, [P, KT, NMEM])
        memf = sb("memf", "MID", 11264, [P, KT, NMEM])
        ktok = sb("ktok", "MID", 22528, [P, 2, D])
        vtok = sb("vtok", "MID", 30976, [P, 2, D])
        parrow = sb("parrow", "MID", 39424, [NPAR, P])
        NPRE = 3 + SEQ + NB * 7
        pre = [sb(f"pre{i}", "X", 4352 * i, [P, NPRE]) for i in range(2)]
        convT = sb("convT", "X", 8704, [P, 10, NB, 3])
        poolT = sb("poolT", "X", 9728, [P, 2, NB, PBUF])
        wpool = sb("wpool", "X", 10752, [P, 2, P])
        ramp = sb("ramp", "X", 11776, [P, 2, PBUF])
        ramp_i = sb("ramp_i", "X", 11904, [P, PBUF], I32)
        fresh = sb("fresh", "X", 12032, [P, 2, NS])
        NUE = PBUF + SEQ + NB * (PBUF + SL)
        dtT = [sb("dtT0", "C", diag_at, [HEADS, 3 * P]), sb("dtT1", "X", 12288, [HEADS, 3 * P])]
        win_a = sb("win_a", "X", 19488, [P, NUE])
        win_b = sb("win_b", "X", 14720, [P, NUE])
        ue = [sb("ue0", "X", 29024, [P, NUE]), sb("ue1", "X", 24256, [P, NUE])]
        convrow = sb("convrow", "X", 24320, [NB * 3, CONV_DIM])
        poolrow = sb("poolrow", "X", 29440, [NB * PBUF, D_POOL])
        z = sb("z", "X", 0, [P, YT, T])
        pool_out = sb("pool_out", "X", YT * T * 4, [P, 2, T])
        bcT = sb("bcT", "MID", 0, [P, 4, T])
        xs = sb("xs", "MID", 4 * T * 4, [P, YT, T])
        tails = sb("tails", "MID", 42240, [P, 2, 256])
        wdt = sb("wdt", "MID", 42240 + 2048, [P, KT, HEADS])
        dtb = sb("dtb", "MID", 42240 + 2048 + 384, [P, 1, HEADS])
        alog = sb("alog", "MID", 42240 + 2048 + 384 + 64, [P, 1, HEADS])
        dsk_all = sb("dsk_all", "MID", 42240 + 2048 + 384 + 128, [P, HEADS])
        ho = [0]

        def hh(name, shape):
            n = 4
            for s in shape[1:]:
                n *= s
            t = sb(name, "HH", ho[0], shape)
            ho[0] += n
            assert ho[0] <= KTB
            return t

        xb = hh("xb", [P, 1024])
        xdt = hh("xdt", [P, HEADS, HD])
        xde = hh("xde", [P, HEADS, HD])
        ud = hh("ud", [P, HEADS * P])
        ew = hh("ew", [P, HEADS * P])
        sm = hh("sm", [P, 2 * P])
        ytok = hh("ytok", [P, HEADS * HD])
        ytmp = hh("ytmp", [P, HEADS * HD])
        hT = hh("hT", [P, HEADS * HD])
        h0T = sb("h0T", "HH", 10240, [P, 2, D_SSM])
        bx = sb("bx", "HH", 16384, [NS, 2, NB, P])
        hc = sb("hc", "HL", 0, [P, HEADS * HD])
        so = [3072]

        def hl(name, shape, dt=F32):
            n = 4
            for s in shape[1:]:
                n *= s
            t = sb(name, "HL", so[0], shape, dt)
            so[0] += (n + 31) // 32 * 32
            assert so[0] <= 8448, name
            return t

        NTT = SEQ // P + 1
        dt_ = hl("dt_", [P, NTT, HEADS])
        dta = hl("dta", [P, NTT, HEADS])
        ea = hl("ea", [P, NTT, HEADS])
        dedt = hl("dedt", [P, NTT, HEADS])
        cd = hl("cd", [P, NTT, HEADS])
        ea_s = hl("ea_s", [P, YT, NS + NB])
        up_s = hl("up_s", [NS, NS + NB])
        be_s = hl("be_s", [NS, NS])
        expa = hl("expa", [P, 1, HEADS])
        ser = [sb(f"ser{i}", "HH", 10240 + 448 * i, [P, NTT, HEADS]) for i in range(7)]
        dtab = sb("dtab", "HH", 10240 + 3584, [NS, HEADS, HD])
        h0 = sb("h0", "HL", 8448, [P, NB, YT, ST])
        hout = sb("hout", "MID", 12288, [P, YT, ST])
        q = sb("q", "MID", 11264, [P, KT, T])
        kTs = sb("kTs", "MID", 0, [P, KT, NMEM])
        pr = [sb("pr0", "MID", 8192, [P, NMEM]), sb("pr1", "MID", 9216, [P, NMEM])]
        pT = [sb("pT0", "MID", 10240, [P, 2, P]), sb("pT1", "X", 32768, [P, 2, P])]
        kT = sb("kT", "X", 0, [P, KT, NMEM])
        v = sb("v", "X", 8192, [P, 2, D])
        kring = [sb(f"kring{i}", "X", 16384 + 8192 * i, [P, 2, D]) for i in range(2)]
        vring = [sb("vring0", "WH", 0, [P, 2, D]), sb("vring1", "WL", 0, [P, 2, D]),
                 sb("vring2", "X", 16384, [P, 2, D]), sb("vring3", "X", 24576, [P, 2, D])]
        amax = sb("amax", "C", co[0], [P, 16])
        co[0] += 64
        qm = [sb("qm0", "C", diag_at, [P, KT, NS]), sb("qm1", "C", upper_at, [P, KT, NS])]
        pm = [sb("pm0", "C", diag_at, [P, 2, P]), sb("pm1", "C", upper_at, [P, 2, P])]
        p_s = sb("p_s", "MID", 1024, [P, NMEM])
        pT_s = sb("pT_s", "MID", 2048, [P, 2, P])
        o_s = sb("o_s", "MID", 3072, [NS, D])
        yrow = sb("yrow", "MID", 22528, [P, 2, D])

        bank = [ctx.enter_context(nc.psum_tensor(f"bank{i}", [P, 512], F32)) for i in range(8)]

        x_spill = nc.dram_tensor("x_spill", [P, KT, T], F32).ap()
        kT_spill = nc.dram_tensor("kT_spill", [P, KT, NMEM], F32).ap()

        def sem(name):
            return ctx.enter_context(nc.semaphore(name))

        w_dma = [sem(f"w_dma{i}") for i in range(3)]
        w_hid, w_ready, kv_used = sem("w_hid"), sem("w_ready"), sem("kv_used")
        s_const, s_par, s_part = sem("s_const"), sem("s_par"), sem("s_part")
        s_x = [sem(f"s_x{i}") for i in range(5)]
        s_mem, mem_a, mem_d = sem("s_mem"), sem("mem_a"), sem("mem_d")
        tr_ready, tr_act, tr_dve = sem("tr_ready"), sem("tr_act"), sem("tr_dve")
        kv_act, kv_dve, kt_ready, kt_copied = (sem("kv_act"), sem("kv_dve"),
                                                         sem("kt_ready"), sem("kt_copied"))
        s_kvout, s_ktout = sem("s_kvout"), sem("s_ktout")
        n_sq, n_st, n_rs, n_bc, n_hf, n_hi, n_lop, n_lod = (sem("n_sq"), sem("n_st"), sem("n_rs"), sem("n_bc"),
                                                            sem("n_hf"), sem("n_hi"), sem("n_lop"), sem("n_lod"))
        f_g, f_u, f_s, f_p, f_mh, f_ml, f_d, f_x = (sem("f_g"), sem("f_u"), sem("f_s"), sem("f_p"),
                                                    sem("f_mh"), sem("f_ml"), sem("f_d"), sem("f_x"))
        dve_c = sem("dve_c")
        act_c = sem("act_c")
        pool_c = sem("pool_c")
        p_ready, p_free = sem("p_ready"), sem("p_free")
        s_spill = sem("s_spill")
        s_back = [sem(f"s_back{n}") for n in range(NT)]
        s_strow, s_stT, s_stc, s_wdt, s_wdtr = sem("s_strow"), sem("s_stT"), sem("s_stc"), sem("s_wdt"), sem("s_wdtr")
        pre_ready, conv_done, xbc_ready = sem("pre_ready"), sem("conv_done"), sem("xbc_ready")
        tail_t, tail_c = sem("tail_t"), sem("tail_c")
        tail_d = [sem("tail_d0"), sem("tail_d1")]
        dt_raw, dt_copied = sem("dt_raw"), sem("dt_copied")
        dt_ready, ue_ready, pmix, pmm = sem("dt_ready"), sem("ue_ready"), sem("pmix"), sem("pmm")
        s_wpool, s_wpz = sem("s_wpool"), sem("s_wpz")
        z_ready = sem("z_ready")
        s_mask, s_dexp, s_dec, s_dece, s_decd = (sem("s_mask"), sem("s_dexp"), sem("s_dec"), sem("s_dece"),
                                                 sem("s_decd"))
        t1, t1_ev, ud_ready, seg_ready, e_done, sc_ready, sm_done = (
            sem("t1"), sem("t1_ev"), sem("ud_ready"), sem("seg_ready"), sem("e_done"), sem("sc_ready"),
            sem("sm_done"))
        wg_ready, xd_ready, yd_ready, yo_ready, st_ready, yc_done, hc_ready, h_upd, yt_ready, y_ev, g_done = (
            sem("wg_ready"), sem("xd_ready"), sem("yd_ready"), sem("yo_ready"), sem("st_ready"), sem("yc_done"),
            sem("hc_ready"), sem("h_upd"), sem("yt_ready"), sem("y_ev"), sem("g_done"))
        s_hout = sem("s_hout")
        s_h0, s_ho, s_hoc, s_h0t, s_h0a, s_h0d, s_h0s, s_h0st, s_h0n, s_h0o = (
            sem("s_h0"), sem("s_ho"), sem("s_hoc"), sem("s_h0t"), sem("s_h0a"), sem("s_h0d"),
            sem("s_h0s"), sem("s_h0st"), sem("s_h0n"), sem("s_h0o"))
        po_hi, po_lo = sem("po_hi"), sem("po_lo")
        s_kv2 = sem("s_kv2")
        s_kr = [sem(f"s_kr{i}") for i in range(2)]
        s_vr = [sem(f"s_vr{i}") for i in range(4)]
        q_ready = sem("q_ready")
        a_s, a_m, a_e, a_n, a_t, a_c, a_o, a_oh, a_ol = (sem("a_s"), sem("a_m"), sem("a_e"), sem("a_n"), sem("a_t"),
                                                         sem("a_c"), sem("a_o"), sem("a_oh"), sem("a_ol"))
        b_t, b_ta, b_s, b_r, b_d, b_e, b_v = (sem("b_t"), sem("b_ta"), sem("b_s"), sem("b_r"), sem("b_d"),
                                              sem("b_e"), sem("b_v"))
        b_q, b_p, b_o = sem("b_q"), sem("b_p"), sem("b_o")
        y_t = sem("y_t")
        y_c = [sem("y_c0"), sem("y_c1")]
        s_y = [sem("s_y0"), sem("s_y1")]
        s_dd = sem("s_dd")

        def kview(name):
            return A[name].rearrange("l (k p) m -> p (l k) m", p=P)

        wv = {n: kview(n) for n in ("w1_gate", "w1_up", "w1_down", "w2_gate", "w2_up", "w2_down", "w_in", "w_out",
                                    "w_mem_k", "w_mem_v", "w_xq", "w_xo")}
        kc = A["cache_mem_k"].rearrange("l b (t p) h d -> p (l b) t (h d)", p=P)
        vc = A["cache_mem_v"].rearrange("l b (t p) h d -> p (l b) t (h d)", p=P)
        h0_in = A["state_ssm"].rearrange("l b (j e) d n -> (e d) (l b j) n", e=2)
        h0_out = O["ssm_sample"].rearrange("l b (j e) d n -> (e d) (l b j) n", e=2)

        def chunk(q):
            ch, M = (8, NS) if q == 0 else (q - 1, P)
            return ch, M, slice(ch * P, ch * P + M)

        def norm_banks(v, n):
            return (bank[1], bank[1]) if v == 2 and n < 2 else (bank[6], bank[7])

        block = ctx.enter_context(nc.Block())


        def wait_used(eng, w, i):
            if isinstance(i, int):
                w, i = w + 6 * i, 0
                if w < 0:
                    return
                if w < U_F1:
                    eng.wait_ge(kv_used, w + 1)
                    return
                if U_IN <= w < U_OUT:
                    eng.wait_ge(p_ready, 6 * ((w - U_IN) // 2 + 1))
                    return
                if U_OUT <= w < U_F2:
                    group, second = divmod((w - U_OUT) // 2, 2)
                    eng.wait_ge(p_ready, 54 + 12 * group + (12 if second else 10))
                    return
                f = 0 if w < U_IN else 1
            else:
                f = 0 if w < U_IN - 6 else 1
            u0 = (U_F1, U_F2)[f]
            stage, it = (w - u0) // 2 % 3, (w - u0) // 6
            if stage < 2:
                eng.wait_ge(f_u, 66 * f + 6 * it + 3 * (stage + 1) + 6 * i)
            else:
                eng.wait_ge(f_d, 264 * f + 24 * (it + 1) + 24 * i)

        @block.sync
        def _(eng):
            def unit(w, ring, src):
                wait(eng, w_ready, w - 2)
                dst = w_raw[:, ring, :].rearrange("p (a b) -> p a b", a=src.shape[1])
                eng.dma_start(dst, src).then_inc(w_dma[ring], 16)

            for row, name in ((G1, "g_ffn1"), (GMIX, "g_mix"), (GMEM, "g_mem"), (GXQ, "g_xq"), (GF2, "g_ffn2"),
                              (GSSM, "ssm_norm"), (PSC, "pool_scale"), (CB, "conv_b")):
                n = A[name].shape[1] // P
                eng.dma_start(parrow[row:row + n, :], A[name].rearrange("l (r c) -> (l r) c", c=P)).then_inc(s_par, 16)
            eng.dma_start(parrow[GFIN:GFIN + KT, :], A["g_final"].rearrange("(r c) -> r c", c=P)).then_inc(s_par, 16)
            eng.dma_start(parrow[CW:CW + 40, :], A["conv_w"].rearrange("l k (r c) -> (l k r) c", c=P)).then_inc(s_par, 16)
            eng.dma_start(mem[:, :, :], A["mem_prompt"].rearrange("a (t p) d -> p (a t) d", p=P)).then_inc(s_mem, 16)
            xp = A["x_prompt"].rearrange("a (t p) d -> p (a t) d", p=P)

            def xload(t):
                if t < 8:
                    eng.dma_start(xtok[:, t, :], xp[:, t, :]).then_inc(s_x[t // 2], 16)
                else:
                    eng.dma_start(xtok[0:NS, t, :], A["x_sample"].rearrange("b s d -> (b s) d")).then_inc(s_x[t // 2], 16)

            for k in range(8):
                unit(U_K + k, (U_K + k) % 3, wv["w_mem_k"][:, k:k + 1, :])
                xload(k)
            xload(8)
            for k in range(8):
                unit(U_V + k, (U_V + k) % 3, wv["w_mem_v"][:, k:k + 1, :])
                if k == 3:
                    eng.wait_ge(kv_act, 2)
                    eng.wait_ge(kv_dve, 2)
                    eng.dma_start(O["mem_k_prompt"].rearrange("l a (t p) h d -> p (l a t) (h d)", p=P), ktok[:, :, :])\
                       .then_inc(s_kvout, 16)
                if k == 7:
                    eng.wait_ge(kt_copied, 4)
                    eng.dma_start(kT_spill, kT0[:, :, :]).then_inc(s_ktout, 16)

            def ffn_units(u0, name, i):
                for j in range(6):
                    w = u0 + j + 6 * i
                    kind = ("gate", "up", "gate", "up", "down", "down")[j]
                    view = wv[f"{name}_{kind}"]
                    if j < 4:
                        first = (2 * i + j // 2) * P
                        src = view[:, :, bass.ds(first, P)]
                    else:
                        src = view[:, bass.ds(2 * i + j - 4, 1), :]
                    unit(w, (u0 + j) % 3, src)

            ffn_units(U_F1, "w1", 0)
            eng.wait_ge(kv_act, 4)
            eng.wait_ge(kv_dve, 4)
            eng.dma_start(O["mem_v_prompt"].rearrange("l a (t p) h d -> p (l a t) (h d)", p=P), vtok[:, :, :])\
               .then_inc(s_kvout, 16)
            eng.dma_start(O["pool_sample"][0, :, 0:PBUF - SL, :], A["state_pool"][0, :, SL:PBUF, :]).then_inc(s_dd, 16)
            with eng.Fori(1, CHUNKS) as i:
                ffn_units(U_F1, "w1", i)

            for k in range(4):
                unit(U_IN + k, (U_IN + k) % 3, wv["w_in"][:, :, IN_BLOCKS[k] * P:(IN_BLOCKS[k] + 1) * P])
            for n in range(NT):
                eng.wait_ge(f_x, 24 * CHUNKS - 16 + 8 * n)
                eng.dma_start(x_spill[:, :, cols(n)], x[:, :, cols(n)]).then_inc(s_spill, 16)
            eng.dma_start(wdt[:, :, :], wv["w_in"][:, :, 2304:2316]).then_inc(s_wdt, 16)
            eng.dma_start(dsk_all[:, :], A["d_skip"][0].partition_broadcast(P)).then_inc(s_wdt, 16)
            eng.dma_start(dtb[:, 0, :], A["dt_bias"][0].partition_broadcast(P)).then_inc(s_wdt, 16)
            eng.dma_start(alog[:, 0, :], A["a_log"][0].partition_broadcast(P)).then_inc(s_wdt, 16)
            for k in range(4, 7):
                unit(U_IN + k, (U_IN + k) % 3, wv["w_in"][:, :, IN_BLOCKS[k] * P:(IN_BLOCKS[k] + 1) * P])
            eng.wait_ge(s_spill, 48)
            eng.wait_ge(n_hf, 12)
            eng.dma_start(convrow[:, :], A["state_conv"].rearrange("l b t c -> (l b t) c")).then_inc(s_strow, 16)
            eng.dma_start(poolrow[:, :], A["state_pool"].rearrange("l b t c -> (l b t) c")).then_inc(s_strow, 16)
            eng.wait_ge(s_wpz, 1)
            for g in range(4):
                a = 64 * (g % 2)
                eng.dma_start(wpool[a:a + 64, g // 2, a:a + 64], A["w_pool"][0, g]).then_inc(s_wpool, 16)

            def tail_out(m):
                eng.wait_ge(tail_c, m + 1)
                s = m % 2
                if m < 10:
                    c = slice(m * P, (m + 1) * P)
                    eng.dma_start(O["conv_prompt"][0, 0, :, c], tails[0:3, s, 0:P]).then_inc(tail_d[s], 16)
                    eng.dma_start(O["conv_sample"].rearrange("l b t c -> (l b t) c")[:, c],
                                  tails[0:NB * 3, s, P:2 * P]).then_inc(tail_d[s], 16)
                else:
                    c = slice((m - 10) * P, (m - 9) * P)
                    eng.dma_start(O["pool_prompt"][0, 0, :, c], tails[0:PBUF, s, 0:P]).then_inc(tail_d[s], 16)
                    for b in range(NB):
                        eng.dma_start(O["pool_sample"][0, b, PBUF - SL:PBUF, c],
                                      tails[SL * b:SL * b + SL, s, P:2 * P]).then_inc(tail_d[s], 16)

            for k in range(7, 18):
                unit(U_IN + k, (U_IN + k) % 3, wv["w_in"][:, :, IN_BLOCKS[k] * P:(IN_BLOCKS[k] + 1) * P])
                if k % 2 and k < 17:
                    tail_out(k - 7)
                    tail_out(k - 6)
            for k in range(4):
                unit(U_OUT + k, (U_OUT + k) % 3, wv["w_out"][:, :, k * P:(k + 1) * P])
            tail_out(10)
            tail_out(11)
            eng.wait_ge(z_ready, 6 * NT)
            eng.dma_start(h0[:, :, :, :].rearrange("p b j n -> p (b j) n"), h0_in).then_inc(s_h0, 16)
            for k in range(4, 7):
                unit(U_OUT + k, (U_OUT + k) % 3, wv["w_out"][:, :, k * P:(k + 1) * P])
            for j in range(YT):
                eng.wait_ge(s_h0n, 2 * (j + 1))
                eng.dma_start(h0_out.rearrange("p (b j) n -> p b j n", j=YT)[:, :, j, :], h0[:, :, j, :])\
                   .then_inc(s_h0o, 16)
            eng.wait_ge(s_hoc, 1)
            eng.dma_start(O["ssm_prompt"].rearrange("l a (j e) d n -> (e d) (l a j) n", e=2), hout[:, :, :])\
               .then_inc(s_hout, 16)
            eng.wait_ge(n_st, 9)
            eng.wait_ge(po_lo, 1)
            for n in range(NT):
                eng.dma_start(x[:, :, cols(n)], x_spill[:, :, cols(n)]).then_inc(s_back[n], 16)
            unit(U_OUT + 7, (U_OUT + 7) % 3, wv["w_out"][:, :, 7 * P:8 * P])
            for k in range(4):
                unit(U_XQ + k, (U_XQ + k) % 3, wv["w_xq"][:, :, k * P:(k + 1) * P])
            for n in range(NT):
                eng.wait_ge(f_x, 24 * CHUNKS + 12 + 4 * (n + 1))
                eng.dma_start(x_spill[:, :, cols(n)], x[:, :, cols(n)]).then_inc(s_spill, 16)
            for k in range(4, 8):
                unit(U_XQ + k, (U_XQ + k) % 3, wv["w_xq"][:, :, k * P:(k + 1) * P])
            eng.wait_ge(s_spill, 96)
            eng.wait_ge(n_hf, 24)
            eng.wait_ge(s_ktout, 16)
            eng.wait_ge(s_kvout, 32)
            eng.dma_start(kT[:, :, :], kT_spill).then_inc(s_kv2, 16)
            eng.dma_start(v[:, :, :], O["mem_v_prompt"].rearrange("l a (t p) h d -> p (l a t) (h d)", p=P))\
               .then_inc(s_kv2, 16)
            for b in range(2):
                eng.dma_start(kring[b][:, :, :], kc[:, b]).then_inc(s_kr[b], 16)
            for k in range(4):
                unit(U_XO + k, (U_XO + k) % 3, wv["w_xo"][:, :, k * P:(k + 1) * P])
            eng.wait_ge(p_ready, 102)
            for b in range(2):
                eng.dma_start(vring[b][:, :, :], vc[:, b]).then_inc(s_vr[b], 16)
            for b in range(2, NB):
                eng.wait_ge(b_t, 4 * (b - 1))
                eng.dma_start(kring[b % 2][:, :, :], kc[:, b]).then_inc(s_kr[b % 2], 16)
            for b in range(2, NB):
                if b < 4:
                    eng.wait_ge(b_t, 4 * (NB - 2 + b - 1))
                else:
                    eng.wait_ge(b_v, b - 3)
                eng.dma_start(vring[b % 4][:, :, :], vc[:, b]).then_inc(s_vr[b % 4], 16)
            for k in range(4, 7):
                unit(U_XO + k, (U_XO + k) % 3, wv["w_xo"][:, :, k * P:(k + 1) * P])
            eng.wait_ge(a_o, 4 * NB)
            eng.wait_ge(b_v, NB)
            for n in range(NT):
                eng.dma_start(x[:, :, cols(n)], x_spill[:, :, cols(n)]).then_inc(s_back[n], 16)
            unit(U_XO + 7, (U_XO + 7) % 3, wv["w_xo"][:, :, 7 * P:8 * P])
            with eng.Fori(0, CHUNKS) as i:
                ffn_units(U_F2, "w2", i)
            yp = O["y_prompt"].rearrange("a (t p) d -> p (a t) d", p=P)
            for t in range(9):
                for h in range(2):
                    eng.wait_ge(y_c[h], t + 1)
                if t < 8:
                    eng.dma_start(yp[:, t, :], yrow[:, t % 2, :]).then_inc(s_y[t % 2], 16)
                else:
                    eng.dma_start(O["y_sample"].rearrange("b s d -> (b s) d"), yrow[0:NS, t % 2, :])\
                       .then_inc(s_y[t % 2], 16)
            eng.wait_ge(s_y[0], 16 * 5)
            eng.wait_ge(s_y[1], 16 * 4)
            eng.wait_ge(s_kvout, 32)
            eng.wait_ge(s_dd, 16)
            eng.wait_ge(s_h0o, 16 * YT)
            eng.wait_ge(s_hout, 16)
            for s in range(2):
                eng.wait_ge(tail_d[s], 16 * (2 * 5 + 9))

        @block.gpsimd
        def _(eng):
            def lo(w, slot, ring):
                eng.wait_ge(w_hid, w + 1)
                eng.tensor_tensor(w_lo[:, slot, :], w_raw[:, ring, :], w_hi[:, slot, :].bitcast(F32), ALU.subtract)\
                   .then_inc(w_ready, 1)

            def lo_pair(w):
                for d in range(2):
                    lo(w + d, (w + d) % 6, (w + d) % 3)

            def norm_lo(v, n, src=None, k0=0, half=4, off=0):
                w = 3 * v + n
                eng.wait_ge(n_hi, 2 * w + 1)
                s = hf[:, 0:half, :] if src is None else src[:, 0:half, cols(n)]
                eng.tensor_tensor(h_lo[:, off:off + half, cols(n)], s,
                                  h_hi[:, off:off + half, cols(n)].bitcast(F32), ALU.subtract).then_inc(n_lop, 1)

            eng.memset(ones[:, :], 1.0).then_inc(s_const, 1)
            eng.memset(ident[:, :], 0.0).then_inc(s_const, 1)
            eng.wait_ge(s_const, 2)
            eng.affine_select(out=ident[:, :], in_=ident[:, :], compare_op=ALU.not_equal, fill=1.0, base=0,
                              pattern=[[-1, P]], channel_multiplier=1).then_inc(s_const, 1)
            eng.affine_select(out=upper[:, :], in_=ones[:, :], compare_op=ALU.is_ge, fill=0.0, base=0,
                              pattern=[[1, P]], channel_multiplier=-1).then_inc(s_const, 1)
            eng.affine_select(out=below[:, :], in_=ones[:, :], compare_op=ALU.is_gt, fill=0.0, base=0,
                              pattern=[[-1, P]], channel_multiplier=1).then_inc(s_const, 1)
            for p in range(U_K // 2, U_F1 // 2 + 2):
                lo_pair(2 * p)
            for n in range(NT):
                norm_lo(0, n)

            def ffn_loop(u0, f):
                def body(i):
                    for stage in range(3):
                        p0 = u0 + 4 + 2 * stage
                        for d in range(2):
                            w = p0 + d + 6 * i
                            if not (isinstance(w, int) and w >= U_END):
                                lo(w, (p0 + d) % 6, (p0 + d) % 3)
                        if stage < 2:
                            for n in range(NT):
                                gi = 66 * f + 3 * stage + n + 6 * i
                                eng.wait_ge(f_mh, gi + 1)
                                eng.tensor_tensor(mid_lo[:, stage, cols(n)], prod[:, (3 * stage + n) % 2, :],
                                                  mid_hi[:, stage, cols(n)].bitcast(F32), ALU.subtract)\
                                   .then_inc(f_ml, 1)
                return body

            body = ffn_loop(U_F1, 0)
            body(0)
            with eng.Fori(1, CHUNKS) as i:
                body(i)
            for n in range(NT):
                norm_lo(1, n)
            eng.wait_ge(s_spill, 48)
            eng.wait_ge(n_hf, 12)
            eng.memset(wpool[:, :, :], 0.0).then_inc(s_wpz, 1)
            eng.iota(ramp_i[:, :], pattern=[[1, PBUF]], base=1, channel_multiplier=0).then_inc(s_wpz, 1)
            eng.wait_ge(s_wdtr, 1)
            eng.tensor_tensor(wdt_lo[:, :, :], wdt[:, :, :], wdt_hi[:, :, :].bitcast(F32), ALU.subtract)\
               .then_inc(s_wdtr, 1)
            for p in range(9):
                lo_pair(U_IN + 4 + 2 * p)
            eng.wait_ge(z_ready, 6 * NT)
            blk = up_s[:, 0:NS].rearrange("p (b t) -> p b t", t=SL)
            mem_b = up_s[:, NS:NS + NB]
            c = [0]

            def link(ins):
                c[0] += 1
                ins.then_inc(pool_c, 1)
                eng.wait_ge(pool_c, c[0])

            link(eng.memset(up_s[:, :], 1.0))
            link(eng.memset(be_s[:, :], 1.0))
            for out_, pat in ((blk, [[-SL, NB], [0, SL]]), (mem_b, [[-SL, NB]])):
                back = [[SL, NB]] + pat[1:]
                link(eng.affine_select(out=out_, in_=out_, compare_op=ALU.is_ge, fill=0.0, base=0, pattern=pat,
                                       channel_multiplier=1))
                link(eng.affine_select(out=out_, in_=out_, compare_op=ALU.is_ge, fill=0.0, base=SL - 1,
                                       pattern=back, channel_multiplier=-1))
            link(eng.affine_select(out=be_s[:, :], in_=up_s[:, 0:NS], compare_op=ALU.is_gt, fill=0.0, base=0,
                                   pattern=[[-1, NS]], channel_multiplier=1))
            link(eng.affine_select(out=up_s[:, 0:NS], in_=up_s[:, 0:NS], compare_op=ALU.is_ge, fill=0.0, base=0,
                                   pattern=[[1, NS]], channel_multiplier=-1))
            eng.memset(hc[:, :], 0.0).then_inc(s_mask, 1)
            eng.wait_ge(s_decd, 2)

            def gate_y(q_):
                sl = chunk(q_)[2]
                eng.wait_ge(y_ev, q_ + 1)
                eng.tensor_tensor(xs[:, :, sl], xs[:, :, sl], z[:, :, sl], ALU.mult).then_inc(g_done, 1)

            for q_ in range(STEPS):
                ch, M, _ = chunk(q_)
                xh = xb[0:M, 0:D_SSM].rearrange("p (h d) -> p h d", d=HD)
                eng.wait_ge(t1_ev, 2 * (q_ + 1))
                wait(eng, yd_ready, q_)
                eng.tensor_tensor(xdt[0:M], xh, bc(dt_[0:M, ch, :].unsqueeze(2), [M, HEADS, HD]), ALU.mult)\
                   .then_inc(xd_ready, 1)
                wait(eng, st_ready, q_ - 1)
                if q_ == 1:
                    eng.wait_ge(s_h0st, 2 * YT)
                eng.tensor_tensor(xde[0:M], xh, bc(dedt[0:M, ch, :].unsqueeze(2), [M, HEADS, HD]), ALU.mult)\
                   .then_inc(xd_ready, 1)
                if q_ == 0:
                    eng.wait_ge(s_h0t, 2 * NB)
                    for j in range(YT):
                        eng.tensor_tensor(h0[:, :, j, :], h0[:, :, j, :],
                                          bc(ea_s[:, j, NS:NS + NB].unsqueeze(2), [P, NB, ST]), ALU.mult)\
                           .then_inc(s_h0s, 1)
                if q_ > 1:
                    eng.wait_ge(h_upd, q_ - 1)
                    eng.tensor_tensor(hc[:, :].rearrange("p (h d) -> p h d", d=HD),
                                      hT[:, :].rearrange("p (h d) -> p h d", d=HD),
                                      bc(cd[:, ch, :].unsqueeze(2), [P, HEADS, HD]), ALU.mult).then_inc(hc_ready, 1)
                if q_:
                    gate_y(q_ - 1)
            gate_y(STEPS - 1)
            for n in range(NT):
                norm_lo(2, n, src=xs, half=3, off=2)
            for p in range(3):
                lo_pair(U_OUT + 4 + 2 * p)
            norm_lo(3, 0)
            lo_pair(U_XQ + 2)
            norm_lo(3, 1)
            norm_lo(3, 2)
            for p in range(4):
                lo_pair(U_XQ + 4 + 2 * p)
            eng.wait_ge(q_ready, 24)
            for i in range(2):
                link(eng.memset(qm[i][:, :, :], 0.0))
            for b in range(NB):
                if b >= 2:
                    eng.wait_ge(b_s, b - 1)
                    link(eng.memset(qm[b % 2][:, :, SL * (b - 2):SL * (b - 1)], 0.0))
                link(eng.tensor_copy(qm[b % 2][:, :, SL * b:SL * b + SL], q[:, :, SEQ + SL * b:SEQ + SL * b + SL]))
                eng.sem_inc(b_q, 1)
            eng.wait_ge(b_d, 3)
            for i in range(2):
                link(eng.memset(pm[i][:, :, :], 0.0))
            by_head = lambda t: t[:, :, :].rearrange("p m (h r) -> p m h r", h=MH)
            for b in range(NB):
                if b >= 2:
                    eng.wait_ge(b_v, b - 1)
                    for m in range(2):
                        link(eng.memset(by_head(pm[b % 2])[:, m, :, SL * (b - 2):SL * (b - 1)], 0.0))
                for m in range(2):
                    link(eng.tensor_copy(by_head(pm[b % 2])[:, m, :, SL * b:SL * b + SL],
                                         by_head(pT_s)[:, m, :, SL * b:SL * b + SL]))
                eng.sem_inc(b_p, 1)
            for p in range(3):
                lo_pair(U_XO + 4 + 2 * p)
            norm_lo(4, 0)
            lo_pair(U_F2 + 2)
            norm_lo(4, 1)
            norm_lo(4, 2)
            body = ffn_loop(U_F2, 1)
            with eng.Fori(0, CHUNKS - 1) as i:
                body(i)
            body(CHUNKS - 1)

        @block.scalar
        def _(eng):
            c = [0]

            def hi_unit(u0, j, i):
                w = u0 + j
                slot, ring = w % 6, w % 3
                if isinstance(i, int) and w + 6 * i >= U_END:
                    return
                wait_used(eng, w - 6, i)
                eng.wait_ge(w_dma[ring], 32 * i + 16 * (w // 3 + 1))
                eng.activation(w_hi[:, slot, :], w_raw[:, ring, :], ACT.Copy).then_inc(w_hid, 1)

            def hi_pair(w):
                hi_unit(w, 0, 0)
                hi_unit(w, 1, 0)

            def link(ins):
                c[0] += 1
                ins.then_inc(act_c, 1)
                eng.wait_ge(act_c, c[0])

            def norm_sq(v, n, src, K=KT, dst=None):
                w = 3 * v + n
                wait(eng, n_st, w)
                out = sq[:, 0:K, :] if dst is None else dst[:, 0:K, cols(n)]
                eng.activation(out, src[:, 0:K, cols(n)], ACT.Square).then_inc(n_sq, 1)

            def norm_hi(v, n, half, src=None, H=4, off=0):
                w = 3 * v + n
                eng.wait_ge(n_hf, 2 * w + half + 1)
                k = slice(H * half, H * half + H)
                s = hf[:, k, :] if src is None else src[:, k, cols(n)]
                eng.activation(h_hi[:, off + H * half:off + H * half + H, cols(n)], s, ACT.Copy).then_inc(n_hi, 1)

            eng.wait_ge(s_mem, 16)
            for t in range(2):
                eng.activation(sq[:, 0:3, 0:TN].rearrange("p a b -> p (a b)")[:, 0:D], mem[:, t, :], ACT.Square,
                               accum_out=nrm[:, 3, t:t + 1]).then_inc(mem_a, 1)
                eng.wait_ge(mem_a, t + 1)
            hi_pair(0)
            hi_pair(2)
            eng.wait_ge(mem_d, 6)
            eng.activation(mem_hi[:, :, :], memf[:, :, :], ACT.Copy).then_inc(mem_a, 1)

            def x_evac(t):
                M = P if t < 8 else NS
                eng.wait_ge(tr_ready, 4 + 2 * t + 1)
                eng.activation(x[:, 0:4, t * P:t * P + M],
                               bank[4][:, :].rearrange("p (k m) -> p k m", k=4)[:, :, 0:M], ACT.Copy).then_inc(tr_act, 1)

            def kv_evac(dst, base_):
                eng.wait_ge(kv_used, 8 * (base_ + 1))
                for h in range(2):
                    eng.activation(dst[:, 0, 512 * h:512 * h + 512], bank[h][:, :], ACT.Copy).then_inc(kv_act, 1)

            for k in range(8):
                if k % 2 == 0:
                    hi_pair(U_K + 4 + k)
                x_evac(k)
            kv_evac(ktok, 0)
            x_evac(8)
            for k in range(8):
                if k % 2 == 0:
                    hi_pair(U_V + 4 + k)
                if k == 2:
                    eng.wait_ge(tr_act, 9)
                    eng.wait_ge(tr_dve, 9)
                    norm_sq(0, 0, x)
                if k == 6:
                    norm_sq(0, 1, x)
            kv_evac(vtok, 1)
            eng.wait_ge(s_ktout, 16)
            norm_hi(0, 0, 0)
            norm_hi(0, 0, 1)
            norm_sq(0, 2, x)
            for n in (1, 2):
                norm_hi(0, n, 0)
                norm_hi(0, n, 1)
            eng.wait_ge(s_kvout, 32)

            def ffn(u0, f, i):
                for stage in range(2):
                    hi_unit(u0, 4 + 2 * stage, i)
                    hi_unit(u0, 5 + 2 * stage, i)
                    for n in range(NT):
                        gl = 3 * stage + n
                        gi = 66 * f + gl + 6 * i
                        eng.wait_ge(f_g, gi + 1)
                        wait(eng, f_p, gi - 1)
                        eng.activation(gate[:, gl % 2, :], bank[gl % 2][:, 0:TN], ACT.Silu).then_inc(f_s, 1)
                        eng.wait_ge(f_p, gi + 1)
                        wait(eng, f_d, 264 * f + 24 * i - 24 + 8 * (n + 1))
                        eng.activation(mid_hi[:, stage, cols(n)], prod[:, gl % 2, :], ACT.Copy).then_inc(f_mh, 1)
                hi_unit(u0, 8, i)
                hi_unit(u0, 9, i)

            F_X1 = 24 * CHUNKS
            F_X2 = 2 * 24 * CHUNKS + 48

            ffn(U_F1, 0, 0)
            with eng.Fori(1, CHUNKS) as i:
                ffn(U_F1, 0, i)
            for n in range(2):
                eng.wait_ge(f_x, F_X1 - 24 + 8 * (n + 1))
                norm_sq(1, n, x)
            norm_hi(1, 0, 0)
            norm_hi(1, 0, 1)
            eng.wait_ge(f_x, F_X1)
            norm_sq(1, 2, x)
            for n in (1, 2):
                norm_hi(1, n, 0)
                norm_hi(1, n, 1)
            eng.wait_ge(s_wdt, 16 * 4)
            eng.activation(wdt_hi[:, :, :], wdt[:, :, :], ACT.Copy).then_inc(s_wdtr, 1)
            eng.wait_ge(s_spill, 48)
            pj = 0
            for pair in range(9):
                hi_pair(U_IN + 4 + 2 * pair)
                if pair == 7:
                    eng.wait_ge(pmix, 2)
                    for i in range(2):
                        for n in range(NT):
                            eng.wait_ge(pmm, 3 * i + n + 1)
                            eng.activation(pool_out[:, i, cols(n)], bank[(6, 7)[(3 * i + n) % 2]][:, 0:TN],
                                           ACT.Copy, scale=par[:, PSC + i:PSC + i + 1]).then_inc(po_hi, 1)
                for n in range(NT):
                    if pair == 5:
                        eng.wait_ge(dt_raw, n + 1)
                        wait(eng, dt_ready, n - 1)
                        eng.activation(dtT[n % 2][0:HEADS, 0:DT_TILES[n][1]],
                                       bank[(4, 7, 6)[n]][0:HEADS, 0:DT_TILES[n][1]], ACT.Copy).then_inc(dt_copied, 1)
                    for mm in range(2):
                        m = 2 * pair + mm
                        src = bank[pj % 4]
                        eng.wait_ge(p_ready, pj + 1)
                        if pair < 5:
                            dst = pre[mm]
                            if n == 0 and m >= 2:
                                eng.wait_ge(conv_done, m - 1)
                                eng.wait_ge(tail_t, m - 1)
                            a = 3 + n * TN
                            w = TN if n < 2 else LASTP
                            ins = eng.activation(dst[:, a:a + w], src[:, 0:w], ACT.Copy)
                            if n == 2:
                                eng.activation(fresh[:, mm, 0:24].rearrange("p (b t) -> p b t", t=3),
                                               src[:, LASTP:TN].rearrange("p (b t) -> p b t", t=SL)[:, :, 1:], ACT.Copy)
                                ins = eng.activation(
                                    dst[:, 3 + SEQ:].rearrange("p (b t) -> p b t", t=7)[:, :, 3:7],
                                    src[:, LASTP:TN].rearrange("p (b t) -> p b t", t=SL), ACT.Copy)
                                ins.then_inc(pre_ready, 1)
                                eng.wait_ge(pre_ready, m + 1)
                                eng.sem_inc(p_free, 1)
                            else:
                                ins.then_inc(p_free, 1)
                        elif pair == 5:
                            dst = ue[mm]
                            a = PBUF + n * TN
                            w = TN if n < 2 else LASTP
                            if n == 0:
                                eng.wait_ge(s_stc, 2)
                            ins = eng.activation(dst[:, a:a + w], src[:, 0:w], ACT.Copy)
                            if n == 2:
                                if mm == 0:
                                    eng.wait_ge(tail_t, 10)
                                eng.activation(fresh[:, mm, :], src[:, LASTP:TN], ACT.Copy)
                                ins = eng.activation(
                                    dst[:, PBUF + SEQ:].rearrange("p (b t) -> p b t", t=PBUF + SL)[:, :, PBUF:],
                                    src[:, LASTP:TN].rearrange("p (b t) -> p b t", t=SL), ACT.Copy)
                                ins.then_inc(ue_ready, 1)
                                eng.wait_ge(ue_ready, mm + 1)
                                eng.sem_inc(p_free, 1)
                            else:
                                ins.then_inc(p_free, 1)
                        else:
                            if n == 0:
                                eng.wait_ge(conv_done, 10)
                            ins = eng.activation(z[:, m - 12, cols(n)], src[:, 0:TN], ACT.Silu)
                            ins.then_inc(z_ready, 1)
                            eng.wait_ge(z_ready, pj - 36 + 1)
                            eng.sem_inc(p_free, 1)
                        pj += 1
                    if n == 1 and 1 <= pair <= 5:
                        for m in (2 * pair - 2, 2 * pair - 1):
                            eng.wait_ge(conv_done, m + 1)
                            d = xs[:, m, :] if m < 6 else bcT[:, m - 6, :]
                            eng.activation(d, d, ACT.Silu).then_inc(xbc_ready, 1)
            eng.wait_ge(s_dexp, 1)
            link(eng.activation(ser[2][:, :, :], ser[1][:, :, :], ACT.Exp, scale=-1.0))
            eng.sem_inc(s_dexp, 1)
            link(eng.activation(expa[:, :, :], alog[:, :, :], ACT.Exp))
            eng.sem_inc(s_dexp, 1)
            eng.wait_ge(s_dec, 1)
            np_ = 8 * HEADS
            B7 = bank[7]
            fl = lambda t: t[:, :, :].rearrange("p c h -> p (c h)")
            link(eng.activation(fl(ea)[:, 0:np_], B7[:, 0:np_], ACT.Exp))
            link(eng.activation(fl(dedt)[:, 0:np_], B7[:, np_:2 * np_], ACT.Exp))
            link(eng.activation(fl(cd)[:, 0:np_], B7[:, 2 * np_:3 * np_], ACT.Exp))
            link(eng.activation(fl(dedt)[0:NS, np_:np_ + HEADS], B7[0:NS, 3 * np_:3 * np_ + HEADS], ACT.Exp))
            link(eng.activation(ea_s[:, :, :].rearrange("p j t -> p (j t)"), bank[6][:, 0:YT * (NS + NB)], ACT.Exp))
            eng.sem_inc(s_dece, 1)
            for q_ in range(STEPS):
                ch, M, _ = chunk(q_)
                for j in range(2):
                    eng.wait_ge(t1, 2 * q_ + j + 1)
                    if j == 0:
                        wait(eng, xd_ready, 2 * q_)
                        wait(eng, st_ready, q_ - 1)
                    eng.activation(xb[0:M, 512 * j:512 * j + 512], bank[j][0:M, :], ACT.Copy).then_inc(t1_ev, 1)
                wait(eng, yd_ready, q_)
                if q_:
                    for j in range(3):
                        eng.wait_ge(seg_ready, 3 * q_ + j - 1)
                        eng.activation(ew[:, 512 * j:512 * j + 512], bank[2 + j][:, :], ACT.Exp).then_inc(e_done, 1)
                else:
                    eng.wait_ge(seg_ready, 1)
                    eng.activation(ew[0:NS, 0:HEADS * NS], bank[2][0:NS, 0:HEADS * NS], ACT.Exp).then_inc(e_done, 1)
                    for b in range(NB):
                        eng.wait_ge(s_h0t, 2 * b + 1)
                        wait(eng, yo_ready, b - 1)
                        eng.activation(h0T[:, b % 2, 0:512], bank[(0, 3)[b % 2]][:, :], ACT.Copy).then_inc(s_h0a, 1)
                if q_ in (Y_STAT0, Y_STAT1):
                    n = 0 if q_ == Y_STAT0 else 1
                    eng.wait_ge(g_done, 4 + 3 * n)
                    norm_sq(2, n, xs, K=YT, dst=z)
            eng.wait_ge(st_ready, STEPS - 1)
            eng.activation(h_hi[:, 0:2, :], pool_out[:, :, :], ACT.Copy).then_inc(po_hi, 1)
            eng.wait_ge(s_ho, 1)
            eng.activation(hout[:, 0:4, :].rearrange("p j n -> p (j n)"), bank[7][:, :], ACT.Copy)
            eng.activation(hout[:, 4:6, :].rearrange("p j n -> p (j n)"), bank[4][:, 0:256], ACT.Copy)\
               .then_inc(s_hoc, 1)
            eng.wait_ge(s_h0o, 16 * YT)
            eng.wait_ge(y_ev, STEPS)
            for half in range(2):
                norm_hi(2, 0, half, src=xs, H=3, off=2)
            eng.wait_ge(g_done, STEPS)
            norm_sq(2, 2, xs, K=YT, dst=z)
            for n in (1, 2):
                for half in range(2):
                    norm_hi(2, n, half, src=xs, H=3, off=2)
            def split_norm(v, base_, last_pair):
                for n in range(2):
                    eng.wait_ge(f_x, base_ + 4 * (n + 1))
                    norm_sq(v, n, x)
                for half in range(2):
                    norm_hi(v, 0, half)
                hi_pair(last_pair)
                eng.wait_ge(f_x, base_ + 12)
                norm_sq(v, 2, x)
                for half in range(2):
                    norm_hi(v, 1, half)

            for pair in range(3):
                hi_pair(U_OUT + 4 + 2 * pair)
            eng.wait_ge(s_hout, 16)
            split_norm(3, F_X1 + 12, U_XQ + 2)
            nq = 0
            for group in range(2):
                hi_pair(U_XQ + 4 + 4 * group)
                for n in range(NT):
                    for m in range(4 * group, 4 * group + 4):
                        if n == 2 and m % 4 == 2:
                            hi_pair(U_XQ + 6 + 4 * group)
                        eng.wait_ge(p_ready, 78 + nq + 1)
                        if group == 1 and n == 0 and m == 4:
                            eng.wait_ge(n_lop, 12)
                            eng.wait_ge(n_lod, 12)
                        eng.activation(q[:, KT - 1 - m, cols(n)], bank[(78 + nq) % 4][:, 0:TN], ACT.Copy)\
                           .then_inc(q_ready, 1)
                        nq += 1
                        eng.wait_ge(q_ready, nq)
                        eng.sem_inc(p_free, 1)
                        if nq == 4:
                            for half in range(2):
                                norm_hi(3, 2, half)
            def att_o(i):
                eng.wait_ge(a_o, i + 1)
                t, h = divmod(i, MH)
                eng.activation(h_hi[:, 2 * h:2 * h + 2, t * P:(t + 1) * P],
                               bank[(2, 5)[i % 2]][:, 0:256].rearrange("p (j t) -> p j t", j=2),
                               ACT.Copy).then_inc(a_oh, 1)

            def att_exp(i):
                t, h = divmod(i, MH)
                eng.wait_ge(a_m, 2 * t + h // 2 + 1)
                wait(eng, a_t, i - 1)
                eng.activation(pr[i % 2][:, :], bank[h // 2][:, 256 * (h % 2):256 * (h % 2) + 256],
                               ACT.Exp, bias=amax[:, 4 * (t % 2) + h:4 * (t % 2) + h + 1], scale=ATT_SCALE,
                               accum_out=amax[:, 8 + i % 2:9 + i % 2]).then_inc(a_e, 1)

            att_exp(0)
            att_exp(1)
            for i in range(NHT):
                if i + 2 < NHT:
                    att_exp(i + 2)
                if i < 2 * NB:
                    for g in (i % 2 * 2, i % 2 * 2 + 1):
                        eng.wait_ge(b_t, 4 * (i // 2) + g + 1)
                        if g == 0:
                            wait(eng, b_s, i // 2)
                        eng.activation(kTs[:, 2 * g:2 * g + 2, :].rearrange("p a b -> p (a b)"),
                                       bank[(3, 6)[g % 2]][:, :], ACT.Copy).then_inc(b_ta, 1)
                if i == S_SOFT:
                    eng.wait_ge(b_d, 1)
                    eng.activation(p_s[:, :], bank[7][:, 0:NMEM], ACT.Exp, bias=amax[:, 10:11], scale=ATT_SCALE,
                                   accum_out=amax[:, 11:12]).then_inc(b_e, 1)
                if i == S_OUT:
                    eng.wait_ge(b_v, NB)
                    eng.activation(o_s[:, 0:512], bank[3][0:NS, :], ACT.Copy).then_inc(b_o, 1)
                if i >= 1:
                    att_o(i - 1)
            att_o(NHT - 1)
            eng.wait_ge(b_r, 2)
            eng.activation(h_hi[:, :, SEQ:T], bank[7][:, 0:256].rearrange("p (j t) -> p j t", j=KT), ACT.Copy)\
               .then_inc(a_oh, 1)
            for pair in range(3):
                hi_pair(U_XO + 4 + 2 * pair)
            split_norm(4, F_X1 + 24 + 12, U_F2 + 2)
            for half in range(2):
                norm_hi(4, 2, half)
            ffn(U_F2, 1, 0)
            with eng.Fori(1, CHUNKS - 1) as i:
                ffn(U_F2, 1, i)
            ffn(U_F2, 1, CHUNKS - 1)
            for n in range(NT):
                eng.wait_ge(f_x, F_X2 - 24 + 8 * (n + 1))
                norm_sq(5, n, x)
            for t in range(9):
                M = P if t < 8 else NS
                eng.wait_ge(y_t, 2 * t + 1)
                if t >= 2:
                    eng.wait_ge(s_y[t % 2], 16 * (t // 2))
                eng.activation(yrow[0:M, t % 2, 0:512], bank[2 * (t % 2)][0:M, :], ACT.Copy).then_inc(y_c[0], 1)

        @block.vector
        def _(eng):
            c = [0]

            def link(ins):
                c[0] += 1
                ins.then_inc(dve_c, 1)
                eng.wait_ge(dve_c, c[0])
                return ins

            def newton(ms, y, s):
                link(eng.tensor_scalar(y.bitcast(I32), ms.bitcast(I32), 1, None, ALU.logical_shift_right))
                link(eng.tensor_scalar(y.bitcast(I32), y.bitcast(I32), -1.0, float(0x5F3759DF), ALU.mult, ALU.add))
                for step in range(4):
                    link(eng.tensor_tensor(s, y, y, ALU.mult))
                    link(eng.scalar_tensor_tensor(out=s, in0=s, scalar=-0.5, in1=ms, op0=ALU.mult, op1=ALU.mult))
                    link(eng.scalar_tensor_tensor(out=y, in0=s, scalar=1.5, in1=y, op0=ALU.add, op1=ALU.mult))

            def norm_rs(v, n, width):
                w = 3 * v + n
                eng.wait_ge(n_st, w + 1)
                ms, y, s = nrm[:, 0, 0:3], nrm[:, 1, 0:3], nrm[:, 2, 0:3]
                link(eng.tensor_scalar(ms, norm_banks(v, n)[0][:, 0:3], 1.0 / width, EPS, ALU.mult, ALU.add))
                newton(ms, y, s)
                wait(eng, n_bc, w)
                eng.tensor_tensor(diag[:, :].rearrange("p (a b) -> p a b", a=3),
                                  bc(ident[:, :].unsqueeze(1), [P, 3, P]), bc(y.unsqueeze(2), [P, 3, P]), ALU.mult)\
                   .then_inc(n_rs, 1)

            def norm_hf(v, n, k, g, src, dst=None, K=KT):
                w = 3 * v + n
                if k == 0:
                    eng.wait_ge(n_bc, w + 1)
                    if dst is None:
                        wait(eng, n_lop, w)
                        wait(eng, n_lod, w)
                out = hf[:, k, :] if dst is None else dst[:, k, cols(n)]
                ins = eng.scalar_tensor_tensor(out=out, in0=src[:, k, cols(n)], scalar=par[:, g + k:g + k + 1],
                                               in1=norm_banks(v, n)[1][:, P:P + TN], op0=ALU.mult, op1=ALU.mult)
                if k % (K // 2) == K // 2 - 1:
                    ins.then_inc(n_hf, 1)

            def norm_lo(v, n, src=None, H=4, off=0):
                w = 3 * v + n
                eng.wait_ge(n_hi, 2 * w + 2)
                s = hf[:, H:2 * H, :] if src is None else src[:, H:2 * H, cols(n)]
                o = slice(off + H, off + 2 * H)
                eng.tensor_tensor(h_lo[:, o, cols(n)], s, h_hi[:, o, cols(n)].bitcast(F32), ALU.subtract)\
                   .then_inc(n_lod, 1)

            eng.wait_ge(s_part, 1)
            link(eng.tensor_copy(par[:, :], bank[6][:, 0:NPAR]))
            eng.wait_ge(mem_a, 2)
            link(eng.tensor_scalar(nrm[:, 0, 0:2], nrm[:, 3, 0:2], 1.0 / D, EPS, ALU.mult, ALU.add))
            newton(nrm[:, 0, 0:2], nrm[:, 1, 0:2], nrm[:, 2, 0:2])
            for t in range(2):
                eng.tensor_scalar(mem[:, t, :], mem[:, t, :], nrm[:, 1, t:t + 1], None, ALU.mult).then_inc(mem_d, 1)
            for g in range(4):
                t, h = divmod(g, 2)
                eng.wait_ge(tr_ready, g + 1)
                eng.tensor_tensor(memf[:, 4 * h:4 * h + 4, t * P:(t + 1) * P],
                                  bank[4 + g % 2][:, :].rearrange("p (k m) -> p k m", k=4),
                                  bc(par[:, GMEM + 4 * h:GMEM + 4 * h + 4].unsqueeze(2), [P, 4, P]), ALU.mult)\
                   .then_inc(mem_d, 1)
            eng.wait_ge(mem_d, 6)
            eng.wait_ge(mem_a, 3)
            eng.tensor_tensor(mem_lo[:, :, :], memf[:, :, :], mem_hi[:, :, :].bitcast(F32), ALU.subtract)\
               .then_inc(mem_d, 1)

            def x_evac(t):
                M = P if t < 8 else NS
                eng.wait_ge(tr_ready, 4 + 2 * t + 2)
                eng.tensor_copy(x[:, 4:8, t * P:t * P + M],
                                bank[5][:, :].rearrange("p (k m) -> p k m", k=4)[:, :, 0:M]).then_inc(tr_dve, 1)

            def kv_evac(dst, base_):
                eng.wait_ge(kv_used, 8 * (base_ + 1))
                for h in range(2):
                    eng.tensor_copy(dst[:, 1, 512 * h:512 * h + 512], bank[2 + h][:, :]).then_inc(kv_dve, 1)

            for k in range(8):
                x_evac(k)
            kv_evac(ktok, 0)
            x_evac(8)
            for g in range(4):
                t, h = divmod(g, 2)
                eng.wait_ge(kt_ready, g + 1)
                eng.tensor_copy(kT0[:, 4 * h:4 * h + 4, t * P:(t + 1) * P],
                                bank[6][:, :].rearrange("p (k m) -> p k m", k=4)).then_inc(kt_copied, 1)
            norm_rs(0, 0, D)
            for k in range(KT):
                norm_hf(0, 0, k, G1, x)
            kv_evac(vtok, 1)
            norm_lo(0, 0)
            for n in (1, 2):
                norm_rs(0, n, D)
                for k in range(KT):
                    norm_hf(0, n, k, G1, x)
                norm_lo(0, n)

            def ffn_products(f, i):
                for stage in range(2):
                    for n in range(NT):
                        gl = 3 * stage + n
                        gi = 66 * f + gl + 6 * i
                        eng.wait_ge(f_s, gi + 1)
                        eng.wait_ge(f_u, gi + 1)
                        wait(eng, f_ml, gi - 1)
                        eng.tensor_tensor(prod[:, gl % 2, :], gate[:, gl % 2, :], bank[2 + gl % 2][:, 0:TN], ALU.mult)\
                           .then_inc(f_p, 1)

            def ffn_add(f, i, n, m):
                dl = 8 * n + m
                eng.wait_ge(f_d, 264 * f + dl + 24 * i + 1)
                xc = x[:, m, cols(n)]
                eng.scalar_tensor_tensor(out=xc, in0=bank[4 + dl % 2][:, 0:TN], scalar=0.5, in1=xc, op0=ALU.mult,
                                         op1=ALU.add).then_inc(f_x, 1)

            def ffn(f, i):
                ffn_products(f, i)
                for n in range(NT):
                    for m in range(KT):
                        ffn_add(f, i, n, m)

            def ffn_last(f, v, g, width, dst=None):
                i = CHUNKS - 1
                ffn_products(f, i)
                for m in range(KT):
                    ffn_add(f, i, 0, m)
                for m in range(4):
                    ffn_add(f, i, 1, m)
                norm_rs(v, 0, width)
                for m in range(4, 8):
                    ffn_add(f, i, 1, m)
                eng.wait_ge(f_x, FX[f] - 16)
                for m in range(4):
                    ffn_add(f, i, 2, m)
                    norm_hf(v, 0, m, g, x, dst)
                norm_rs(v, 1, width)
                for m in range(4, 8):
                    ffn_add(f, i, 2, m)
                    norm_hf(v, 0, m, g, x, dst)

            FX = (24 * CHUNKS, 2 * 24 * CHUNKS + 48)
            ffn(0, 0)
            with eng.Fori(1, CHUNKS - 1) as i:
                ffn(0, i)
            ffn_last(0, 1, GMIX, D)
            norm_lo(1, 0)
            for k in range(KT):
                norm_hf(1, 1, k, GMIX, x)
            norm_rs(1, 2, D)
            norm_lo(1, 1)
            for k in range(KT):
                norm_hf(1, 2, k, GMIX, x)
            norm_lo(1, 2)
            eng.wait_ge(s_spill, 48)
            for i in range(2):
                link(eng.memset(pre[i][:, 0:3], 0.0))
            eng.wait_ge(s_stT, 1)
            link(eng.tensor_copy(convT[:, :, :, :].rearrange("p m b t -> p (m b t)"), bank[5][:, 0:240]))
            link(eng.tensor_copy(poolT[:, :, :, :].rearrange("p m b t -> p (m b t)"), bank[5][:, 240:480]))
            eng.sem_inc(s_stc, 1)
            eng.wait_ge(s_wpz, 2)
            link(eng.tensor_copy(ramp[:, 0, :], ramp_i[:, :]))
            link(eng.tensor_copy(ramp[:, 1, :], ramp[:, 0, :]))
            for g, wn in enumerate(WINDOWS):
                r = ramp[64 * (g % 2):64 * (g % 2) + 64, g // 2, :]
                link(eng.tensor_scalar(r, r, float(wn), 1.0 / wn, ALU.min, ALU.mult))
            link(eng.reciprocal(ramp[:, :, :], ramp[:, :, :]))
            eng.sem_inc(s_stc, 1)

            def conv(m):
                pc = pre[m % 2]
                ps = pc[:, 3 + SEQ:].rearrange("p (b t) -> p b t", t=7)
                if m >= 2:
                    eng.wait_ge(conv_done, m - 1)
                link(eng.tensor_copy(ps[:, :, 0:3], convT[:, m, :, :]))
                eng.wait_ge(pre_ready, m + 1)
                d = xs[:, m, :] if m < 6 else bcT[:, m - 6, :]
                ds_ = d[:, SEQ:T].rearrange("p (b t) -> p b t", t=SL)
                for k in range(4):
                    wk = par[:, CW + 10 * k + m:CW + 10 * k + m + 1]
                    if k == 0:
                        bias = par[:, CB + m:CB + m + 1]
                        eng.tensor_scalar(d[:, 0:SEQ], pc[:, 0:SEQ], wk, bias, ALU.mult, ALU.add)
                        link(eng.tensor_scalar(ds_, ps[:, :, 0:SL], wk, bias, ALU.mult, ALU.add))
                    else:
                        eng.scalar_tensor_tensor(out=d[:, 0:SEQ], in0=pc[:, k:k + SEQ], scalar=wk, in1=d[:, 0:SEQ],
                                                 op0=ALU.mult, op1=ALU.add)
                        ins = eng.scalar_tensor_tensor(out=ds_, in0=ps[:, :, k:k + SL], scalar=wk, in1=ds_,
                                                       op0=ALU.mult, op1=ALU.add)
                        if k < 3:
                            link(ins)
                        else:
                            ins.then_inc(conv_done, 1)

            def tail(m):
                eng.wait_ge(tail_t, m // 2 * 2 + 2)
                s = m % 2
                if m >= 2:
                    eng.wait_ge(tail_d[s], 32 * (m // 2))
                np_, ns_ = (3, 24) if m < 10 else (PBUF, NS)
                eng.tensor_copy(tails[0:np_, s, 0:P], bank[5][0:np_, 256 * s:256 * s + P])
                eng.tensor_copy(tails[0:ns_, s, P:2 * P], bank[5][0:ns_, 256 * s + P:256 * s + 256])\
                   .then_inc(tail_c, 1)

            for pair in range(5):
                for m in (2 * pair, 2 * pair + 1):
                    conv(m)
                for m in (2 * pair, 2 * pair + 1):
                    tail(m)
            for i in range(2):
                u_ = ue[i]
                us = u_[:, PBUF + SEQ:].rearrange("p (b t) -> p b t", t=PBUF + SL)
                eng.wait_ge(ue_ready, i + 1)
                eng.memset(u_[:, 0:PBUF], 0.0)
                link(eng.tensor_copy(us[:, :, 0:PBUF], poolT[:, i, :, :]))
                L = NUE

                def shift_add(dst, src, d, lo_):
                    link(eng.tensor_tensor(dst[:, lo_:L], src[:, lo_:L], src[:, lo_ - d:L - d], ALU.add))

                if i == 0:
                    link(eng.memset(win_a[:, 0:PBUF], 0.0))
                    link(eng.memset(win_b[:, 0:PBUF], 0.0))
                shift_add(win_a, u_, 1, 1)
                shift_add(win_b, win_a, 2, 3)
                if i == 1:
                    shift_add(win_a, win_b, 4, 7)
                    shift_add(win_b, win_a, 8, 15)
                if i == 0:
                    eng.wait_ge(tail_t, 12)
                for half, wn in ((0, WINDOWS[2 * i]), (1, WINDOWS[2 * i + 1])):
                    r = slice(64 * half, 64 * half + 64)
                    s = (win_a, win_b)[half]
                    link(eng.tensor_tensor(s[r, PBUF:2 * PBUF], s[r, PBUF:2 * PBUF], ramp[r, i, :], ALU.mult))
                    link(eng.scalar_tensor_tensor(out=(u_, win_a)[i][r, PBUF:], in0=s[r, PBUF:], scalar=1.0 / wn,
                                                  in1=u_[r, PBUF:], op0=ALU.mult, op1=ALU.subtract))
                eng.sem_inc(pmix, 1)
            for m in (10, 11):
                tail(m)
            eng.wait_ge(z_ready, 6 * NT)
            eng.wait_ge(dt_ready, NT)
            raw, ab, e_, r_, zz, qq, mx = ser
            link(eng.memset(raw[:, :, :], 0.0))
            np_ = 8 * HEADS
            link(eng.tensor_tensor(raw[:, 0:8, :], bank[4][:, 0:np_].rearrange("p (c h) -> p c h", h=HEADS),
                                   bc(dtb[:, :, :], [P, 8, HEADS]), ALU.add))
            link(eng.tensor_tensor(raw[0:NS, 8, :], bank[4][0:NS, np_:np_ + HEADS], dtb[0:NS, 0, :], ALU.add))
            link(eng.scalar_tensor_tensor(out=ab[:, :, :], in0=raw[:, :, :], scalar=-1.0, in1=raw[:, :, :],
                                          op0=ALU.mult, op1=ALU.max))
            eng.sem_inc(s_dexp, 1)
            link(eng.tensor_scalar(mx[:, :, :], raw[:, :, :], 0.0, None, ALU.max))
            eng.wait_ge(s_dexp, 2)
            link(eng.tensor_scalar(r_[:, :, :], e_[:, :, :], 2.0, None, ALU.add))
            link(eng.reciprocal(r_[:, :, :], r_[:, :, :]))
            link(eng.tensor_tensor(r_[:, :, :], e_[:, :, :], r_[:, :, :], ALU.mult))
            link(eng.tensor_tensor(zz[:, :, :], r_[:, :, :], r_[:, :, :], ALU.mult))
            link(eng.tensor_scalar(qq[:, :, :], zz[:, :, :], 1.0 / 17, None, ALU.mult))
            for k in (15, 13, 11, 9, 7, 5, 3):
                link(eng.scalar_tensor_tensor(out=qq[:, :, :], in0=qq[:, :, :], scalar=1.0 / k, in1=zz[:, :, :],
                                              op0=ALU.add, op1=ALU.mult))
            link(eng.scalar_tensor_tensor(out=qq[:, :, :], in0=qq[:, :, :], scalar=1.0, in1=r_[:, :, :],
                                          op0=ALU.add, op1=ALU.mult))
            link(eng.scalar_tensor_tensor(out=dt_[:, :, :], in0=qq[:, :, :], scalar=2.0, in1=mx[:, :, :],
                                          op0=ALU.mult, op1=ALU.add))
            eng.wait_ge(s_dexp, 3)
            link(eng.scalar_tensor_tensor(out=dta[:, :, :], in0=dt_[:, :, :], scalar=-1.0,
                                          in1=bc(expa[:, :, :], [P, NTT, HEADS]), op0=ALU.mult, op1=ALU.mult))
            link(eng.tensor_copy(dtab[:, :, :], bc(dta[0:NS, 8, :].unsqueeze(2), [NS, HEADS, HD])))
            eng.sem_inc(s_decd, 1)
            eng.wait_ge(s_dece, 1)
            link(eng.tensor_tensor(dedt[:, 0:8, :], dedt[:, 0:8, :], dt_[:, 0:8, :], ALU.mult))
            link(eng.tensor_tensor(dedt[0:NS, 8, :], dedt[0:NS, 8, :], dt_[0:NS, 8, :], ALU.mult))
            eng.sem_inc(s_decd, 1)
            eng.wait_ge(s_wdt, 16 * 4)
            for e in range(2):
                link(eng.tensor_copy(dskip[64 * e:64 * e + 64, :],
                                     dsk_all[64 * e:64 * e + 64, :].rearrange("p (j e) -> p e j", e=2)[:, e, :]))

            def make_ud(q_):
                ch, M, _ = chunk(q_)
                if q_:
                    eng.wait_ge(seg_ready, 3 * q_ - 2)
                tri = upper[:, :] if q_ else up_s[:, 0:NS]
                eng.tensor_tensor(ud[0:M, 0:HEADS * M].rearrange("p (h l) -> p h l", h=HEADS),
                                  bc(tri.unsqueeze(1), [M, HEADS, M]),
                                  bc(dta[0:M, ch, :].unsqueeze(2), [M, HEADS, M]), ALU.mult).then_inc(ud_ready, 1)

            eng.wait_ge(s_mask, 1)
            make_ud(0)
            for q_ in range(STEPS):
                ch, M, tok = chunk(q_)
                tri = upper[:, :] if q_ else up_s[:, 0:NS]
                eng.wait_ge(sc_ready, q_ + 1)
                wait(eng, wg_ready, 2 * q_)
                link(eng.tensor_tensor(sm[0:M, 0:2 * M].rearrange("p (g l) -> p g l", g=2),
                                       bank[0][0:M, 0:2 * M].rearrange("p (g l) -> p g l", g=2),
                                       bc(tri.unsqueeze(1), [M, 2, M]), ALU.mult))
                eng.sem_inc(sm_done, 1)
                for g in range(2):
                    eng.wait_ge(e_done, 3 * q_ + g if q_ else 1)
                    e3 = ew[0:M, g * HG * M:(g + 1) * HG * M].rearrange("p (h l) -> p h l", h=HG)
                    eng.tensor_tensor(e3, e3, bc(sm[0:M, g * M:(g + 1) * M].unsqueeze(1), [M, HG, M]), ALU.mult)\
                       .then_inc(wg_ready, 1)
                if q_ == Y_STAT0:
                    norm_rs(2, 0, D_SSM)
                if q_ == Y_BC0:
                    for k in range(YT):
                        norm_hf(2, 0, k, GSSM, xs, dst=xs, K=YT)
                if q_ == Y_STAT1:
                    norm_rs(2, 1, D_SSM)
                if 0 < q_ < STEPS - 1:
                    make_ud(q_ + 1)
                eng.wait_ge(yd_ready, q_ + 1)
                wait(eng, yt_ready, q_)
                if q_ > 1:
                    eng.wait_ge(yo_ready, NB + q_ - 1)
                    for g in range(2):
                        link(eng.tensor_tensor(
                            ytmp[:, 384 * g:384 * g + 384].rearrange("p (h d) -> p h d", h=HG),
                            bank[(7, 4)[g]][:, 0:384].rearrange("p (h d) -> p h d", h=HG),
                            bc(ea[:, ch, HG * g:HG * g + HG].unsqueeze(2), [P, HG, HD]), ALU.mult))
                    for g in range(2):
                        link(eng.tensor_tensor(ytok[:, 384 * g:384 * g + 384], ytmp[:, 384 * g:384 * g + 384],
                                               bank[5 + g][:, 0:384], ALU.add))
                else:
                    for g in range(2):
                        link(eng.tensor_copy(ytok[0:M, 384 * g:384 * g + 384], bank[5 + g][0:M, 0:384]))
                eng.sem_inc(yc_done, 1)
                if q_:
                    eng.wait_ge(st_ready, q_)
                    if q_ > 1:
                        eng.wait_ge(hc_ready, q_ - 1)
                    for g in range(2):
                        o = hT[:, 384 * g:384 * g + 384]
                        if q_ > 1:
                            link(eng.tensor_tensor(o, hc[:, 384 * g:384 * g + 384], bank[2 + g][:, 0:384], ALU.add))
                        else:
                            link(eng.tensor_copy(o, bank[2 + g][:, 0:384]))
                    eng.sem_inc(h_upd, 1)
                eng.wait_ge(yt_ready, q_ + 1)
                for j in range(YT):
                    if q_:
                        ps = bank[5][:, P * j:P * j + P] if j < 4 else bank[6][:, P * (j - 4):P * (j - 4) + P]
                    else:
                        ps = bank[5][:, NS * j:NS * j + NS]
                    ins = eng.scalar_tensor_tensor(out=xs[:, j, tok], in0=xs[:, j, tok], scalar=dskip[:, j:j + 1],
                                                   in1=ps, op0=ALU.mult, op1=ALU.add)
                link(ins)
                if q_ == 0:
                    for b in range(NB):
                        eng.wait_ge(s_h0t, 2 * b + 2)
                        wait(eng, yo_ready, b - 1)
                        eng.tensor_copy(h0T[:, b % 2, 512:768], bank[(1, 4)[b % 2]][:, 0:256]).then_inc(s_h0d, 1)
                    for g in range(2):
                        eng.tensor_tensor(bx[:, g, :, :],
                                          bc(xb[0:NS, D_SSM + P * g:D_SSM + P * g + P].unsqueeze(1), [NS, NB, P]),
                                          bc(up_s[:, NS:NS + NB].unsqueeze(2), [NS, NB, P]), ALU.mult).then_inc(s_h0d, 1)
                    eng.wait_ge(yo_ready, NB)
                    t3 = hT[:, 0:YT * NS].rearrange("p (j t) -> p j t", j=YT)
                    link(eng.tensor_tensor(t3, bank[7][:, 0:YT * NS].rearrange("p (j t) -> p j t", j=YT),
                                           ea_s[:, :, 0:NS], ALU.mult))
                    link(eng.tensor_tensor(xs[:, :, tok], xs[:, :, tok], t3, ALU.add))
                    eng.sem_inc(y_ev, 1)
                    for j in range(YT):
                        eng.wait_ge(s_h0s, j + 1)
                        for half in range(2):
                            eng.wait_ge(s_h0st, 2 * j + half + 1)
                            hb = h0[:, 4 * half:4 * half + 4, j, :]
                            eng.tensor_tensor(hb, hb, bank[(2, 3, 5, 6)[2 * (j % 2) + half]][:, :]
                                              .rearrange("p (b n) -> p b n", b=4), ALU.add).then_inc(s_h0n, 1)
                    make_ud(1)
                else:
                    eng.sem_inc(y_ev, 1)
            for k in range(YT):
                norm_hf(2, 1, k, GSSM, xs, dst=xs, K=YT)
            eng.wait_ge(po_hi, 7)
            eng.tensor_tensor(h_lo[:, 0:2, :], pool_out[:, :, :], h_hi[:, 0:2, :].bitcast(F32), ALU.subtract)\
               .then_inc(po_lo, 1)
            norm_lo(2, 0, src=xs, H=3, off=2)
            norm_lo(2, 1, src=xs, H=3, off=2)
            norm_rs(2, 2, D_SSM)
            for k in range(YT):
                norm_hf(2, 2, k, GSSM, xs, dst=xs, K=YT)
            norm_lo(2, 2, src=xs, H=3, off=2)

            def add_out(p0, back, v, g):
                def add(group, n, four):
                    for c_ in four:
                        j = p0 + 12 * group + 4 * n + c_
                        if group == 0 and c_ == 0:
                            eng.wait_ge(s_back[n], 16 * (back + 1))
                        eng.wait_ge(p_ready, j + 1)
                        xc = x[:, 4 * group + c_, cols(n)]
                        link(eng.tensor_tensor(xc, xc, bank[j % 4][:, 0:TN], ALU.add))
                        eng.sem_inc(p_free, 1)
                        eng.sem_inc(f_x, 1)

                for n in range(NT):
                    add(0, n, range(4))
                add(1, 0, range(4))
                add(1, 1, (0, 1))
                norm_rs(v, 0, D)
                add(1, 1, (2, 3))
                for k in range(KT):
                    norm_hf(v, 0, k, g, x)
                add(1, 2, (0, 1))
                norm_rs(v, 1, D)
                add(1, 2, (2, 3))
                norm_lo(v, 0)
                for k in range(KT):
                    norm_hf(v, 1, k, g, x)
                norm_lo(v, 1)
                norm_rs(v, 2, D)
                for k in range(KT):
                    norm_hf(v, 2, k, g, x)
                norm_lo(v, 2)

            add_out(54, 0, 3, GXQ)

            def sample_softmax(i):
                if i == S_MAX:
                    eng.wait_ge(b_s, NB)
                    link(eng.tensor_reduce(amax[:, 10:11], bank[7][:, 0:NMEM], AX.X, ALU.max))
                    link(eng.tensor_scalar(amax[:, 10:11], amax[:, 10:11], -ATT_SCALE, None, ALU.mult))
                    eng.sem_inc(b_d, 1)
                if i == S_SCALE:
                    eng.wait_ge(b_e, 1)
                    link(eng.reciprocal(amax[:, 11:12], amax[:, 11:12]))
                    link(eng.tensor_scalar(p_s[:, :], p_s[:, :], amax[:, 11:12], None, ALU.mult))
                    eng.sem_inc(b_d, 1)
                if i == S_BACK:
                    eng.wait_ge(b_r, 1)
                    eng.tensor_copy(pT_s[:, :, :].rearrange("p a b -> p (a b)"), bank[7][:, 0:256]).then_inc(b_d, 1)
                if i == S_OUT:
                    eng.wait_ge(b_v, NB)
                    eng.tensor_copy(o_s[:, 512:1024], bank[6][0:NS, :]).then_inc(b_o, 1)

            def att_lo(i):
                eng.wait_ge(a_oh, i + 1)
                t, h = divmod(i, MH)
                tk = slice(t * P, (t + 1) * P)
                eng.tensor_tensor(h_lo[:, 2 * h:2 * h + 2, tk],
                                  bank[(2, 5)[i % 2]][:, 0:256].rearrange("p (j t) -> p j t", j=2),
                                  h_hi[:, 2 * h:2 * h + 2, tk].bitcast(F32), ALU.subtract).then_inc(a_ol, 1)

            def att_max(t, hb):
                m_ = amax[:, 4 * (t % 2) + 2 * hb:4 * (t % 2) + 2 * hb + 2]
                eng.wait_ge(a_s, MH * t + 2 * hb + 2)
                link(eng.tensor_reduce(m_, bank[hb][:, :].rearrange("p (h m) -> p h m", h=2), AX.X, ALU.max))
                link(eng.tensor_scalar(m_, m_, -ATT_SCALE, None, ALU.mult))
                eng.sem_inc(a_m, 1)

            def att_scale(i):
                eng.wait_ge(a_e, i + 1)
                r = amax[:, 12 + i % 2:13 + i % 2]
                link(eng.reciprocal(r, amax[:, 8 + i % 2:9 + i % 2]))
                eng.tensor_scalar(pr[i % 2][:, :], pr[i % 2][:, :], r, None, ALU.mult).then_inc(a_n, 1)

            att_max(0, 0)
            att_max(0, 1)
            att_scale(0)
            for i in range(NHT):
                t, h = divmod(i, MH)
                if i + 1 < NHT:
                    att_scale(i + 1)
                eng.wait_ge(a_t, i + 1)
                wait(eng, a_o, i - 1)
                eng.tensor_copy(pT[i % 2][:, :, :].rearrange("p a b -> p (a b)"), bank[4][:, 0:256]).then_inc(a_c, 1)
                if h % 2 == 0 and t < 7:
                    att_max(t + 1, h // 2)
                sample_softmax(i)
                if i >= 1:
                    att_lo(i - 1)
            att_lo(NHT - 1)
            eng.wait_ge(a_oh, 33)
            eng.tensor_tensor(h_lo[:, :, SEQ:T], bank[7][:, 0:256].rearrange("p (j t) -> p j t", j=KT),
                              h_hi[:, :, SEQ:T].bitcast(F32), ALU.subtract).then_inc(a_ol, 1)
            add_out(102, 1, 4, GF2)
            with eng.Fori(0, CHUNKS - 1) as i:
                ffn(1, i)
            ffn_last(1, 5, GFIN, D, dst=x)
            for k in range(KT):
                norm_hf(5, 1, k, GFIN, x, dst=x)

            def y_out(t):
                M = P if t < 8 else NS
                eng.wait_ge(y_t, 2 * t + 2)
                if t >= 2:
                    eng.wait_ge(s_y[t % 2], 16 * (t // 2))
                eng.tensor_copy(yrow[0:M, t % 2, 512:1024], bank[2 * (t % 2) + 1][0:M, :]).then_inc(y_c[1], 1)

            y_out(0)
            norm_rs(5, 2, D)
            y_out(1)
            for k in range(KT):
                norm_hf(5, 2, k, GFIN, x, dst=x)
            for t in range(2, 9):
                y_out(t)

        @block.tensor
        def _(eng):
            def three(out, a_hi, a_lo, b_hi, b_lo, first, last):
                eng.matmul(out, a_hi, b_hi, start=first, stop=False)
                eng.matmul(out, a_hi, b_lo, start=False, stop=False)
                return eng.matmul(out, a_lo, b_hi, start=False, stop=last)

            def norm_stat(v, n, K=KT):
                w = 3 * v + n
                eng.wait_ge(n_sq, w + 1)
                wait(eng, n_rs, w)
                for j, (o, m) in enumerate(NORM_SUBS):
                    for k in range(K):
                        s_ = sq[:, k, o:o + m] if v != 2 else z[:, k, n * TN + o:n * TN + o + m]
                        mm = eng.matmul(norm_banks(v, n)[0][0:m, j:j + 1], s_, ones[:, 0:1], start=(k == 0),
                                        stop=(k == K - 1))
                mm.then_inc(n_st, 1)

            def norm_bc(v, n):
                w = 3 * v + n
                eng.wait_ge(n_rs, w + 1)
                wait(eng, n_hf, 2 * w)
                eng.matmul(norm_banks(v, n)[1][:, P:P + TN], ones[:, :], diag[:, 0:TN], start=True, stop=True).then_inc(n_bc, 1)

            def norm_ready(v, n):
                eng.wait_ge(n_lop, 3 * v + n + 1)
                eng.wait_ge(n_lod, 3 * v + n + 1)

            eng.wait_ge(s_const, 5)
            eng.wait_ge(s_par, 16 * 10)
            eng.transpose(bank[6][:, 0:NPAR], parrow[:, :], ident[0:NPAR, 0:NPAR]).then_inc(s_part, 1)
            eng.wait_ge(mem_d, 2)
            for g in range(4):
                t, h = divmod(g, 2)
                wait(eng, mem_d, g + 1 if g >= 2 else 0)
                for k in range(4):
                    mm = eng.transpose(bank[4 + g % 2][:, k * P:(k + 1) * P], mem[:, t, (4 * h + k) * P:(4 * h + k + 1) * P],
                                       ident[:, :])
                mm.then_inc(tr_ready, 1)
            eng.wait_ge(mem_d, 6)

            def x_turn(t):
                M = P if t < 8 else NS
                eng.wait_ge(s_x[t // 2], 32 if t < 8 else 16)
                for h in range(2):
                    wait(eng, (tr_act, tr_dve)[h], t)
                    for k in range(4):
                        mm = eng.transpose(bank[4 + h][:, k * P:k * P + M],
                                           xtok[0:M, t, (4 * h + k) * P:(4 * h + k + 1) * P], ident[0:M, 0:M])
                    mm.then_inc(tr_ready, 1)

            def mem_unit(w, k):
                eng.wait_ge(w_ready, w + 1)
                s = w % 6
                for t in range(2):
                    for h in range(2):
                        ms, wc = slice(t * P, (t + 1) * P), slice(512 * h, 512 * h + 512)
                        out = bank[2 * t + h][:, :]
                        eng.matmul(out, mem_hi[:, k, ms], w_hi[:, s, wc], start=(k == 0), stop=False)
                        eng.matmul(out, mem_hi[:, k, ms], w_lo[:, s, wc], start=False, stop=False)
                        mm = eng.matmul(out, mem_lo[:, k, ms], w_hi[:, s, wc], start=False, stop=(k == KT - 1))
                mm.then_inc(kv_used, 1)
                return mm

            eng.wait_ge(mem_d, 7)
            for k in range(KT):
                mem_unit(U_K + k, k)
                x_turn(k)
            x_turn(8)
            eng.wait_ge(kv_act, 2)
            eng.wait_ge(kv_dve, 2)
            for k in range(KT):
                mem_unit(U_V + k, k)
                if 1 <= k <= 4:
                    g = k - 1
                    t, h = divmod(g, 2)
                    wait(eng, kt_copied, g)
                    for kk in range(4):
                        mm = eng.transpose(bank[6][:, kk * P:(kk + 1) * P],
                                           ktok[:, t, (4 * h + kk) * P:(4 * h + kk + 1) * P], ident[:, :])
                    mm.then_inc(kt_ready, 1)
                if k == 5:
                    eng.wait_ge(kt_copied, 4)
                    norm_stat(0, 0)
                if k == 6:
                    norm_bc(0, 0)
            norm_stat(0, 1)
            eng.wait_ge(kv_act, 4)
            eng.wait_ge(kv_dve, 4)

            def ffn_half(u0, f, i, stage, n, what):
                gl = 3 * stage + n
                gi = 66 * f + gl + 6 * i
                slot = (u0 + 2 * stage + what) % 6
                wait(eng, (f_s, f_p)[what], gi - 1)
                out = bank[2 * what + gl % 2][:, 0:TN]
                for k in range(KT):
                    ks = slice(k * P, (k + 1) * P)
                    mm = three(out, w_hi[:, slot, ks], w_lo[:, slot, ks], h_hi[:, k, cols(n)], h_lo[:, k, cols(n)],
                               k == 0, k == KT - 1)
                mm.then_inc((f_g, f_u)[what], 1)
                return mm

            def ffn_down(u0, f, i, n, m):
                dl = 8 * n + m
                wait(eng, f_x, FXB[f] + dl + 24 * i - 1)
                out = bank[4 + dl % 2][:, 0:TN]
                ms = slice(m * P, (m + 1) * P)
                for fi in range(2):
                    slot = (u0 + 4 + fi) % 6
                    mm = three(out, w_hi[:, slot, ms], w_lo[:, slot, ms], mid_hi[:, fi, cols(n)],
                               mid_lo[:, fi, cols(n)], fi == 0, fi == 1)
                mm.then_inc(f_d, 1)
                return mm

            FXB = (0, 24 * CHUNKS + 48)

            def ffn(u0, f, i, first=None, steps=((), ()), last=None):
                for stage in range(2):
                    eng.wait_ge(w_ready, u0 + 2 * stage + 2 + 6 * i)
                    for n in range(NT):
                        if first is not None and stage == 0:
                            norm_ready(first, n)
                        for what in range(2):
                            ffn_half(u0, f, i, stage, n, what)
                            if stage == 0 and n == 0:
                                for step, v, tile in steps[what]:
                                    step(v, tile)
                eng.wait_ge(w_ready, u0 + 6 + 6 * i)
                for n in range(NT):
                    eng.wait_ge(f_ml, 66 * f + 3 + n + 1 + 6 * i)
                    for m in range(KT):
                        ffn_down(u0, f, i, n, m)
                        if last is not None and m == 3:
                            if n == 1:
                                norm_stat(last, 0)
                            if n == 2:
                                norm_stat(last, 1)
                    if last is not None and n == 1:
                        norm_bc(last, 0)
                    if last is not None and n == 2:
                        norm_bc(last, 1)

            ffn(U_F1, 0, 0, first=0, steps=(((norm_bc, 0, 1),), ((norm_stat, 0, 2), (norm_bc, 0, 2))))
            with eng.Fori(1, CHUNKS - 1) as i:
                ffn(U_F1, 0, i)
            ffn(U_F1, 0, CHUNKS - 1, last=1)

            pj = [0]

            def project(w, n):
                wait(eng, p_free, pj[0] - 3)
                s = w % 6
                out = bank[pj[0] % 4][:, 0:TN]
                for k in range(KT):
                    ks = slice(k * P, (k + 1) * P)
                    mm = three(out, w_hi[:, s, ks], w_lo[:, s, ks], h_hi[:, k, cols(n)], h_lo[:, k, cols(n)],
                               k == 0, k == KT - 1)
                mm.then_inc(p_ready, 1)
                pj[0] += 1

            def tail_turn(m):
                s = m % 2
                wait(eng, tail_c, m // 2 * 2)
                if m < 10:
                    eng.wait_ge(pre_ready, m + 1)
                    t_ = pre[s]
                    np_, ns_ = 3, 24
                    a = t_[:, SEQ:SEQ + 3]
                    b_ = fresh[:, s, 0:24]
                else:
                    eng.wait_ge(ue_ready, m - 9)
                    t_ = ue[m - 10]
                    np_, ns_ = PBUF, NS
                    a = t_[:, SEQ:SEQ + PBUF]
                    b_ = fresh[:, s, :]
                eng.transpose(bank[5][0:np_, 256 * s:256 * s + P], a, ident[:, :])
                eng.transpose(bank[5][0:ns_, 256 * s + P:256 * s + 256], b_, ident[:, :]).then_inc(tail_t, 1)

            for pair in range(9):
                w = U_IN + 2 * pair
                eng.wait_ge(w_ready, w + 2)
                if pair == 5:
                    eng.wait_ge(s_wdtr, 2)
                    for c_, (a, w_) in enumerate(DT_TILES):
                        for k in range(KT):
                            mm = three(bank[(4, 7, 6)[c_]][0:HEADS, 0:w_], wdt_hi[:, k, :], wdt_lo[:, k, :],
                                       h_hi[:, k, a:a + w_], h_lo[:, k, a:a + w_], k == 0, k == KT - 1)
                        mm.then_inc(dt_raw, 1)
                for n in range(NT):
                    if pair == 0:
                        norm_ready(1, n)
                    if pair == 0 and n == 0:
                        norm_stat(1, 2)
                    for mm in range(2):
                        project(w + mm, n)
                        if pair == 0 and n == 0 and mm == 0:
                            norm_bc(1, 2)
                    if pair == 5:
                        eng.wait_ge(dt_copied, n + 1)
                        a, w_ = DT_TILES[n]
                        for t in range(a // P, (a + w_ + P - 1) // P):
                            M = min(P, T - t * P)
                            mm = eng.transpose(bank[4][0:M, HEADS * t:HEADS * t + HEADS],
                                               dtT[n % 2][0:HEADS, t * P - a:t * P - a + M], ident[0:HEADS, 0:HEADS])
                        mm.then_inc(dt_ready, 1)
                    if n == 0 and 1 <= pair <= 5:
                        tail_turn(2 * pair - 2)
                        tail_turn(2 * pair - 1)
                    if n == 0 and pair == 6:
                        tail_turn(10)
                        tail_turn(11)
                if pair == 0:
                    eng.wait_ge(s_strow, 32)
                    for m in range(10):
                        eng.transpose(bank[5][:, 24 * m:24 * m + 24], convrow[:, m * P:(m + 1) * P],
                                      ident[0:24, 0:24])
                    for i in range(2):
                        t_ = eng.transpose(bank[5][:, 240 + 120 * i:360 + 120 * i],
                                           poolrow[:, i * P:(i + 1) * P], ident[0:120, 0:120])
                    t_.then_inc(s_stT, 1)
                    eng.wait_ge(s_stc, 1)
                if pair == 6:
                    eng.wait_ge(s_wpool, 64)
                    mean = (ue[0], win_a)
                    for i in range(2):
                        eng.wait_ge(pmix, i + 1)
                        for n in range(NT):
                            g = 3 * i + n
                            wait(eng, po_hi, g - 1)
                            bk = bank[(6, 7)[g % 2]]
                            if n < 2:
                                a = PBUF + n * TN
                                mm = eng.matmul(bk[:, 0:TN], wpool[:, i, :], mean[i][:, a:a + TN], start=True, stop=True)
                            else:
                                a = PBUF + 2 * TN
                                eng.matmul(bk[:, 0:LASTP], wpool[:, i, :], mean[i][:, a:a + LASTP], start=True,
                                           stop=True)
                                mm = eng.matmul(bk[:, LASTP:TN], wpool[:, i, :],
                                                mean[i][:, PBUF + SEQ:].rearrange("p (b t) -> p b t", t=PBUF + SL)[:, :, PBUF:],
                                                start=True, stop=True)
                            mm.then_inc(pmm, 1)

            eng.wait_ge(s_decd, 1)
            eng.wait_ge(s_mask, 1)
            np_ = 8 * HEADS
            dfl = dta[:, 0:8, :].rearrange("p c h -> p (c h)")
            for j, m_ in enumerate((upper, below, ones)):
                eng.matmul(bank[7][:, j * np_:(j + 1) * np_], m_[:, :], dfl, start=True, stop=True)
            eng.matmul(bank[7][0:NS, 3 * np_:3 * np_ + HEADS], be_s[:, :], dta[0:NS, 8, :], start=True, stop=True)
            for j in range(YT):
                mm = eng.matmul(bank[6][:, j * (NS + NB):(j + 1) * (NS + NB)],
                                dtab[:, 2 * j:2 * j + 2, :].rearrange("p a b -> p (a b)"), up_s[:, :], start=True, stop=True)
            mm.then_inc(s_dec, 1)
            eng.wait_ge(xbc_ready, 10)
            eng.wait_ge(s_dece, 1)

            def turn_x(q_):
                ch, M, tok = chunk(q_)
                wait(eng, sm_done, q_)
                if q_ == 1:
                    eng.wait_ge(s_h0a, NB)
                    eng.wait_ge(s_h0d, NB)
                if q_ == Y_STAT0 + 1:
                    eng.wait_ge(n_rs, 7)
                if q_ == Y_BC0 + 1:
                    eng.wait_ge(n_hf, 14)
                for j in range(8):
                    src = xs[:, j, tok] if j < 6 else bcT[:, j - 6, tok]
                    mm = eng.transpose(bank[j // 4][0:M, P * (j % 4):P * (j % 4) + P], src, ident[:, :])
                    if j % 4 == 3:
                        mm.then_inc(t1, 1)

            def scores_bc(q_):
                ch, M, tok = chunk(q_)
                eng.wait_ge(t1_ev, 2 * q_ + 2)
                for g in range(2):
                    mm = eng.matmul(bank[0][0:M, M * g:M * g + M], bcT[:, g, tok], bcT[:, 2 + g, tok], start=True, stop=True)
                mm.then_inc(sc_ready, 1)

            def segments(q_):
                eng.wait_ge(ud_ready, q_ + 1)
                if q_ == 0:
                    eng.matmul(bank[2][0:NS, 0:HEADS * NS], be_s[:, :], ud[0:NS, 0:HEADS * NS], start=True, stop=True)\
                       .then_inc(seg_ready, 1)
                    return
                wait(eng, h_upd, q_ - 1)
                if q_ == 1:
                    eng.wait_ge(s_h0n, 2 * YT)
                for j in range(3):
                    if j == 2:
                        scores_bc(q_)
                        wait(eng, yc_done, q_)
                    eng.matmul(bank[2 + j][:, :], below[:, :], ud[:, 512 * j:512 * j + 512], start=True, stop=True)\
                       .then_inc(seg_ready, 1)

            turn_x(0)
            segments(0)
            scores_bc(0)
            for q_ in range(STEPS):
                ch, M, tok = chunk(q_)
                eng.wait_ge(e_done, 3 * q_ + 1)
                if q_ > 1:
                    for g in range(2):
                        mm = eng.matmul(bank[(7, 4)[g]][:, 0:384], bcT[:, 2 + g, tok], hT[:, 384 * g:384 * g + 384],
                                        start=True, stop=True)
                    mm.then_inc(yo_ready, 1)
                if q_ == Y_STAT0:
                    norm_stat(2, 0, K=YT)
                if q_ == Y_BC0:
                    norm_bc(2, 0)
                if q_ == Y_STAT1:
                    norm_stat(2, 1, K=YT)
                eng.wait_ge(xd_ready, 2 * q_ + 1)
                wait(eng, y_ev, q_)
                for h in range(HEADS):
                    if h % HG == 0:
                        eng.wait_ge(wg_ready, 2 * q_ + h // HG + 1)
                    mm = eng.matmul(bank[5 + h // HG][0:M, HD * (h % HG):HD * (h % HG) + HD], ew[0:M, M * h:M * h + M],
                                    xdt[0:M, h, :], start=True, stop=True)
                mm.then_inc(yd_ready, 1)
                eng.wait_ge(xd_ready, 2 * q_ + 2)
                if q_:
                    for g in range(2):
                        mm = eng.matmul(bank[2 + g][:, 0:384], xb[:, D_SSM + P * g:D_SSM + P * g + P],
                                        xde[:, HG * g:HG * g + HG, :].rearrange("p a b -> p (a b)"), start=True, stop=True)
                    mm.then_inc(st_ready, 1)
                if 0 < q_ < STEPS - 1:
                    turn_x(q_ + 1)
                if q_ == STEPS - 1:
                    norm_bc(2, 1)
                    eng.wait_ge(h_upd, 8)
                    eng.wait_ge(yc_done, STEPS)
                    for j in range(YT):
                        o = bank[7][:, P * j:P * j + P] if j < 4 else bank[4][:, P * (j - 4):P * (j - 4) + P]
                        mm = eng.transpose(o, hT[:, P * j:P * j + P], ident[:, :])
                    mm.then_inc(s_ho, 1)
                eng.wait_ge(yc_done, q_ + 1)
                for j in range(YT):
                    if q_:
                        o = bank[5][:, P * j:P * j + P] if j < 4 else bank[6][:, P * (j - 4):P * (j - 4) + P]
                    else:
                        o = bank[5][:, NS * j:NS * j + NS]
                    mm = eng.transpose(o, ytok[0:M, P * j:P * j + P], ident[0:M, 0:M])
                mm.then_inc(yt_ready, 1)
                if q_:
                    if q_ < STEPS - 1:
                        segments(q_ + 1)
                    continue
                eng.wait_ge(s_h0, 16)
                eng.wait_ge(sm_done, 1)
                def turn_state(b):
                    wait(eng, s_h0a, b - 1)
                    wait(eng, s_h0d, b - 1)
                    for j in range(YT):
                        bk = bank[((0, 1), (3, 4))[b % 2][j // 4]]
                        mm = eng.transpose(bk[:, P * (j % 4):P * (j % 4) + P], h0[:, b, j, :], ident[:, :])
                        if j in (3, 5):
                            mm.then_inc(s_h0t, 1)

                turn_state(0)
                for b in range(NB):
                    if b + 1 < NB:
                        turn_state(b + 1)
                    eng.wait_ge(s_h0a, b + 1)
                    eng.wait_ge(s_h0d, b + 1)
                    for j in range(YT):
                        c_ = NS * j + SL * b
                        mm = eng.matmul(bank[7][:, c_:c_ + SL], h0T[:, b % 2, P * j:P * j + P],
                                        bcT[:, 2 + j // 3, SEQ + SL * b:SEQ + SL * b + SL], start=True, stop=True)
                    mm.then_inc(yo_ready, 1)
                eng.wait_ge(s_h0d, NB + 2)
                for j in range(YT):
                    for half in range(2):
                        bk = bank[(2, 3, 5, 6)[2 * (j % 2) + half]]
                        wait(eng, s_h0n, 2 * j + half - 3)
                        eng.matmul(bk[:, :], xde[0:NS, 2 * j:2 * j + 2, :].rearrange("p a b -> p (a b)"),
                                   bx[:, j // 3, 4 * half:4 * half + 4, :].rearrange("p a b -> p (a b)"), start=True,
                                   stop=True).then_inc(s_h0st, 1)
                turn_x(1)
                segments(1)
            norm_stat(2, 2, K=YT)
            eng.wait_ge(po_lo, 1)

            def project_all(u0, first=None, last=None):
                for group in range(2):
                    for n in range(NT):
                        for second in range(2):
                            w = u0 + 4 * group + 2 * second
                            if n == 0:
                                eng.wait_ge(w_ready, w + 2)
                            if first is not None and group == 0 and second == 0:
                                norm_ready(first, n)
                            for mm in range(2):
                                project(w + mm, n)
                            step = (norm_stat, norm_bc)[second]
                            if last is not None and group == 1 and n > 0:
                                step(last, n - 1)
                            if first == 2 and group == 0 and n == 0 and second == 0:
                                norm_bc(2, 2)
                            if first == 3 and group == 0 and n == 0:
                                step(3, 2)

            project_all(U_OUT, first=2, last=3)
            project_all(U_XQ, first=3)

            eng.wait_ge(q_ready, 24)
            eng.wait_ge(s_kv2, 32)

            def scores(t, hb):
                wait(eng, a_e, MH * (t - 1) + 2 * hb + 2)
                for h in (2 * hb, 2 * hb + 1):
                    o = bank[h // 2][:, 256 * (h % 2):256 * (h % 2) + 256]
                    for kd in range(2):
                        mm = eng.matmul(o, q[:, KT - 1 - 2 * h - kd, t * P:(t + 1) * P], kT[:, 2 * h + kd, :], start=(kd == 0),
                                        stop=(kd == 1))
                    mm.then_inc(a_s, 1)

            def values(i):
                t, h = divmod(i, MH)
                eng.wait_ge(a_c, i + 1)
                wait(eng, a_ol, i - 1)
                for dt2 in range(2):
                    o = bank[(2, 5)[i % 2]][:, P * dt2:P * dt2 + P]
                    for m in range(2):
                        c_ = (2 * h + dt2) * P
                        mm = eng.matmul(o, v[:, m, c_:c_ + P], pT[i % 2][:, m, :], start=(m == 0), stop=(m == 1))
                mm.then_inc(a_o, 1)

            def turn_p(i):
                eng.wait_ge(a_n, i + 1)
                wait(eng, a_c, i)
                for m in range(2):
                    mm = eng.transpose(bank[4][:, P * m:P * m + P],
                                       pr[i % 2][:, m * P:(m + 1) * P], ident[:, :])
                mm.then_inc(a_t, 1)

            def sample_turn(b, g):
                if g == 0:
                    eng.wait_ge(s_kr[b % 2], 16 * (b // 2 + 1))
                wait(eng, b_ta, 4 * b + g - 1)
                for c_ in range(4):
                    f_, m = 2 * g + c_ // 2, c_ % 2
                    mm = eng.transpose(bank[(3, 6)[g % 2]][:, P * c_:P * c_ + P],
                                       kring[b % 2][:, m, f_ * P:(f_ + 1) * P], ident[:, :])
                mm.then_inc(b_t, 1)

            def sample_scores(b):
                eng.wait_ge(b_ta, 4 * b + 4)
                eng.wait_ge(b_q, b + 1)
                for h in range(MH):
                    for kd in range(2):
                        mm = eng.matmul(bank[7][NS * h:NS * h + NS, 0:NMEM], qm[b % 2][:, KT - 1 - 2 * h - kd, :],
                                        kTs[:, 2 * h + kd, :], start=(b == 0 and kd == 0),
                                        stop=(b == NB - 1 and kd == 1))
                mm.then_inc(b_s, 1)

            def sample_values(b):
                eng.wait_ge(s_vr[b % 4], 16 * (b // 4 + 1))
                eng.wait_ge(b_p, b + 1)
                for h in range(MH):
                    for m in range(2):
                        mm = eng.matmul(bank[(3, 6)[h // 2]][0:NS, MHD * (h % 2):MHD * (h % 2) + MHD],
                                        pm[b % 2][:, m, NS * h:NS * h + NS], vring[b % 4][:, m, MHD * h:MHD * h + MHD],
                                        start=(b == 0 and m == 0 and h % 2 == 0),
                                        stop=(b == NB - 1 and m == 1 and h % 2 == 1))
                mm.then_inc(b_v, 1)

            scores(0, 0)
            scores(0, 1)
            turn_p(0)
            for i in range(NHT):
                t, h = divmod(i, MH)
                if i < 2 * NB:
                    sample_turn(i // 2, i % 2 * 2)
                    sample_turn(i // 2, i % 2 * 2 + 1)
                if i + 1 < NHT:
                    turn_p(i + 1)
                if h % 2 == 0 and t < 7:
                    scores(t + 1, h // 2)
                values(i)
                if i < 2 * NB and i % 2:
                    sample_scores(i // 2)
                if i == S_SCALE + 1:
                    eng.wait_ge(b_d, 2)
                    for m in range(2):
                        mm = eng.transpose(bank[7][:, P * m:P * m + P], p_s[:, m * P:(m + 1) * P], ident[:, :])
                    mm.then_inc(b_r, 1)
                if S_VALUES <= i < S_VALUES + NB:
                    sample_values(i - S_VALUES)
                if i == S_TURN:
                    eng.wait_ge(b_o, 2)
                    for j in range(KT):
                        mm = eng.transpose(bank[7][:, NS * j:NS * j + NS], o_s[:, j * P:(j + 1) * P], ident[0:NS, 0:NS])
                    mm.then_inc(b_r, 1)
            eng.wait_ge(a_ol, 33)
            project_all(U_XO, last=4)
            ffn(U_F2, 1, 0, first=4, steps=(((norm_stat, 4, 2),), ((norm_bc, 4, 2),)))
            with eng.Fori(1, CHUNKS - 1) as i:
                ffn(U_F2, 1, i)
            ffn(U_F2, 1, CHUNKS - 1, last=5)

            def y_turn(t):
                M = P if t < 8 else NS
                eng.wait_ge(n_hf, 2 * (15 + min(2, (t * P + M - 1) // TN) + 1))
                if t == 0:
                    eng.wait_ge(f_s, 132)
                    eng.wait_ge(f_p, 132)
                for h in range(2):
                    wait(eng, y_c[h], t - 1)
                    for k in range(4):
                        mm = eng.transpose(bank[2 * (t % 2) + h][0:M, k * P:(k + 1) * P],
                                           x[:, 4 * h + k, t * P:t * P + M], ident[:, :])
                    mm.then_inc(y_t, 1)

            y_turn(0)
            norm_stat(5, 2)
            y_turn(1)
            norm_bc(5, 2)
            for t in range(2, 9):
                y_turn(t)


_INS = ['x_prompt', 'x_sample', 'mem_prompt', 'cache_mem_k', 'cache_mem_v', 'state_pool', 'state_conv', 'state_ssm',
        'g_ffn1', 'w1_gate', 'w1_up', 'w1_down', 'g_mix', 'w_in', 'conv_w', 'conv_b', 'dt_bias', 'a_log', 'd_skip',
        'ssm_norm', 'w_pool', 'pool_scale', 'w_out', 'g_mem', 'w_mem_k', 'w_mem_v', 'g_xq', 'w_xq', 'w_xo',
        'g_ffn2', 'w2_gate', 'w2_up', 'w2_down', 'g_final']
_OUTS = [('y_prompt', (1, SEQ, D)), ('y_sample', (NB, SL, D)), ('mem_k_prompt', (1, 1, NMEM, MH, MHD)),
         ('mem_v_prompt', (1, 1, NMEM, MH, MHD)), ('pool_prompt', (1, 1, PBUF, D_POOL)),
         ('conv_prompt', (1, 1, 3, CONV_DIM)), ('ssm_prompt', (1, 1, HEADS, HD, ST)),
         ('pool_sample', (1, NB, PBUF, D_POOL)), ('conv_sample', (1, NB, 3, CONV_DIM)),
         ('ssm_sample', (1, NB, HEADS, HD, ST))]


def kernel(**inputs):
    import numpy as _np
    import concourse.bacc as _bacc
    from concourse import mybir as _mybir
    from concourse.bass_utils import run_bass_kernel_spmd as _run

    nc = _bacc.Bacc("TRN2", target_bir_lowering=False, num_devices=1)
    arrays, ins, outs = {}, {}, {}
    for name in _INS:
        a = _np.ascontiguousarray(inputs[name])
        arrays[f"in_{name}_dram"] = a
        ins[name] = nc.dram_tensor(f"in_{name}_dram", a.shape, _mybir.dt.from_np(a.dtype), kind="ExternalInput").ap()
    for name, shape in _OUTS:
        outs[name] = nc.dram_tensor(f"out_{name}_dram", shape, _mybir.dt.float32, kind="ExternalOutput").ap()
    build(nc, ins, outs)
    r = _run(nc, [arrays], core_ids=[0])
    return tuple(r.results[0][f"out_{name}_dram"] for name, _ in _OUTS)
```
